# Optimizing a Trainium2 kernel written in Bass

```python
import jax, jax.numpy as jnp
from jax import lax
import numpy as np
import math

D_MODEL = 1024
BATCH = 1
SEQ = 512
DEPTH = 1

CHUNK = 64
D_MIX = D_MODEL
SSD_WIDTH = D_MIX // 2
ATTN_WIDTH = D_MIX - SSD_WIDTH
SSD_HEAD_DIM = 64
SSD_HEADS = SSD_WIDTH // SSD_HEAD_DIM
SSD_GROUPS = 2
SSD_HPG = SSD_HEADS // SSD_GROUPS
SSD_STATE = 128
SSD_CONV = 4
SSD_CHUNK = CHUNK
XBC_DIM = SSD_WIDTH + 2 * SSD_GROUPS * SSD_STATE
ATTN_HEAD_DIM = 64
ATTN_HEADS = ATTN_WIDTH // ATTN_HEAD_DIM
LEFT_CHUNKS = 8
BAND = (LEFT_CHUNKS + 1) * CHUNK
MAX_REL = 128
N_REL = 2 * MAX_REL + 1
FFN_DIM = 2816
FFN_CONV = 3
ADA_DIM = 6 * D_MODEL
IN_SIZES = (SSD_WIDTH, XBC_DIM, SSD_HEADS, ATTN_WIDTH, ATTN_WIDTH, ATTN_WIDTH)
IN_DIM = sum(IN_SIZES)
IN_SPLITS = [int(v) for v in np.cumsum(IN_SIZES)[:-1]]
EPS = 1e-6


def rmsnorm(x, w):
    xf = x.astype(jnp.float32)
    y = xf * lax.rsqrt(jnp.mean(xf * xf, axis=-1, keepdims=True) + EPS)
    return (y * w.astype(jnp.float32)).astype(x.dtype)

def causal_dwconv(x, w):
    k, ch = w.shape
    return lax.conv_general_dilated(x, w[:, None, :].astype(x.dtype), window_strides=(1,),
                                    padding=[(k - 1, 0)], dimension_numbers=('NWC', 'WIO', 'NWC'),
                                    feature_group_count=ch)

def ssd_scan(xdt, adt, bm, cm):
    b, s = xdt.shape[:2]
    nc = s // SSD_CHUNK
    L = SSD_CHUNK
    X = xdt.reshape(b, nc, L, SSD_GROUPS, SSD_HPG, SSD_HEAD_DIM)
    A = adt.reshape(b, nc, L, SSD_GROUPS, SSD_HPG)
    Bm = bm.reshape(b, nc, L, SSD_GROUPS, SSD_STATE)
    Cm = cm.reshape(b, nc, L, SSD_GROUPS, SSD_STATE)
    a_cs = jnp.cumsum(A, axis=2)
    seg = a_cs[:, :, :, None] - a_cs[:, :, None]
    causal = jnp.tril(jnp.ones((L, L), dtype=bool))[:, :, None, None]
    decay_ls = jnp.exp(jnp.where(causal, seg, -jnp.inf))
    cb = jnp.einsum('bclgn,bcsgn->bclsg', Cm, Bm)
    y_diag = jnp.einsum('bclsg,bclsge,bcsgep->bclgep', cb, decay_ls, X)
    decay_to_end = jnp.exp(a_cs[:, :, -1:] - a_cs)
    states = jnp.einsum('bclgn,bclge,bclgep->bcgepn', Bm, decay_to_end, X)
    chunk_decay = jnp.exp(a_cs[:, :, -1])

    def step(h, inp):
        st, dec = inp
        return h * dec[..., None, None] + st, h

    _, prev = lax.scan(step, jnp.zeros_like(states[:, 0]),
                       (jnp.moveaxis(states, 1, 0), jnp.moveaxis(chunk_decay, 1, 0)))
    prev = jnp.moveaxis(prev, 0, 1)
    y_off = jnp.einsum('bclgn,bcgepn,bclge->bclgep', Cm, prev, jnp.exp(a_cs))
    return (y_diag + y_off).reshape(b, s, SSD_HEADS, SSD_HEAD_DIM)

def ssd_mixer(z, xbc, dt_raw, conv_w, conv_b, dt_bias, a_log, d_skip, norm_w):
    b, s, _ = xbc.shape
    xbc = jax.nn.silu(causal_dwconv(xbc, conv_w) + conv_b.astype(xbc.dtype))
    xs, bm, cm = jnp.split(xbc.astype(jnp.float32), [SSD_WIDTH, SSD_WIDTH + SSD_GROUPS * SSD_STATE], axis=-1)
    xs = xs.reshape(b, s, SSD_HEADS, SSD_HEAD_DIM)
    bm = bm.reshape(b, s, SSD_GROUPS, SSD_STATE)
    cm = cm.reshape(b, s, SSD_GROUPS, SSD_STATE)
    dt = jax.nn.softplus(dt_raw.astype(jnp.float32) + dt_bias.astype(jnp.float32))
    A = -jnp.exp(a_log.astype(jnp.float32))
    y = ssd_scan(xs * dt[..., None], dt * A, bm, cm)
    y = y + d_skip.astype(jnp.float32)[:, None] * xs
    y = y.reshape(b, s, SSD_WIDTH) * jax.nn.silu(z.astype(jnp.float32))
    return rmsnorm(y, norm_w).astype(z.dtype)

def chunk_attention(q, k, v, rel_bias):
    b, s, _ = q.shape
    nc = s // CHUNK
    pad = LEFT_CHUNKS * CHUNK
    qc = q.reshape(b, nc, CHUNK, ATTN_HEADS, ATTN_HEAD_DIM)

    def band(t):
        tp = jnp.pad(t.reshape(b, s, ATTN_HEADS, ATTN_HEAD_DIM), ((0, 0), (pad, 0), (0, 0), (0, 0)))
        tp = tp.reshape(b, nc + LEFT_CHUNKS, CHUNK, ATTN_HEADS, ATTN_HEAD_DIM)
        return jnp.concatenate([tp[:, w:w + nc] for w in range(LEFT_CHUNKS + 1)], axis=2)

    kb, vb = band(k), band(v)
    scores = jnp.einsum('bcqhd,bckhd->bhcqk', qc, kb).astype(jnp.float32) * (ATTN_HEAD_DIM ** -0.5)
    qi = jnp.arange(CHUNK)[:, None]
    kj = jnp.arange(BAND)[None, :]
    rel_idx = jnp.clip(qi - kj + pad, -MAX_REL, MAX_REL) + MAX_REL
    bias = rel_bias.astype(jnp.float32)[:, rel_idx]
    key_pos = jnp.arange(nc)[:, None] * CHUNK - pad + kj
    valid = (key_pos >= 0)[:, None, :]
    scores = jnp.where(valid, scores + bias[:, None], jnp.finfo(jnp.float32).min)
    p = jax.nn.softmax(scores, axis=-1).astype(v.dtype)
    o = jnp.einsum('bhcqk,bckhd->bcqhd', p, vb)
    return o.reshape(b, s, ATTN_WIDTH)

def conv_ffn(h, w_up, conv_w, w_down):
    u = causal_dwconv(h @ w_up, conv_w)
    g, val = jnp.split(u, 2, axis=-1)
    return (jax.nn.silu(g) * val) @ w_down

def first_inputs(seed: int = 0) -> dict:
    key = jax.random.key(seed)
    ks = jax.random.split(key, 24)
    f32 = jnp.float32
    nrm = lambda k, shape, sc: jax.random.normal(k, shape, f32) * sc
    u = jax.random.uniform(ks[10], (DEPTH, SSD_HEADS), f32)
    dt0 = jnp.exp(u * (jnp.log(0.1) - jnp.log(0.001)) + jnp.log(0.001))
    return {
        "x": nrm(ks[0], (BATCH, SEQ, D_MODEL), 1.0),
        "c": nrm(ks[1], (BATCH, D_MODEL), 1.0),
        "norm_mix_w": 1.0 + nrm(ks[2], (DEPTH, D_MODEL), 0.05),
        "w_ada": nrm(ks[3], (DEPTH, D_MODEL, ADA_DIM), 0.02),
        "b_ada": nrm(ks[4], (DEPTH, ADA_DIM), 0.02),
        "w_in": nrm(ks[5], (DEPTH, D_MODEL, IN_DIM), D_MODEL ** -0.5),
        "ssd_conv_w": nrm(ks[6], (DEPTH, SSD_CONV, XBC_DIM), SSD_CONV ** -0.5),
        "ssd_conv_b": nrm(ks[7], (DEPTH, XBC_DIM), 0.02),
        "dt_bias": dt0 + jnp.log(-jnp.expm1(-dt0)),
        "a_log": jnp.log(jax.random.uniform(ks[8], (DEPTH, SSD_HEADS), f32, 1.0, 16.0)),
        "d_skip": 1.0 + nrm(ks[9], (DEPTH, SSD_HEADS), 0.1),
        "ssd_norm_w": 1.0 + nrm(ks[11], (DEPTH, SSD_WIDTH), 0.05),
        "rel_bias": nrm(ks[12], (DEPTH, ATTN_HEADS, N_REL), 0.5),
        "w_out": nrm(ks[13], (DEPTH, D_MIX, D_MODEL), D_MIX ** -0.5),
        "norm_ffn_w": 1.0 + nrm(ks[14], (DEPTH, D_MODEL), 0.05),
        "w_up": nrm(ks[15], (DEPTH, D_MODEL, 2 * FFN_DIM), D_MODEL ** -0.5),
        "ffn_conv_w": nrm(ks[16], (DEPTH, FFN_CONV, 2 * FFN_DIM), FFN_CONV ** -0.5),
        "w_down": nrm(ks[17], (DEPTH, FFN_DIM, D_MODEL), FFN_DIM ** -0.5),
        "final_norm_w": 1.0 + nrm(ks[18], (D_MODEL,), 0.05),
    }

def first_block(x, c, norm_mix_w, w_ada, b_ada, w_in, ssd_conv_w, ssd_conv_b, dt_bias, a_log, d_skip,
              ssd_norm_w, rel_bias, w_out, norm_ffn_w, w_up, ffn_conv_w, w_down, final_norm_w):
    c_act = jax.nn.silu(c)
    for l in range(DEPTH):
        mod = (c_act @ w_ada[l] + b_ada[l])[:, None, :]
        sh_m, sc_m, g_m, sh_f, sc_f, g_f = jnp.split(mod, 6, axis=-1)
        h = rmsnorm(x, norm_mix_w[l]) * (1 + sc_m) + sh_m
        z, xbc, dt_raw, q, k, v = jnp.split(h @ w_in[l], IN_SPLITS, axis=-1)
        y_ssd = ssd_mixer(z, xbc, dt_raw, ssd_conv_w[l], ssd_conv_b[l], dt_bias[l], a_log[l],
                          d_skip[l], ssd_norm_w[l])
        y_att = chunk_attention(q, k, v, rel_bias[l])
        x = x + g_m * (jnp.concatenate([y_ssd, y_att], axis=-1) @ w_out[l])
        h = rmsnorm(x, norm_ffn_w[l]) * (1 + sc_f) + sh_f
        x = x + g_f * conv_ffn(h, w_up[l], ffn_conv_w[l], w_down[l])
    return rmsnorm(x, final_norm_w)


N_HEADS_ATTN = 8
N_KV_HEADS = 2
HEAD_DIM_ATTN = 64
ATTN_GROUP = N_HEADS_ATTN // N_KV_HEADS
WINDOW = 128
ATTN_BLOCK = WINDOW
N_REL_BUCKETS = 32
REL_MAX_DISTANCE = 128
N_HEADS_MLSTM = 4
HEAD_DIM_MLSTM = 128
MLSTM_CHUNK = 64
CONV_WIDTH = 5
ATTN_Q_W = N_HEADS_ATTN * HEAD_DIM_ATTN
ATTN_KV_W = N_KV_HEADS * HEAD_DIM_ATTN
MLSTM_W = N_HEADS_MLSTM * HEAD_DIM_MLSTM
MLSTM_GATE_W = 2 * 2 * N_HEADS_MLSTM
MERGE_W = 2 * D_MODEL
IN_SPLITS_2 = (ATTN_Q_W, ATTN_KV_W, ATTN_KV_W, MLSTM_W, MLSTM_W, MLSTM_W, MLSTM_W, MLSTM_GATE_W, MERGE_W)
D_IN_PROJ = sum(IN_SPLITS_2)
N_GROUPS = 4
EXPERTS_PER_GROUP = 8
N_EXPERTS = N_GROUPS * EXPERTS_PER_GROUP
TOP_K_EXPERT = 2
D_EXPERT = 512
MOE_BLOCK = 128
RMS_EPS = 1e-6
NEG_INF = -1e30


def rmsnorm_2(x, g):
    xf = x.astype(jnp.float32)
    y = xf * lax.rsqrt(jnp.mean(xf * xf, axis=-1, keepdims=True) + RMS_EPS)
    return (y * g.astype(jnp.float32)).astype(x.dtype)

def split_cols(t, sizes):
    outs, start = [], 0
    for s in sizes:
        outs.append(t[..., start:start + s])
        start += s
    return outs

def t5_bucket(rel):
    half = N_REL_BUCKETS // 2
    max_exact = half // 2
    sign = jnp.where(rel > 0, half, 0)
    n = jnp.abs(rel)
    nf = jnp.maximum(n, 1).astype(jnp.float32)
    large = max_exact + (jnp.log(nf / max_exact) / math.log(REL_MAX_DISTANCE / max_exact)
                         * (half - max_exact)).astype(jnp.int32)
    large = jnp.minimum(large, half - 1)
    return sign + jnp.where(n < max_exact, n, large)

def band_windows(t, nb):
    B = t.shape[0]
    tp = jnp.pad(t, ((0, 0), (ATTN_BLOCK, ATTN_BLOCK), (0, 0), (0, 0)))
    tp = tp.reshape(B, nb + 2, ATTN_BLOCK, t.shape[2], t.shape[3])
    return jnp.concatenate([tp[:, :-2], tp[:, 1:-1], tp[:, 2:]], axis=2)

def windowed_gqa(q, k, v, q_gain, k_gain, rel_table, sink):
    B, S = q.shape[0], q.shape[1]
    nb = S // ATTN_BLOCK
    q = q.reshape(B, S, N_HEADS_ATTN, HEAD_DIM_ATTN)
    k = k.reshape(B, S, N_KV_HEADS, HEAD_DIM_ATTN)
    v = v.reshape(B, S, N_KV_HEADS, HEAD_DIM_ATTN)
    q = rmsnorm_2(q, q_gain) * (HEAD_DIM_ATTN ** -0.5)
    k = rmsnorm_2(k, k_gain)
    qb = q.reshape(B, nb, ATTN_BLOCK, N_KV_HEADS, ATTN_GROUP, HEAD_DIM_ATTN)
    kw = band_windows(k, nb)
    vw = band_windows(v, nb)
    scores = jnp.einsum('bnqkgd,bnskd->bkgnqs', qb, kw).astype(jnp.float32)
    qi = jnp.arange(ATTN_BLOCK)
    ks = jnp.arange(3 * ATTN_BLOCK) - ATTN_BLOCK
    rel = ks[None, :] - qi[:, None]
    bias = jnp.transpose(rel_table[t5_bucket(rel)].astype(jnp.float32), (2, 0, 1))
    bias = bias.reshape(N_KV_HEADS, ATTN_GROUP, 1, ATTN_BLOCK, 3 * ATTN_BLOCK)
    kpos = jnp.arange(nb)[:, None, None] * ATTN_BLOCK + ks[None, None, :]
    valid = (jnp.abs(rel) <= WINDOW)[None] & (kpos >= 0) & (kpos < S)
    scores = jnp.where(valid, scores + bias, NEG_INF)
    sink_col = jnp.broadcast_to(sink.astype(jnp.float32).reshape(N_KV_HEADS, ATTN_GROUP, 1, 1, 1),
                                scores.shape[:-1] + (1,))
    probs = jax.nn.softmax(jnp.concatenate([scores, sink_col], axis=-1), axis=-1)[..., :-1]
    out = jnp.einsum('bkgnqs,bnskd->bnqkgd', probs.astype(v.dtype), vw)
    return out.reshape(B, S, ATTN_Q_W)

def mlstm_scan(q, k, v, ig, lf):
    B, H, S, d = q.shape
    L = MLSTM_CHUNK
    nc = S // L

    def chunks(t):
        return jnp.moveaxis(t.reshape((B, H, nc, L) + t.shape[3:]), 2, 0)

    tril = jnp.tril(jnp.ones((L, L), dtype=bool))

    def step(carry, inp):
        C, n, m = carry
        qc, kc, vc, igc, lfc = inp
        b = jnp.cumsum(lfc, axis=-1)
        dlog = jnp.where(tril, b[..., :, None] - b[..., None, :] + igc[..., None, :], -jnp.inf)
        g_inter = b + m[..., None]
        m_row = jnp.maximum(g_inter, jnp.max(dlog, axis=-1))
        w = jnp.exp(dlog - m_row[..., None])
        s = jnp.einsum('bhtd,bhsd->bhts', qc, kc) * w
        inter = jnp.exp(g_inter - m_row)
        num = jnp.einsum('bhts,bhsd->bhtd', s, vc) + inter[..., None] * jnp.einsum('bhtd,bhde->bhte', qc, C)
        den = jnp.sum(s, axis=-1) + inter * jnp.einsum('bhtd,bhd->bht', qc, n)
        h = num / jnp.maximum(jnp.abs(den), jnp.exp(-m_row))[..., None]
        b_last = b[..., -1]
        wlog = b_last[..., None] - b + igc
        m_new = jnp.maximum(b_last + m, jnp.max(wlog, axis=-1))
        decay = jnp.exp(b_last + m - m_new)
        ws = jnp.exp(wlog - m_new[..., None])
        C_new = decay[..., None, None] * C + jnp.einsum('bhs,bhsd,bhse->bhde', ws, kc, vc)
        n_new = decay[..., None] * n + jnp.einsum('bhs,bhsd->bhd', ws, kc)
        return (C_new, n_new, m_new), h

    init = (jnp.zeros((B, H, d, d), jnp.float32), jnp.zeros((B, H, d), jnp.float32),
            jnp.zeros((B, H), jnp.float32))
    _, h = lax.scan(step, init, (chunks(q), chunks(k), chunks(v), chunks(ig), chunks(lf)))
    return jnp.moveaxis(h, 0, 2).reshape(B, H, S, d)

def mlstm_branch(qm, km, vm, om, gates, conv_w, conv_b, gate_b, out_gain):
    B, S = qm.shape[0], qm.shape[1]
    qk = jnp.concatenate([qm, km], axis=-1)
    qk = lax.conv_general_dilated(qk, conv_w[:, None, :].astype(qk.dtype), (1,),
                                  [(CONV_WIDTH // 2, CONV_WIDTH // 2)],
                                  dimension_numbers=('NWC', 'WIO', 'NWC'),
                                  feature_group_count=qk.shape[-1]) + conv_b
    qk = jax.nn.silu(qk)
    qm, km = qk[..., :MLSTM_W], qk[..., MLSTM_W:]

    def heads(t):
        return t.reshape(B, S, N_HEADS_MLSTM, HEAD_DIM_MLSTM).transpose(0, 2, 1, 3).astype(jnp.float32)

    q = heads(qm)
    k = heads(km) * (HEAD_DIM_MLSTM ** -0.5)
    v = heads(vm)
    g = gates.astype(jnp.float32).reshape(B, S, 2, 2, N_HEADS_MLSTM) + gate_b.astype(jnp.float32)
    g = jnp.transpose(g, (2, 3, 0, 4, 1))
    h_f = mlstm_scan(q, k, v, g[0, 0], jax.nn.log_sigmoid(g[0, 1]))

    def flip(t):
        return jnp.flip(t, axis=2)

    h_b = flip(mlstm_scan(flip(q), flip(k), flip(v), flip(g[1, 0]), flip(jax.nn.log_sigmoid(g[1, 1]))))
    h = (h_f + h_b).transpose(0, 2, 1, 3)
    h = rmsnorm_2(h, out_gain)
    return h.reshape(B, S, MLSTM_W).astype(om.dtype) * jax.nn.sigmoid(om)

def hier_moe(h, w_rg, b_rg, w_re, b_re, w_gate, w_up, w_down):
    B, S, D = h.shape
    T = B * S
    xt = h.reshape(T, D)
    xf = xt.astype(jnp.float32)
    g_logits = xf @ w_rg.astype(jnp.float32) + b_rg.astype(jnp.float32)
    g_idx = jnp.argmax(g_logits, axis=-1).astype(jnp.int32)
    p_group = jnp.take_along_axis(jax.nn.softmax(g_logits, axis=-1), g_idx[:, None], axis=1)[:, 0]
    e_logits = (xf @ w_re.astype(jnp.float32) + b_re.astype(jnp.float32)).reshape(T, N_GROUPS, EXPERTS_PER_GROUP)
    e_in = jnp.take_along_axis(e_logits, g_idx[:, None, None], axis=1)[:, 0]
    top_v, top_i = lax.top_k(e_in, TOP_K_EXPERT)
    top_w = jax.nn.softmax(top_v, axis=-1) * p_group[:, None]
    expert_ids = (g_idx[:, None] * EXPERTS_PER_GROUP + top_i).reshape(-1).astype(jnp.int32)
    weights = top_w.reshape(-1)
    token_ids = jnp.repeat(jnp.arange(T, dtype=jnp.int32), TOP_K_EXPERT)
    A = T * TOP_K_EXPERT
    order = jnp.argsort(expert_ids)
    se, stok, sw = expert_ids[order], token_ids[order], weights[order]
    counts = jnp.bincount(expert_ids, length=N_EXPERTS)
    starts = jnp.cumsum(counts) - counts
    pcounts = ((counts + MOE_BLOCK - 1) // MOE_BLOCK) * MOE_BLOCK
    pends = jnp.cumsum(pcounts)
    pstarts = pends - pcounts
    dest = pstarts[se] + (jnp.arange(A, dtype=jnp.int32) - starts[se])
    P = A + N_EXPERTS * MOE_BLOCK
    nblk = P // MOE_BLOCK
    row_tok = jnp.zeros((P,), jnp.int32).at[dest].set(stok)
    row_w = jnp.zeros((P,), jnp.float32).at[dest].set(sw)
    blk_e = jnp.minimum(jnp.searchsorted(pends, jnp.arange(nblk) * MOE_BLOCK, side='right'),
                        N_EXPERTS - 1).astype(jnp.int32)
    xs = xt[row_tok].reshape(nblk, MOE_BLOCK, D)

    def expert_block(args):
        xb, e = args
        return (jax.nn.silu(xb @ w_gate[e]) * (xb @ w_up[e])) @ w_down[e]

    ys = lax.map(expert_block, (xs, blk_e)).reshape(P, D)
    y = jnp.zeros((T, D), ys.dtype).at[row_tok].add(ys * row_w[:, None].astype(ys.dtype))
    return y.reshape(B, S, D).astype(h.dtype)

def second_inputs(seed: int = 0) -> dict:
    key = jax.random.key(seed)
    ks = jax.random.split(key, 24)

    def nrm(k, shape, scale):
        return jax.random.normal(k, shape, jnp.float32) * scale

    ib = nrm(ks[9], (DEPTH, 2, 1, N_HEADS_MLSTM), 0.1)
    fb = jnp.linspace(3.0, 6.0, N_HEADS_MLSTM, dtype=jnp.float32)[None, None, None, :] + nrm(ks[10], (DEPTH, 2, 1, N_HEADS_MLSTM), 0.01)
    return {
        'x': nrm(ks[0], (BATCH, SEQ, D_MODEL), 1.0),
        'norm1_g': 1.0 + nrm(ks[1], (DEPTH, D_MODEL), 0.01),
        'w_in': nrm(ks[2], (DEPTH, D_MODEL, D_IN_PROJ), D_MODEL ** -0.5),
        'attn_q_gain': 1.0 + nrm(ks[3], (DEPTH, HEAD_DIM_ATTN), 0.01),
        'attn_k_gain': 1.0 + nrm(ks[4], (DEPTH, HEAD_DIM_ATTN), 0.01),
        'attn_sink': nrm(ks[5], (DEPTH, N_HEADS_ATTN), 0.5),
        'rel_bias_table': nrm(ks[6], (N_REL_BUCKETS, N_HEADS_ATTN), 0.5),
        'mlstm_conv_w': nrm(ks[7], (DEPTH, CONV_WIDTH, 2 * MLSTM_W), CONV_WIDTH ** -0.5),
        'mlstm_conv_b': nrm(ks[8], (DEPTH, 2 * MLSTM_W), 0.01),
        'mlstm_gate_b': jnp.concatenate([ib, fb], axis=2),
        'mlstm_out_gain': 1.0 + nrm(ks[11], (DEPTH, N_HEADS_MLSTM, HEAD_DIM_MLSTM), 0.01),
        'w_branch_attn': nrm(ks[12], (DEPTH, ATTN_Q_W, D_MODEL), ATTN_Q_W ** -0.5),
        'w_branch_mlstm': nrm(ks[13], (DEPTH, MLSTM_W, D_MODEL), MLSTM_W ** -0.5),
        'merge_b': nrm(ks[14], (DEPTH, MERGE_W), 0.01),
        'w_out': nrm(ks[15], (DEPTH, D_MODEL, D_MODEL), D_MODEL ** -0.5),
        'norm2_g': 1.0 + nrm(ks[16], (DEPTH, D_MODEL), 0.01),
        'w_router_group': nrm(ks[17], (DEPTH, D_MODEL, N_GROUPS), D_MODEL ** -0.5),
        'b_router_group': nrm(ks[18], (DEPTH, N_GROUPS), 0.01),
        'w_router_expert': nrm(ks[19], (DEPTH, D_MODEL, N_EXPERTS), D_MODEL ** -0.5),
        'b_router_expert': nrm(ks[20], (DEPTH, N_EXPERTS), 0.01),
        'w_expert_gate': nrm(ks[21], (DEPTH, N_EXPERTS, D_MODEL, D_EXPERT), D_MODEL ** -0.5),
        'w_expert_up': nrm(ks[22], (DEPTH, N_EXPERTS, D_MODEL, D_EXPERT), D_MODEL ** -0.5),
        'w_expert_down': nrm(ks[23], (DEPTH, N_EXPERTS, D_EXPERT, D_MODEL), D_EXPERT ** -0.5),
    }

def second_block(x, norm1_g, w_in, attn_q_gain, attn_k_gain, attn_sink, rel_bias_table,
              mlstm_conv_w, mlstm_conv_b, mlstm_gate_b, mlstm_out_gain,
              w_branch_attn, w_branch_mlstm, merge_b, w_out, norm2_g,
              w_router_group, b_router_group, w_router_expert, b_router_expert,
              w_expert_gate, w_expert_up, w_expert_down):
    for l in range(DEPTH):
        h = rmsnorm_2(x, norm1_g[l])
        proj = h @ w_in[l]
        qa, ka, va, qm, km, vm, om, gm, mg = split_cols(proj, IN_SPLITS_2)
        ya = windowed_gqa(qa, ka, va, attn_q_gain[l], attn_k_gain[l], rel_bias_table, attn_sink[l])
        ym = mlstm_branch(qm, km, vm, om, gm, mlstm_conv_w[l], mlstm_conv_b[l],
                          mlstm_gate_b[l], mlstm_out_gain[l])
        gates = jax.nn.sigmoid(mg + merge_b[l])
        u = gates[..., :D_MODEL] * (ya @ w_branch_attn[l]) + gates[..., D_MODEL:] * (ym @ w_branch_mlstm[l])
        x = x + u @ w_out[l]
        x = x + hier_moe(rmsnorm_2(x, norm2_g[l]), w_router_group[l], b_router_group[l],
                         w_router_expert[l], b_router_expert[l],
                         w_expert_gate[l], w_expert_up[l], w_expert_down[l])
    return x


def setup_inputs(seed=0):
    out = dict(first_inputs(seed))
    for name, value in second_inputs(seed + 1).items():
        if name != "x":
            out[name + "_2"] = value
    return out


def reference(
    x, c, norm_mix_w, w_ada, b_ada, w_in, ssd_conv_w, ssd_conv_b, dt_bias, a_log, d_skip,
    ssd_norm_w, rel_bias, w_out, norm_ffn_w, w_up, ffn_conv_w, w_down, final_norm_w, norm1_g_2,
    w_in_2, attn_q_gain_2, attn_k_gain_2, attn_sink_2, rel_bias_table_2, mlstm_conv_w_2,
    mlstm_conv_b_2, mlstm_gate_b_2, mlstm_out_gain_2, w_branch_attn_2, w_branch_mlstm_2,
    merge_b_2, w_out_2, norm2_g_2, w_router_group_2, b_router_group_2, w_router_expert_2,
    b_router_expert_2, w_expert_gate_2, w_expert_up_2, w_expert_down_2,
):
    x = first_block(
        x, c, norm_mix_w, w_ada, b_ada, w_in, ssd_conv_w, ssd_conv_b, dt_bias, a_log, d_skip,
        ssd_norm_w, rel_bias, w_out, norm_ffn_w, w_up, ffn_conv_w, w_down, final_norm_w,
    )
    return second_block(
        x, norm1_g_2, w_in_2, attn_q_gain_2, attn_k_gain_2, attn_sink_2, rel_bias_table_2,
        mlstm_conv_w_2, mlstm_conv_b_2, mlstm_gate_b_2, mlstm_out_gain_2, w_branch_attn_2,
        w_branch_mlstm_2, merge_b_2, w_out_2, norm2_g_2, w_router_group_2, b_router_group_2,
        w_router_expert_2, b_router_expert_2, w_expert_gate_2, w_expert_up_2, w_expert_down_2,
    )


_drawn_inputs = setup_inputs


def setup_inputs(seed=0):
    import zlib

    import numpy as np

    out = dict(_drawn_inputs(seed))
    spreads = {}
    factors = {'norm1_g_2': 2.852,
     'attn_q_gain_2': 8.0,
     'attn_k_gain_2': 8.0,
     'attn_sink_2': 8.0,
     'mlstm_conv_b_2': 62.773,
     'mlstm_out_gain_2': 24.881,
     'merge_b_2': 21.411,
     'b_router_expert_2': 15.778,
     'norm2_g_2': 8.0,
     'b_router_group_2': 6.636}
    for name, (base, spread) in spreads.items():
        noise = np.random.default_rng([zlib.crc32(name.encode()), seed]).standard_normal(out[name].shape)
        drawn = base * np.exp(spread * noise) if base else spread * noise
        out[name] = __import__('jax').numpy.asarray(drawn.astype(out[name].dtype))
    for name, factor in factors.items():
        out[name] = (out[name] * factor).astype(out[name].dtype)
    return out
```

```python
import math
from contextlib import ExitStack

import numpy as np

import concourse.bass as bass
from concourse import mybir

F32 = mybir.dt.float32
I32 = mybir.dt.int32
U32 = mybir.dt.uint32
ALU = mybir.AluOpType
ACT = mybir.ActivationFunctionType
AX = mybir.AxisListType.X
ds = bass.ds

P = 128
T = 512
NT = T // P
D = 1024
KD = D // P
EPS = 1e-6
NEG = -1e30

HEADS = 8
HD = 64
FFN = 2816
FT = FFN // P
MAX_REL = 128
Z0, XBC0, DT0, Q0, K0, V0 = 0, 512, 1536, 1544, 2056, 2568
QA0, KA0, QM0, KM0, VM0, OM0, GM0, MG0 = 0, 512, 768, 1280, 1792, 2304, 2816, 2832
WIN = 128
BUCKETS = 32
MH = 4
E = 32
EF = 512
CAP = 64
OVB = (2 * T) // CAP - 1
ROWS = 3072
assert ROWS >= (E + OVB) * CAP

COLS = {}
_at = 0
for _n, _w in (("c", 8), ("norm_mix", 8), ("b_ada", 48), ("ssd_cw", 32), ("ssd_cb", 8), ("norm_ffn", 8),
               ("ffn_cw", 3 * 2 * FT), ("final_norm", 8), ("norm1", 8), ("ssd_norm", 4), ("ml_cw", 40),
               ("ml_cb", 8), ("merge_b", 16), ("norm2", 8), ("q_gain", 1), ("k_gain", 1)):
    COLS[_n] = (_at, _w)
    _at += _w
NCOL = _at
ROWP = {}
_at = 0
for _n, _w in (("dt_bias", 8), ("a_log", 8), ("d_skip", 8), ("rel_far", 8), ("sink", 8), ("b_router", 36),
               ("gate_b", 16), ("out_gain", 512)):
    ROWP[_n] = (_at, _w)
    _at += _w
NROW = _at


def bucket_runs():
    half, exact = BUCKETS // 2, BUCKETS // 4
    rel = np.arange(-WIN, WIN + 1)
    n = np.abs(rel)
    nf = np.maximum(n, 1).astype(np.float32)
    large = exact + (np.log(nf / exact) / math.log(128 / exact) * (half - exact)).astype(np.int32)
    b = np.where(rel > 0, half, 0) + np.where(n < exact, n, np.minimum(large, half - 1))
    runs, s = [], 0
    for i in range(1, len(b) + 1):
        if i == len(b) or b[i] != b[s]:
            runs.append((s - WIN + 255, i - WIN + 255, int(b[s])))
            s = i
    return runs


def two_blocks(nc, a, out, dbg=None, stop="end"):
    ctx = ExitStack()
    with ctx:
        def sb(name, shape, dt=F32):
            return ctx.enter_context(nc.sbuf_tensor(name, shape, dt))

        def sem(name):
            return ctx.enter_context(nc.semaphore(name))

        bank = [ctx.enter_context(nc.psum_tensor(f"bank{i}", [P, 512], F32)) for i in range(8)]

        SLOT = 4096
        ring = [sb(f"slot{i}", [P, SLOT]) for i in range(4)]
        upper = sb("upper", [P, 2 * SLOT])
        xT = sb("xT", [P, KD, T])
        hT = sb("hT", [P, KD, T])
        W = 16896
        arena = sb("arena", [P, W])
        cols = sb("cols", [P, NCOL])
        rows = sb("rows", [P, NROW])
        ident = sb("ident", [P, P])
        ones = sb("ones", [P, P])
        tri = sb("tri", [P, P])
        trib = sb("trib", [P, P])
        tris = sb("tris", [P, P])
        block1 = sb("block1", [P, P])
        w_dt = sb("w_dt", [P, KD, 8])
        w_gm = sb("w_gm", [P, KD, 16])
        w_rt = sb("w_rt", [P, KD, 36])
        mod = sb("mod", [P, 48])
        cact = sb("cact", [P, 8])
        aff = sb("aff", [P, 8])
        small = sb("small", [P, 960])
        smi = sb("smi", [P, 64], I32)
        tabT = arena[0:8, 13336:13336 + BUCKETS]
        e1 = arena[0:8, 13400:13400 + 383]
        zero = arena[:, 16128:16128 + 256]

        def view(base, at, *shape):
            n = int(np.prod(shape))
            v = base[:, at:at + n]
            if len(shape) == 1:
                return v
            if len(shape) == 2:
                return v.rearrange("p (a b) -> p a b", b=shape[1])
            return v.rearrange("p (a b c) -> p a b c", b=shape[1], c=shape[2])

        sm_at = [0]

        def sm(*shape):
            at = sm_at[0]
            sm_at[0] += int(np.prod(shape))
            assert sm_at[0] <= 960
            return view(small, at, *shape)

        def col(name, i=0, n=1):
            at, w = COLS[name]
            return cols[:, at + i:at + i + n]

        def row(name, i=0, n=None):
            at, w = ROWP[name]
            return rows[:, at + i:at + i + (w if n is None else n)]

        qT = view(upper, 0, 4, T)
        kT = view(upper, 2048, 4, T)
        vtok = view(upper, 4096, NT, 512)
        ztok = view(upper, 6144, NT, 512)
        xraw = view(arena, 0, KD, T + 3)
        yT = view(arena, 0, KD, T)
        xbcT = view(arena, 4120, KD, T)
        T1 = view(arena, 8216, HEADS, 256)
        Btok = view(arena, 10264, NT, 256)
        xstok = view(arena, 11288, NT, 512)
        pr = view(arena, 13336, 2, 512)
        prT = view(arena, 14360, 2, 512)
        diag = view(arena, 8216, 8, P)
        Mt = view(arena, 9240, 8, P)
        xdt = view(arena, 13336, 512)
        xde = view(arena, 13848, 512)
        H = view(arena, 14360, 512)
        y = view(arena, 14872, 512)
        y2 = view(upper, 0, 512)
        CBm = view(arena, 15872, 2, P)
        actT = view(arena, 0, FT, T)
        acc = view(arena, FT * T, 2, 4, T)
        mraw = view(arena, 0, KD, T + 4)
        yaT = view(arena, 0, 4, T)
        ymT = view(arena, 2048, 4, T)
        vaug = view(arena, 4128, NT, MH * (P + 1))
        omtok = view(arena, 6192, NT, 512)
        qaT = view(arena, 8240, 5, T)
        kaS = view(arena, 10800, T)
        vatok = view(arena, 11312, NT, P)
        T2 = view(arena, 11824, HEADS, 384)
        pr2 = view(arena, 14896, 2, 384)
        pr2T = view(arena, 15664, 2, 384)
        mconv = view(upper, 0, KD, T)
        sq2 = view(upper, 4096, 5, T)
        Wm = view(upper, 4096, NT, T)
        dgm = view(upper, 6144, NT, P)
        hm = view(upper, 6656, NT, P)
        rowv = view(upper, 7168, 2, T)
        uT = view(upper, 0, KD, T)
        mg_s = view(arena, 8240, 2, 4, T)
        xtok = view(arena, 0, NT, D)
        htok = view(arena, 4096, NT, D)
        xsr = view(arena, 8192, 2, D)
        xsT = view(arena, 10240, KD, P)
        sg = view(arena, 11264, 2, 256)
        hE = view(arena, 11776, 2, 256)
        ysb = view(arena, 12288, D)
        ws = [ring[0], ring[1], ring[2], ring[3], upper[:, 0:SLOT], upper[:, SLOT:2 * SLOT]]

        def slot(i, k, n):
            return ws[i][:, 0:k * n].rearrange("p (k n) -> p k n", n=n)

        dtr = sm(NT, 8)
        dtv = sm(NT, 8)
        adt = sm(NT, 8)
        acs = sm(NT, 8)
        nacs = sm(NT, 8)
        tot = sm(NT, 8)
        ea = sm(NT, 8)
        dte = sm(NT, 8)
        cd = sm(NT, 8)
        expa = sm(8)
        lp = [sm(64) for _ in range(4)]
        nmax = sm(2)
        asum = sm(2)
        arec = sm(2)
        esk = sm(2)
        ssq = sm(4)
        rsq = sm(4)
        gt = sm(NT, 16)
        lf = sm(NT, 8)
        Ft = sm(NT, 8)
        vt = sm(NT, 8)
        nM = sm(NT, 8)
        em = sm(NT, 8)
        dn = sm(4)
        gk = sm(2)
        eps = sm(1)
        one = sm(1)

        def scratch(name, shape):
            return nc.dram_tensor(name, shape, F32, kind="Internal").ap()

        ext1 = scratch("ext1", (8, 383))
        ext2 = scratch("ext2", (8, 512))
        skew1 = scratch("skew1", (P, HEADS, 383))
        skew2 = scratch("skew2", (P, HEADS, 512))
        xs_d = scratch("xs_d", (ROWS, D))
        ys_d = scratch("ys_d", (ROWS, D))

        names = """ld_cols ld_x ld_rows ld_small ld_tab ld_rel e1_rdy ext1_w ld_T1 ext2_w ld_T2
        consts zeroed t1_masked cact_rdy ada_full mod_rdy
        nsq nsum nvar nroot h_rdy
        dense_full act_free dve_free pads dt_full dt_raw
        s_full s_bias p_max p_exp p_norm pt_full pt_ev o_full o_ev
        conv_rdy conv_silu lx_rdy lx_exp alog_exp dta a_full a_rdy a_exp e2_rdy row_var row_root negs tk_full tk_ev z_rdy
        cb_full dg_rdy r_full seg_rdy seg_exp mt_rdy xd_rdy y_full st_full y_rdy y_sq y_nrm yt_full yt_ev h_upd
        up_full up_first up_g up_silu up_free up_seq dn_full dn_free
        gt_full gt_rdy f_full vt_rdy vr_full scan_rdy mk_full m_rdy m_exp
        qsq qsum qvar qroot qn_rdy swapped ms_full dgm_rdy u_full wd_rdy w_exp w_rdy n_full hm_rdy hm_sq hm_fin hmt_full hmt_ev
        mg_full mg_sig mg_free u_rdy
        xk_full xk_ev xk_sq htok_rdy xg_rdy lg_full lg_rdy lg_exp top_rdy oh_rdy rank_full slots_rdy tab_rdy scattered
        ld_xs xt_full xt_ev g_full uu_full sil_rdy he_rdy yy_full yy_ev y_st
        ov_w ov_xs ov_xt ov_xte ov_g ov_sil ov_he ov_y ov_ye ov_st stored comb out_st
        vseq pseq """.split()
        S = {n: sem(n) for n in names}
        landed = [sem(f"landed{i}") for i in range(6)]
        gath = [sem(f"gathered{t}") for t in range(NT)]


        owners = []

        def groups(n, who):
            first = len(owners)
            owners.extend(who[i % len(who)] for i in range(n))
            return first

        G_Q = groups(4, "AV")
        G_K = groups(4, "AV")
        G_V = groups(4, "AV")
        G_XBC = groups(8, "AV")
        G_Z = groups(4, "AV")
        G_WO = groups(8, "V")
        G_QA = groups(4, "AV")
        G_KA = groups(1, "A")
        G_VA = groups(1, "V")
        G_QM = groups(8, "AV")
        G_VM = groups(4, "AV")
        G_OM = groups(4, "A")
        G_WO2 = groups(8, "V")

        def emptied(g):
            who = owners[g]
            return (S["act_free"] if who == "A" else S["dve_free"]), owners[:g + 1].count(who)

        loads = [0] * 6

        ATT1 = [(h, q, 0, q + 1) for h in range(HEADS) for q in range(NT)]
        ATT2 = [(h, q, max(q - 1, 0), min(q + 1, NT - 1) - max(q - 1, 0) + 1) for h in range(HEADS) for q in range(NT)]
        NI = len(ATT1)

        R = {}
        r_at = 13312
        for name, shape in (("lg", (NT, 36)), ("gs", (NT, 4)), ("ge", (NT, 4)), ("g1", (NT, 4)), ("r4", (4,)), ("io", (E,)),
                            ("gm", (NT,)), ("gx", (NT,)), ("pg", (NT,)), ("em", (NT, E)), ("top", (NT, 8)), ("ix", (NT, 8)),
                            ("d", (NT,)), ("w1", (NT,)), ("ed", (NT,)), ("oh1", (NT, E)), ("oh2", (NT, E)), ("ohs", (NT, E)),
                            ("rk", (NT, E)), ("ct", (E,)), ("nb", (E,)), ("t1", (E,)), ("cin", (E,)), ("adj", (E,)),
                            ("fs", (NT, E)), ("t2", (NT, E)), ("sl", (2, NT)), ("be", (OVB + 1, E)), ("bx", (OVB + 1,)),
                            ("i15", (OVB + 1,))):
            R[name] = view(arena, r_at, *shape)
            r_at += int(np.prod(shape))
        assert r_at <= W, r_at
        wt = sm(2, NT)
        io_i = smi[:, 0:32]
        slot_i = smi[:, 32:40]
        e2 = view(arena, 15360, 512)
        rs = view(arena, W - 512, 512)
        mnf = sb("mnf", [P, P])
        mnb = sb("mnb", [P, P])
        junk = view(arena, 14896, NT, P)

        dest = {}
        for c in range(4):
            dest[G_Q + c] = (qT[:, c, :], HD ** -0.5)
            dest[G_K + c] = (kT[:, c, :], 1.0)
            dest[G_V + c] = (vtok[:, c, :], 1.0)
            dest[G_Z + c] = (ztok[:, c, :], 1.0)
            dest[G_QA + c] = (qaT[:, c, :], 1.0)
            dest[G_VM + c] = (vaug[:, c, :].rearrange("p (h d) -> p h d", d=P + 1)[:, :, 0:P], 1.0)
        dest[G_KA] = (qaT[:, 4, :], 1.0)
        dest[G_VA] = (vatok.rearrange("p t d -> p (t d)"), 1.0)
        for c in range(8):
            dest[G_XBC + c] = (xraw[:, c, 3:3 + T], 1.0)
            dest[G_QM + c] = (mraw[:, c, 2:2 + T], 1.0)

        def src_of(g):
            b = bank[g % 4][:, :]
            return b.rearrange("p (h d) -> p h d", d=P) if G_VM <= g < G_VM + 4 else b

        block = ctx.enter_context(nc.Block())
        stages = ["ada", "norm", "proj", "att", "ssd", "wout", "ffn", "norm2", "proj2", "att2", "mlstm", "merge", "route", "end"]
        last = stages.index(stop)

        def on(st):
            return stages.index(st) <= last

        def kp(w, c0, n):
            return w[:, c0:c0 + n].rearrange("(k p) n -> p k n", p=P)

        arrived = {}

        @block.sync
        def _(sp):
            def load(tag, i, src, after=None, part=None):
                if after is not None:
                    sp.wait_ge(*after)
                k, n = src.shape[1], src.shape[2]
                dst = slot(i, k, n) if part is None else slot(i, k, 512)[:, :, part:part + n]
                sp.dma_start(dst, src).then_inc(landed[i], 16)
                loads[i] += 1
                arrived[tag] = (landed[i], 16 * loads[i])

            def dense(g):
                return (S["dense_full"], g)

            sp.dma_start(cols[:, :], a["cols"]).then_inc(S["ld_cols"], 16)
            sp.dma_start(xT[:, :, :], a["x_t"].rearrange("(k p) t -> p k t", p=P)).then_inc(S["ld_x"], 16)
            for j in range(4):
                load(("ada", j), j, kp(a["w_ada"], j * 512, 512))
            if on("proj"):
                w = a["w_in"]
                load("q", 0, kp(w, Q0, 512), (S["ada_full"], 1))
                load("k", 1, kp(w, K0, 512), (S["ada_full"], 2))
                load("v", 2, kp(w, V0, 512), (S["ada_full"], 3))
                load("xbc0", 3, kp(w, XBC0, 512), (S["ada_full"], 4))
                load("xbc1", 0, kp(w, XBC0 + 512, 512), dense(G_K))
                load("z", 1, kp(w, Z0, 512), dense(G_V))
                for j, (i, after) in enumerate(((2, dense(G_XBC)), (3, dense(G_XBC + 4)), (0, dense(G_Z)), (1, dense(G_WO)),
                                                (2, (S["ada_full"], 5)), (3, (S["ada_full"], 6)), (0, (S["ada_full"], 7)),
                                                (1, (S["ada_full"], 8)))):
                    load(("ada", 4 + j), i, kp(a["w_ada"], (4 + j) * 512, 512), after)
            if on("wout"):
                load("wo0", 2, kp(a["w_out"], 0, 512), (S["ada_full"], 9))
                load("wo1", 3, kp(a["w_out"], 512, 512), (S["ada_full"], 10))
            if on("ffn"):
                wu, wd = a["w_up"], a["w_down"]

                def up(n, i, after):
                    load(("up", i), i, kp(wu, n * 256, 256), after, part=0) if isinstance(n, int) else None
                    load(("up", i), i, kp(wu, FFN + n * 256, 256), None, part=256) if isinstance(n, int) else None

                up(0, 0, (S["ada_full"], 11))
                arrived["up0"] = arrived[("up", 0)]
                up(1, 1, (S["ada_full"], 12))
                arrived["up1"] = arrived[("up", 1)]
                load("dn0", 2, kp(wd, 0, P), dense(G_WO + 4))
                load("dn1", 3, kp(wd, P, P), dense(G_WO + 8))
                with sp.Fori(1, 5) as i:
                    for j in range(2):
                        sp.wait_ge(S["up_full"], i * 8 + (4 * j - 4))
                        for half in range(2):
                            src = wu[:, ds(i * 512 + (j * 256 + half * FFN), 256)].rearrange("(k p) n -> p k n", p=P)
                            sp.dma_start(slot(j, KD, 512)[:, :, half * 256:half * 256 + 256], src).then_inc(landed[j], 16)
                for j in range(2):
                    loads[j] += 8
                up(10, 0, (S["up_full"], 36))
                arrived["up10"] = arrived[("up", 0)]
            if on("proj2"):
                w = a["w_in_2"]
                load("kv", 1, kp(w, KA0, 256), (S["up_full"], 40))
                load("qa", 0, kp(w, QA0, 512), (S["up_full"], 44))
            if on("ffn"):
                with sp.Fori(1, 4) as i:
                    for j in range(2):
                        sp.wait_ge(S["dn_full"], i * 2 + (j - 1))
                        sp.dma_start(slot(2 + j, FT, P), wd[:, ds(i * 256 + j * P, P)].rearrange("(k p) n -> p k n", p=P))\
                          .then_inc(landed[2 + j], 16)
                loads[2] += 3
                loads[3] += 3
            if on("proj2"):
                load("qm", 2, kp(w, QM0, 512), (S["dn_full"], 7))
                load("km", 3, kp(w, KM0, 512), (S["dn_full"], 8))
                load("vm", 0, kp(w, VM0, 512), dense(G_KA))
                load("om", 1, kp(w, OM0, 512), dense(G_QM))
            if on("merge"):
                load("wa", 2, a["w_branch_attn_2"].rearrange("(k p) n -> p k n", p=P), dense(G_QM + 4))
                load("wm", 3, a["w_branch_mlstm_2"].rearrange("(k p) n -> p k n", p=P), dense(G_VM))
                for j in range(4):
                    after = (dense(G_OM), dense(G_WO2), (S["mg_full"], 8), (S["mg_full"], 16))[j]
                    load(("mg", j), j % 2, kp(w, MG0 + j * 256, 256), after, part=0)
                    load(("mg", j), j % 2, kp(w, MG0 + D + j * 256, 256), None, part=256)
                load("wo2_0", 2, kp(a["w_out_2"], 0, 512), (S["mg_full"], 32))
                load("wo2_1", 3, kp(a["w_out_2"], 512, 512), (S["mg_full"], 32))
            if on("end"):
                wg, wu, wd = a["w_expert_gate_2"], a["w_expert_up_2"], a["w_expert_down_2"]

                def gate_of(e):
                    return wg[ds(e * D, D), :].rearrange("(k p) f -> p k f", p=P)

                def up_of(e):
                    return wu[ds(e * D, D), :].rearrange("(k p) f -> p k f", p=P)

                def down_of(e):
                    return wd[ds(e * EF, EF), :].rearrange("(k p) d -> p k d", p=P)

                load(("eg", 0), 0, gate_of(0), (S["mg_full"], 24))
                load(("eu", 0), 1, up_of(0), (S["mg_full"], 32))
                load(("ed", 0), 2, down_of(0), dense(G_WO2 + 4))
                load(("eg", 1), 3, gate_of(1), dense(G_WO2 + 8))
                load(("eu", 1), 4, up_of(1))
                load(("ed", 1), 5, down_of(1))
                with sp.Fori(1, E // 2) as p:
                    for b in range(2):
                        sp.wait_ge(S["g_full"], p * 2 + (b - 1))
                        sp.dma_start(slot(3 * b, KD, EF), gate_of(p * 2 + b)).then_inc(landed[3 * b], 16)
                        sp.wait_ge(S["uu_full"], p * 2 + (b - 1))
                        sp.dma_start(slot(3 * b + 1, KD, EF), up_of(p * 2 + b)).then_inc(landed[3 * b + 1], 16)
                        sp.wait_ge(S["yy_full"], p * 2 + (b - 1))
                        sp.dma_start(slot(3 * b + 2, 4, D), down_of(p * 2 + b)).then_inc(landed[3 * b + 2], 16)
                sp.wait_ge(S["yy_full"], E)
                sp.wait_ge(S["tab_rdy"], 1)
                n_more = sp.value_load(smi[0:1, 40:41], min_val=0, max_val=OVB)
                with sp.Fori(0, OVB) as i:
                    with sp.If(n_more > i):
                        e = sp.value_load(smi[0:1, ds(i + 41, 1)], min_val=0, max_val=E - 1)
                        sp.wait_ge(S["ov_y"], i + 1)
                        sp.dma_start(slot(0, KD, EF), gate_of(e)).then_inc(S["ov_w"], 16)
                        sp.dma_start(slot(1, KD, EF), up_of(e)).then_inc(S["ov_w"], 16)
                        sp.dma_start(slot(2, 4, D), down_of(e)).then_inc(S["ov_w"], 16)
                for t in range(NT):
                    sp.wait_ge(S["comb"], t + 1)
                    sp.dma_start(out[t * P:(t + 1) * P, :], xtok[:, t, :]).then_inc(S["out_st"], 16)
                sp.wait_ge(S["out_st"], 16 * NT)
            if dbg is not None:
                sp.wait_ge(S["vseq"], dbg["v"]) if dbg.get("v") else None

        @block.tensor
        def _(pe):
            def full_k(bk, lhs, rhs, n_k=KD, sl=None):
                dst = bank[bk][:, :] if sl is None else sl
                for k in range(n_k):
                    ins = pe.matmul(dst, lhs(k), rhs(k), start=(k == 0), stop=(k == n_k - 1))
                return ins

            def come(tag):
                pe.wait_ge(*arrived[tag])

            def free(g):
                if g >= 4:
                    pe.wait_ge(*emptied(g - 4))

            def feature(g, w, c0, src=None):
                src = hT if src is None else src
                free(g)
                full_k(g % 4, lambda k: w[:, k, c0:c0 + P], lambda k: src[:, k, :]).then_inc(S["dense_full"], 1)

            def token(g, w, t):
                free(g)
                full_k(g % 4, lambda k: hT[:, k, t * P:(t + 1) * P], lambda k: w[:, k, :]).then_inc(S["dense_full"], 1)

            def ada(j):
                come(("ada", j))
                w = slot(j % 4 if j < 4 else (2, 3, 0, 1)[(j - 4) % 4], KD, 512)
                for c in range(4):
                    m = 4 * j + c
                    ins = full_k(0, lambda k: w[:, k, c * P:(c + 1) * P], lambda k: cact[:, k:k + 1],
                                 sl=bank[7][:, m:m + 1])
                ins.then_inc(S["ada_full"], 1)

            def norm_sums(n):
                pe.wait_ge(S["nsq"], n + 1)
                full_k(0, lambda k: ones[:, :], lambda k: hT[:, k, :], sl=bank[6][:, :]).then_inc(S["nsum"], 1)

            def attention(items, first, q_of, k_of, v_of, nblk, pT):
                def scores(i):
                    h, q, k0, n = items[i]
                    x = first + i
                    if x >= 2:
                        pe.wait_ge(S["s_bias"], x - 1)
                    pe.matmul(bank[4 + x % 2][:, 0:n * P], q_of(h, q), k_of(h, k0, n), start=True, stop=True)\
                      .then_inc(S["s_full"], 1)

                def turn(i):
                    h, q, k0, n = items[i]
                    x = first + i
                    pe.wait_ge(S["p_norm"], x + 1)
                    if x >= 2:
                        pe.wait_ge(S["pt_ev"], x - 1)
                    for b in range(n):
                        ins = pe.transpose(bank[6 + x % 2][:, b * P:(b + 1) * P], nblk[:, x % 2, b * P:(b + 1) * P],
                                           ident[:, :])
                    ins.then_inc(S["pt_full"], 1)

                def values(i):
                    h, q, k0, n = items[i]
                    x = first + i
                    pe.wait_ge(S["pt_ev"], x + 1)
                    if i % 8 == 0 and x >= 16:
                        pe.wait_ge(S["o_ev"], x // 8 - 1)
                    po = HD * (h % 2)
                    dst = bank[2 + (x // 8) % 2][po:po + HD, q * P:(q + 1) * P]
                    for b in range(n):
                        ins = pe.matmul(dst, v_of(h, k0 + b), pT[:, x % 2, b * P:(b + 1) * P], start=(b == 0), stop=(b == n - 1))
                    ins.then_inc(S["o_full"], 1)

                scores(0)
                for i in range(NI):
                    if i + 1 < NI:
                        scores(i + 1)
                    turn(i)
                    if i >= 1:
                        values(i - 1)
                values(NI - 1)

            pe.wait_ge(S["consts"], 1)
            pe.wait_ge(S["cact_rdy"], 1)
            for j in range(4):
                ada(j)
            if on("norm"):
                norm_sums(0)
            if on("proj"):
                pe.wait_ge(S["h_rdy"], 1)
                come("q")
                for c in range(4):
                    feature(G_Q + c, slot(0, KD, 512), c * P)
                come("k")
                for c in range(4):
                    feature(G_K + c, slot(1, KD, 512), c * P)
                come("v")
                for t in range(NT):
                    token(G_V + t, slot(2, KD, 512), t)
                come("xbc0")
                for c in range(4):
                    feature(G_XBC + c, slot(3, KD, 512), c * P)
                come("xbc1")
                for c in range(4):
                    feature(G_XBC + 4 + c, slot(0, KD, 512), c * P)
                come("z")
                for t in range(NT):
                    token(G_Z + t, slot(1, KD, 512), t)
                pe.wait_ge(S["ld_small"], 48)
                for t in range(NT):
                    ins = full_k(0, lambda k: hT[:, k, t * P:(t + 1) * P], lambda k: w_dt[:, k, :],
                                 sl=bank[5][:, t * 8:t * 8 + 8])
                ins.then_inc(S["dt_full"], 1)
                for j in range(4, 12):
                    ada(j)
            if on("att"):
                pe.wait_ge(S["mod_rdy"], 2)
                pe.wait_ge(S["dt_raw"], 1)
                pe.wait_ge(*emptied(G_Z + 3))
                pe.wait_ge(*emptied(G_Z + 2))
                attention(ATT1, 0,
                          lambda h, q: qT[HD * (h % 2):HD * (h % 2) + HD, h // 2, q * P:(q + 1) * P],
                          lambda h, k0, n: kT[HD * (h % 2):HD * (h % 2) + HD, h // 2, 0:n * P],
                          lambda h, kt: vtok[:, kt, h * HD:(h + 1) * HD], pr, prT)
            if on("ssd"):
                pe.wait_ge(S["dta"], 1)
                pe.wait_ge(S["o_ev"], 4)
                pe.matmul(bank[0][:, 0:32], tri[:, :], adt.rearrange("p t e -> p (t e)"), start=True, stop=True)
                pe.matmul(bank[0][:, 32:64], ones[:, :], adt.rearrange("p t e -> p (t e)"), start=True, stop=True)\
                  .then_inc(S["a_full"], 1)
                pe.wait_ge(S["conv_silu"], 8)
                for t in range(NT):
                    if t >= 1:
                        pe.wait_ge(S["tk_ev"], 2 * t)
                    for f in range(4):
                        ins = pe.transpose(bank[1][:, f * P:(f + 1) * P], xbcT[:, f, t * P:(t + 1) * P], ident[:, :])
                    ins.then_inc(S["tk_full"], 1)
                    for g in range(2):
                        ins = pe.transpose(bank[2][:, g * P:(g + 1) * P], xbcT[:, 4 + g, t * P:(t + 1) * P], ident[:, :])
                    ins.then_inc(S["tk_full"], 1)
                pe.wait_ge(S["tk_ev"], 8)
                for c in range(NT):
                    ch = slice(c * P, (c + 1) * P)
                    if c >= 1:
                        pe.wait_ge(S["mt_rdy"], c)
                    for g in range(2):
                        ins = pe.matmul(bank[3][:, g * P:(g + 1) * P], xbcT[:, 4 + g, ch], xbcT[:, 6 + g, ch],
                                        start=True, stop=True)
                    ins.then_inc(S["cb_full"], 1)
                    pe.wait_ge(S["dg_rdy"], c + 1)
                    for g in range(2):
                        ins = pe.matmul(bank[4 + g][:, :], ones[:, :], diag[:, 4 * g:4 * g + 4, :],
                                        start=True, stop=True)
                    ins.then_inc(S["r_full"], 1)
                    pe.wait_ge(S["xd_rdy"], c + 1)
                    if c >= 1:
                        pe.wait_ge(S["h_upd"], c)
                    for g in range(2):
                        gs = slice(g * 256, (g + 1) * 256)
                        ins = pe.matmul(bank[7][:, gs], Btok[:, c, g * P:(g + 1) * P], xde[:, gs], start=True, stop=True)
                    ins.then_inc(S["st_full"], 1)
                    if c >= 1:
                        for g in range(2):
                            gs = slice(g * 256, (g + 1) * 256)
                            pe.matmul(bank[6][:, gs], xbcT[:, 6 + g, ch], H[:, gs], start=True, stop=True)
                    pe.wait_ge(S["mt_rdy"], c + 1)
                    for e in range(HEADS):
                        ins = pe.matmul(bank[0][:, e * HD:(e + 1) * HD], Mt[:, e, :], xdt[:, e * HD:(e + 1) * HD],
                                        start=True, stop=True)
                    ins.then_inc(S["y_full"], 1)
                    pe.wait_ge(S["y_nrm"], c + 1)
                    if c >= 1:
                        pe.wait_ge(S["yt_ev"], c)
                    for f in range(4):
                        ins = pe.transpose(bank[1][:, f * P:(f + 1) * P], y[:, f * P:(f + 1) * P], ident[:, :])
                    ins.then_inc(S["yt_full"], 1)
            if on("wout"):
                pe.wait_ge(S["yt_ev"], NT)
                for i in range(2):
                    come(f"wo{i}")
                    for c in range(4):
                        feature(G_WO + 4 * i + c, slot(2 + i, KD, 512), c * P, yT)
            if on("ffn"):
                norm_sums(1)
                pe.wait_ge(S["h_rdy"], 2)

                def up_slab(j, landed_at, reuse):
                    pe.wait_ge(landed[j], landed_at)
                    w = slot(j, KD, 512)
                    for c in range(4):
                        if reuse is not None:
                            pe.wait_ge(S["up_free"], reuse + (c + 1))
                        half = (c % 2) * 256 + (c // 2) * P
                        full_k(4 * j + c, lambda k: w[:, k, half:half + P], lambda k: hT[:, k, :]).then_inc(S["up_full"], 1)

                base = [arrived["up0"][1], arrived["up1"][1]]
                up_slab(0, base[0], None)
                up_slab(1, base[1], None)
                with pe.Fori(1, 5) as i:
                    for j in range(2):
                        up_slab(j, i * 32 + base[j], i * 8 + (4 * j - 8))
                up_slab(0, arrived["up10"][1], 32)
                pe.wait_ge(S["up_free"], 44)
                pe.wait_ge(S["up_silu"], 22)
                pe.wait_ge(S["up_g"], 22)
                base = [arrived["dn0"][1], arrived["dn1"][1]]

                def down_tile(j, landed_at, reuse):
                    pe.wait_ge(landed[2 + j], landed_at)
                    if reuse is not None:
                        pe.wait_ge(S["dn_free"], reuse)
                    w = slot(2 + j, FT, P)
                    full_k(j, lambda k: w[:, k, :], lambda k: actT[:, k, :], n_k=FT).then_inc(S["dn_full"], 1)

                down_tile(0, base[0], None)
                down_tile(1, base[1], None)
                with pe.Fori(1, 4) as i:
                    for j in range(2):
                        down_tile(j, i * 16 + base[j], i * 2 + (j - 1))
                pe.wait_ge(S["dn_free"], 8)
            if on("norm2"):
                norm_sums(2)
                norm_sums(3)
                pe.wait_ge(S["h_rdy"], 4)
            if on("proj2"):
                come("qa")
                for c in range(4):
                    feature(G_QA + c, slot(0, KD, 512), c * P)
                come("kv")
                feature(G_KA, slot(1, KD, 256), 0)
                free(G_VA)
                wkv = slot(1, KD, 256)
                for t in range(NT):
                    ins = full_k(0, lambda k: hT[:, k, t * P:(t + 1) * P], lambda k: wkv[:, k, P:2 * P],
                                 sl=bank[G_VA % 4][:, t * P:(t + 1) * P])
                ins.then_inc(S["dense_full"], 1)
                for i, tag in enumerate(("qm", "km")):
                    come(tag)
                    for c in range(4):
                        feature(G_QM + 4 * i + c, slot(2 + i, KD, 512), c * P)
                for i, (tag, g0) in enumerate((("vm", G_VM), ("om", G_OM))):
                    come(tag)
                    for t in range(NT):
                        token(g0 + t, slot(i, KD, 512), t)
                for t in range(NT):
                    ins = full_k(0, lambda k: hT[:, k, t * P:(t + 1) * P], lambda k: w_gm[:, k, :],
                                 sl=bank[5][:, t * 16:t * 16 + 16])
                ins.then_inc(S["gt_full"], 1)
            if on("att2"):
                pe.wait_ge(S["qsq"], 1)
                pe.wait_ge(*emptied(G_OM + 3))
                pe.wait_ge(*emptied(G_VM + 3))
                for i in range(5):
                    b = (0, 1, 2, 3, 4)[i]
                    pe.matmul(bank[b][:, :], block1[:, :], sq2[:, i, :], start=True, stop=True).then_inc(S["qsum"], 1)
                pe.wait_ge(S["qn_rdy"], 5)
                pe.wait_ge(S["swapped"], 32)
                pe.wait_ge(S["gt_rdy"], 1)

                def k2(h, k0, n):
                    po, kv = HD * (h % 2), h // 4
                    src = qaT[:, 4, :] if kv == h % 2 else kaS
                    return src[po:po + HD, k0 * P:(k0 + n) * P]

                attention(ATT2, NI,
                          lambda h, q: qaT[HD * (h % 2):HD * (h % 2) + HD, h // 2, q * P:(q + 1) * P], k2,
                          lambda h, kt: vatok[:, kt, (h // 4) * HD:(h // 4 + 1) * HD], pr2, pr2T)
            if on("mlstm"):
                pe.wait_ge(S["dta"], 2)
                pe.wait_ge(S["o_ev"], 8)
                for t in range(NT):
                    for d in range(2):
                        others = range(t) if d == 0 else range(t + 1, NT)
                        dst = bank[0][:, t * 8 + 4 * d:t * 8 + 4 * d + 4]
                        for n, i in enumerate(others):
                            pe.matmul(dst, ones[:, :], lf[:, i, 4 * d:4 * d + 4], start=(n == 0), stop=False)
                        ins = pe.matmul(dst, (tri if d == 0 else trib)[:, :], lf[:, t, 4 * d:4 * d + 4],
                                        start=(len(others) == 0), stop=True)
                ins.then_inc(S["f_full"], 1)
                pe.wait_ge(S["vt_rdy"], 1)
                for d in range(2):
                    for t in range(NT):
                        ins = pe.transpose(bank[1 + d][0:4, t * P:(t + 1) * P], vt[:, t, 4 * d:4 * d + 4], ident[:, :])
                ins.then_inc(S["vr_full"], 1)
                pe.wait_ge(S["scan_rdy"], 2)
                for d in range(2):
                    for t in range(NT):
                        ins = pe.transpose(bank[3][:, t * 8 + 4 * d:t * 8 + 4 * d + 4],
                                           rowv[0:4, d, t * P:(t + 1) * P], ident[0:4, 0:4])
                ins.then_inc(S["mk_full"], 1)
                pe.wait_ge(S["m_rdy"], 1)
                pe.wait_ge(S["conv_silu"], 16)
                for h in range(MH):
                    if h >= 1:
                        pe.wait_ge(S["w_rdy"], 8 * h)
                    for j in range(NT):
                        pe.matmul(bank[4 + j][:, :], mconv[:, 4 + h, j * P:(j + 1) * P], mconv[:, h, :],
                                  start=True, stop=True).then_inc(S["ms_full"], 1)
                    for d in range(2):
                        x = 2 * h + d
                        pe.wait_ge(S["dgm_rdy"], x + 1)
                        if x >= 1:
                            pe.wait_ge(S["w_exp"], 4 * x)
                        pe.matmul(bank[0][:, :], ones[:, :], dgm[:, :, :], start=True, stop=True).then_inc(S["u_full"], 1)
                        pe.wait_ge(S["w_rdy"], 4 * x + 4)
                        if x >= 1:
                            pe.wait_ge(S["hm_rdy"], x)
                        if x >= 2 and d == 0:
                            pe.wait_ge(S["hmt_ev"], h)
                        for t in range(NT):
                            js = list(range(t + 1)) if d == 0 else list(range(t, NT))
                            dst = bank[2 + t // 2][:, (t % 2) * (P + 1):(t % 2 + 1) * (P + 1)]
                            for n, j in enumerate(js):
                                ins = pe.matmul(dst, Wm[:, j, t * P:(t + 1) * P], vaug[:, j, h * (P + 1):(h + 1) * (P + 1)],
                                                start=(n == 0), stop=(n == len(js) - 1))
                        ins.then_inc(S["n_full"], 1)
                    pe.wait_ge(S["hm_fin"], h + 1)
                    for t in range(NT):
                        ins = pe.transpose(bank[1][:, t * P:(t + 1) * P], hm[:, t, :], ident[:, :])
                    ins.then_inc(S["hmt_full"], 1)
            if on("merge"):
                pe.wait_ge(S["hmt_ev"], MH)
                pe.wait_ge(S["w_rdy"], 32)
                come("wa")
                come("wm")
                for m in range(KD):
                    if m % 2 == 0:
                        come(("mg", m // 2))
                    wgm = slot((m // 2) % 2, KD, 512)
                    for c in range(4):
                        g = 4 * m + c
                        if g >= 8:
                            pe.wait_ge(S["mg_free"], m - 1)
                        bk = g % 8
                        if c < 2:
                            o = 256 * c + (m % 2) * P
                            ins = full_k(bk, lambda k: wgm[:, k, o:o + P], lambda k: hT[:, k, :])
                        else:
                            w, src = (slot(2, 4, D), yaT) if c == 2 else (slot(3, 4, D), ymT)
                            ins = full_k(bk, lambda k: w[:, k, m * P:(m + 1) * P], lambda k: src[:, k, :], n_k=4)
                        ins.then_inc(S["mg_full"], 1)
                pe.wait_ge(S["u_rdy"], KD)
                for i in range(2):
                    come(f"wo2_{i}")
                    for c in range(4):
                        feature(G_WO2 + 4 * i + c, slot(2 + i, KD, 512), c * P, uT)
            if on("route"):
                pe.wait_ge(*emptied(G_WO2 + 7))
                for x in range(2 * NT):
                    if x >= 2:
                        pe.wait_ge(S["xk_ev"], x - 1)
                    for f in range(4):
                        k = 4 * (x % 2) + f
                        ins = pe.transpose(bank[x % 2][:, f * P:(f + 1) * P], xT[:, k, (x // 2) * P:(x // 2 + 1) * P],
                                           ident[:, :])
                    ins.then_inc(S["xk_full"], 1)
                pe.wait_ge(S["xg_rdy"], KD)
                for t in range(NT):
                    ins = full_k(0, lambda k: hT[:, k, t * P:(t + 1) * P], lambda k: w_rt[:, k, :],
                                 sl=bank[4][:, t * 36:t * 36 + 36])
                ins.then_inc(S["lg_full"], 1)
                pe.wait_ge(S["oh_rdy"], 1)
                for t in range(NT):
                    dst = bank[5][:, t * E:(t + 1) * E]
                    for i in range(t):
                        pe.matmul(dst, ones[:, :], R["ohs"][:, i, :], start=(i == 0), stop=False)
                    pe.matmul(dst, tris[:, :], R["ohs"][:, t, :], start=(t == 0), stop=True)
                full_k(0, lambda k: ones[:, :], lambda k: R["ohs"][:, k, :], n_k=NT, sl=bank[5][:, NT * E:(NT + 1) * E])\
                    .then_inc(S["rank_full"], 1)
            if on("end"):
                base = [arrived[(n, b)][1] for b in range(2) for n in ("eg", "eu", "ed")]

                def pair(p, first):
                    pe.wait_ge(S["ld_xs"], p * 16 + 16)
                    for x in range(2):
                        if not first:
                            pe.wait_ge(S["xt_ev"], p * 2 + (x - 1))
                        for f in range(4):
                            ins = pe.transpose(bank[x][:, f * P:(f + 1) * P],
                                               xsr[:, 0, (4 * x + f) * P:(4 * x + f + 1) * P], ident[:, :])
                        ins.then_inc(S["xt_full"], 1)
                    pe.wait_ge(S["xt_ev"], p * 2 + 2)
                    for b in range(2):
                        ro = slice(b * CAP, (b + 1) * CAP)
                        for half, (sem_full, who) in enumerate(((S["g_full"], S["sil_rdy"]), (S["uu_full"], S["he_rdy"]))):
                            pe.wait_ge(landed[3 * b + half], p * 16 + base[3 * b + half])
                            if not first:
                                pe.wait_ge(who, p * 2 + (b - 1))
                            w = slot(3 * b + half, KD, EF)
                            for f in range(4):
                                ins = full_k(0, lambda k: w[:, k, f * P:(f + 1) * P], lambda k: xsT[:, k, ro],
                                             sl=bank[2 + b + 2 * half][:, f * CAP:(f + 1) * CAP])
                            ins.then_inc(sem_full, 1)
                    for b in range(2):
                        pe.wait_ge(landed[3 * b + 2], p * 16 + base[3 * b + 2])
                        pe.wait_ge(S["he_rdy"], p * 2 + (b + 1))
                        if not first:
                            pe.wait_ge(S["yy_ev"], p)
                        w = slot(3 * b + 2, 4, D)
                        ro = slice(b * CAP, (b + 1) * CAP)
                        for half in range(2):
                            ins = full_k(0, lambda k: hE[:, b, k * CAP:(k + 1) * CAP],
                                         lambda k: w[:, k, half * 512:(half + 1) * 512], n_k=4, sl=bank[6 + half][ro, :])
                        ins.then_inc(S["yy_full"], 1)

                pair(0, True)
                with pe.Fori(1, E // 2) as p:
                    pair(p, False)
                pe.wait_ge(S["yy_ev"], E // 2)
                pe.sem_inc(S["ov_y"], 1)
                pe.wait_ge(S["tab_rdy"], 1)
                n_more = pe.value_load(smi[0:1, 40:41], min_val=0, max_val=OVB)
                with pe.Fori(0, OVB) as i:
                    with pe.If(n_more > i):
                        pe.wait_ge(S["ov_xs"], i * 16 + 16)
                        for x in range(2):
                            for f in range(4):
                                ins = pe.transpose(bank[x][:, f * P:(f + 1) * P],
                                                   xsr[:, 0, (4 * x + f) * P:(4 * x + f + 1) * P], ident[:, :])
                        ins.then_inc(S["ov_xt"], 1)
                        pe.wait_ge(S["ov_xte"], i + 1)
                        pe.wait_ge(S["ov_w"], i * 48 + 48)
                        for half in range(2):
                            w = slot(half, KD, EF)
                            for f in range(4):
                                ins = full_k(0, lambda k: w[:, k, f * P:(f + 1) * P], lambda k: xsT[:, k, 0:CAP],
                                             sl=bank[2 + half][:, f * CAP:(f + 1) * CAP])
                        ins.then_inc(S["ov_g"], 1)
                        pe.wait_ge(S["ov_he"], i + 1)
                        w = slot(2, 4, D)
                        for half in range(2):
                            ins = full_k(0, lambda k: hE[:, 0, k * CAP:(k + 1) * CAP],
                                         lambda k: w[:, k, half * 512:(half + 1) * 512], n_k=4, sl=bank[6 + half][0:CAP, :])
                        ins.then_inc(S["ov_y"], 1)

        def bmid(v, n):
            return v.unsqueeze(1).to_broadcast([v.shape[0], n, v.shape[1]])

        def blast(v, n):
            return v.unsqueeze(len(v.shape)).to_broadcast(list(v.shape) + [n])

        @block.vector
        def _(ve):
            done = {n: 0 for n in S}

            def tell(ins, name):
                ins.then_inc(S[name], 1)
                done[name] += 1
                return done[name]

            def own(name):
                ve.wait_ge(S[name], done[name])

            def seq(ins):
                tell(ins, "vseq")
                own("vseq")

            def empty(g):
                dst, f = dest[g]
                ve.wait_ge(S["dense_full"], g + 1)
                if f == 1.0:
                    ins = ve.tensor_copy(dst, src_of(g))
                else:
                    ins = ve.tensor_scalar(dst, src_of(g), f, None, ALU.mult)
                tell(ins, "dve_free")

            def empties(g0, n):
                for g in range(g0, g0 + n):
                    if owners[g] == "V":
                        empty(g)

            def norm(n, weight, shift, dst):
                ve.wait_ge(S["nsum"], n + 1)
                tell(ve.tensor_scalar(rs, bank[6][:, :], 1.0 / D, EPS, ALU.mult, ALU.add), "nvar")
                ve.wait_ge(S["nroot"], n + 1)
                seq(ve.reciprocal(rs, rs))
                for k in range(KD):
                    if shift is None:
                        ins = ve.scalar_tensor_tensor(dst[:, k, :], xT[:, k, :], weight[:, k:k + 1], rs, ALU.mult, ALU.mult)
                    else:
                        seq(ve.tensor_tensor(dst[:, k, :], xT[:, k, :], rs, ALU.mult))
                        ins = ve.tensor_scalar(dst[:, k, :], dst[:, k, :], weight[:, k:k + 1], shift[:, k:k + 1],
                                               ALU.mult, ALU.add)
                tell(ins, "h_rdy")
                own("h_rdy")

            def log1p_exp(x, n):
                e, z, z2, p = (v[:, 0:n] for v in lp)
                tell(ve.scalar_tensor_tensor(e, x, -1.0, x, ALU.mult, ALU.max), "lx_rdy")
                ve.wait_ge(S["lx_exp"], done["lx_rdy"])
                seq(ve.tensor_scalar(z2, e, 2.0, None, ALU.add))
                seq(ve.reciprocal(z2, z2))
                seq(ve.tensor_tensor(z, e, z2, ALU.mult))
                seq(ve.tensor_tensor(z2, z, z, ALU.mult))
                seq(ve.tensor_scalar(p, z2, 1.0 / 17, None, ALU.mult))
                for m in (15, 13, 11, 9, 7, 5, 3):
                    seq(ve.scalar_tensor_tensor(p, p, 1.0 / m, z2, ALU.add, ALU.mult))
                seq(ve.scalar_tensor_tensor(p, p, 1.0, z, ALU.add, ALU.mult))
                seq(ve.tensor_scalar(p, p, 2.0, None, ALU.mult))
                return p

            def conv(src, dst, f, taps, name, n_f):
                seq(ve.tensor_scalar(dst[:, f, :], src[:, f, 0:T], col(name, f), None, ALU.mult))
                for j in range(1, taps):
                    ins = ve.scalar_tensor_tensor(dst[:, f, :], src[:, f, j:j + T], col(name, j * n_f + f), dst[:, f, :],
                                                  ALU.mult, ALU.add)
                    if j < taps - 1:
                        seq(ins)
                tell(ins, "conv_rdy")

            def attention(items, first, bias, P_, out_of, sink):
                def masked_max(i):
                    h, q, k0, n = items[i]
                    x = first + i
                    ve.wait_ge(S["s_full"], x + 1)
                    if x >= 2:
                        ve.wait_ge(S["pt_full"], x - 1)
                    sc, p = bank[4 + x % 2], P_[:, x % 2, :]
                    tell(bias(h, q, n, sc, p), "s_bias")
                    own("s_bias")
                    m = nmax[:, x % 2:x % 2 + 1]
                    if sink:
                        seq(ve.tensor_reduce(m, p[:, 0:n * P], AX, ALU.max))
                        tell(ve.tensor_scalar(m, m, row("sink", h, 1), -1.0, ALU.max, ALU.mult), "p_max")
                    else:
                        tell(ve.tensor_reduce(m, p[:, 0:n * P], AX, ALU.max, negate=True), "p_max")

                def normalize(i):
                    h, q, k0, n = items[i]
                    x = first + i
                    b = slice(x % 2, x % 2 + 1)
                    ve.wait_ge(S["p_exp"], x + 1)
                    if sink:
                        seq(ve.tensor_tensor(asum[:, b], asum[:, b], esk[:, b], ALU.add))
                    seq(ve.reciprocal(arec[:, b], asum[:, b]))
                    tell(ve.tensor_scalar(P_[:, x % 2, 0:n * P], P_[:, x % 2, 0:n * P], arec[:, b], None, ALU.mult), "p_norm")

                def take(j):
                    ve.wait_ge(S["o_full"], first + 8 * j + 8)
                    tell(ve.tensor_copy(out_of(j), bank[2 + (first // 8 + j) % 2][:, :]), "o_ev")

                masked_max(0)
                for i in range(NI):
                    if i + 1 < NI:
                        masked_max(i + 1)
                    normalize(i)
                    if i % 8 == 3 and i > 8:
                        take(i // 8 - 1)
                take(NI // 8 - 1)

            ve.wait_ge(S["consts"], 1)
            tell(ve.tensor_scalar(mnf[:, :], tri[:, :], -NEG, NEG, ALU.mult, ALU.add), "negs")
            tell(ve.tensor_scalar(mnb[:, :], trib[:, :], -NEG, NEG, ALU.mult, ALU.add), "negs")
            seq(ve.memset(e2[0:8, :], NEG))
            ve.wait_ge(S["ld_tab"], 16)
            for m0, m1, b in bucket_runs():
                ins = ve.tensor_copy(e2[0:8, m0:m1], tabT[:, b:b + 1].to_broadcast([8, m1 - m0]))
            tell(ins, "e2_rdy")

            ve.wait_ge(S["ld_cols"], 16)
            ve.wait_ge(S["ada_full"], 4)
            tell(ve.tensor_tensor(mod[:, 0:16], bank[7][:, 0:16], col("b_ada", 0, 16), ALU.add), "mod_rdy")
            own("mod_rdy")
            seq(ve.scalar_tensor_tensor(aff[:, :], mod[:, 8:16], 1.0, col("norm_mix", 0, 8), ALU.add, ALU.mult))
            if on("norm"):
                ve.wait_ge(S["ld_x"], 16)
                norm(0, aff, mod[:, 0:8], hT)
            if on("proj"):
                empties(G_Q, 24)
                ve.wait_ge(S["dt_full"], 1)
                ve.wait_ge(S["ld_rows"], 16)
                tell(ve.tensor_tensor(dtr, bank[5][:, 0:32].rearrange("p (t e) -> p t e", e=8), bmid(row("dt_bias"), NT), ALU.add),
                     "dt_raw")
                ve.wait_ge(*emptied(G_XBC + 6))
                own("dve_free")
                for f in range(KD):
                    conv(xraw, xbcT, f, 4, "ssd_cw", 8)
                ve.wait_ge(S["ada_full"], 12)
                tell(ve.tensor_tensor(mod[:, 16:48], bank[7][:, 16:48], col("b_ada", 16, 32), ALU.add), "mod_rdy")
            if on("att"):
                ve.wait_ge(S["t1_masked"], 1)
                own("conv_rdy")

                def bias1(h, q, n, sc, p):
                    if q == 0:
                        return ve.tensor_tensor(p[:, 0:P], sc[:, 0:P], T1[:, h, P:2 * P], ALU.add)
                    far = (q - 1) * P
                    if far:
                        ve.tensor_scalar(p[:, 0:far], sc[:, 0:far], row("rel_far", h, 1), None, ALU.add)
                    return ve.tensor_tensor(p[:, far:far + 2 * P], sc[:, far:far + 2 * P], T1[:, h, :], ALU.add)

                attention(ATT1, 0, bias1, pr, lambda j: yT[:, 4 + j, :], False)
            if on("ssd"):
                x = dtr.rearrange("p t e -> p (t e)")
                own("dt_raw")
                l = log1p_exp(x, 32)
                seq(ve.scalar_tensor_tensor(dtv.rearrange("p t e -> p (t e)"), x, 0.0, l, ALU.max, ALU.add))
                ve.wait_ge(S["alog_exp"], 1)
                tell(ve.scalar_tensor_tensor(adt, dtv, -1.0, bmid(expa, NT), ALU.mult, ALU.mult), "dta")
                ve.wait_ge(S["a_full"], 1)
                flat = lambda v: v.rearrange("p t e -> p (t e)")
                seq(ve.tensor_copy(flat(acs), bank[0][:, 0:32]))
                seq(ve.tensor_copy(flat(tot), bank[0][:, 32:64]))
                seq(ve.tensor_scalar(flat(nacs), flat(acs), -1.0, None, ALU.mult))
                tell(ve.tensor_tensor(flat(dte), flat(tot), flat(acs), ALU.subtract), "a_rdy")
                for t in range(NT):
                    ve.wait_ge(S["tk_full"], 2 * t + 1)
                    tell(ve.tensor_copy(xstok[:, t, :], bank[1][:, :]), "tk_ev")
                    ve.wait_ge(S["tk_full"], 2 * t + 2)
                    tell(ve.tensor_copy(Btok[:, t, :], bank[2][:, 0:256]), "tk_ev")
                ve.wait_ge(S["a_exp"], 1)
                ve.wait_ge(S["z_rdy"], 1)
                own("tk_ev")

                def heads(v):
                    return v.rearrange("p (e d) -> p e d", d=HD)

                for c in range(NT):
                    tell(ve.tensor_tensor(diag, bmid(ident[:, :], 8), blast(acs[:, c, :], P), ALU.mult), "dg_rdy")
                    ve.wait_ge(S["cb_full"], c + 1)
                    seq(ve.tensor_tensor(CBm, bank[3][:, 0:256].rearrange("p (g l) -> p g l", l=P), bmid(tri[:, :], 2), ALU.mult))
                    seq(ve.tensor_tensor(heads(xdt), heads(xstok[:, c, :]), blast(dtv[:, c, :], HD), ALU.mult))
                    tell(ve.tensor_tensor(heads(xde), heads(xdt), blast(dte[:, c, :], HD), ALU.mult), "xd_rdy")
                    ve.wait_ge(S["r_full"], c + 1)
                    for e in range(HEADS):
                        ins = ve.tensor_scalar(Mt[:, e, :], bank[4 + e // 4][:, (e % 4) * P:(e % 4 + 1) * P],
                                               nacs[:, c, e:e + 1], 0.0, ALU.add, ALU.min)
                    tell(ins, "seg_rdy")
                    ve.wait_ge(S["seg_exp"], c + 1)
                    ve.tensor_tensor(Mt[:, 0:4, :], Mt[:, 0:4, :], bmid(CBm[:, 0, :], 4), ALU.mult)
                    tell(ve.tensor_tensor(Mt[:, 4:8, :], Mt[:, 4:8, :], bmid(CBm[:, 1, :], 4), ALU.mult), "mt_rdy")
                    seq(ve.tensor_tensor(heads(y2), heads(xstok[:, c, :]), blast(row("d_skip"), HD), ALU.mult))
                    ve.wait_ge(S["y_full"], c + 1)
                    if c == 0:
                        tell(ve.tensor_copy(H, bank[7][:, :]), "h_upd")
                    else:
                        seq(ve.tensor_tensor(heads(H), heads(H), blast(cd[:, c, :], HD), ALU.mult))
                        tell(ve.tensor_tensor(H, H, bank[7][:, :], ALU.add), "h_upd")
                        own("h_upd")
                    seq(ve.tensor_tensor(y2, y2, bank[0][:, :], ALU.add))
                    if c >= 1:
                        seq(ve.tensor_tensor(heads(y), heads(bank[6][:, :]), blast(ea[:, c, :], HD), ALU.mult))
                        seq(ve.tensor_tensor(y2, y, y2, ALU.add))
                    own("h_upd")
                    tell(ve.tensor_tensor(y, y2, ztok[:, c, :], ALU.mult), "y_rdy")
                    ve.wait_ge(S["y_sq"], c + 1)
                    tell(ve.tensor_scalar(rsq[:, 0:1], ssq[:, 0:1], 1.0 / 512, EPS, ALU.mult, ALU.add), "row_var")
                    ve.wait_ge(S["row_root"], c + 1)
                    seq(ve.reciprocal(rsq[:, 0:1], rsq[:, 0:1]))
                    tell(ve.tensor_scalar(y, y, rsq[:, 0:1], None, ALU.mult), "y_nrm")
                    ve.wait_ge(S["yt_full"], c + 1)
                    tell(ve.tensor_tensor(yT[:, 0:4, c * P:(c + 1) * P], bank[1][:, :].rearrange("p (f t) -> p f t", t=P),
                                          blast(col("ssd_norm", 0, 4), P), ALU.mult), "yt_ev")
            if on("wout"):
                own("mod_rdy")
                for m in range(KD):
                    ve.wait_ge(S["dense_full"], G_WO + m + 1)
                    tell(ve.scalar_tensor_tensor(xT[:, m, :], bank[(G_WO + m) % 4][:, :], mod[:, 16 + m:17 + m],
                                                 xT[:, m, :], ALU.mult, ALU.add), "dve_free")
            if on("ffn"):
                own("dve_free")
                seq(ve.scalar_tensor_tensor(aff[:, :], mod[:, 32:40], 1.0, col("norm_ffn", 0, 8), ALU.add, ALU.mult))
                norm(1, aff, mod[:, 24:32], hT)

                def scal(name, i):
                    return cols[:, ds(i + COLS[name][0], 1)] if not isinstance(i, int) else col(name, i)

                def slab(n, j):
                    for c in range(4):
                        bk, ac = bank[4 * j + c], acc[:, j, c, :]
                        tile = n * 2 + (c // 2 + (FT if c % 2 else 0))
                        ve.wait_ge(S["up_first"], n * 4 + (c + 1))
                        ve.scalar_tensor_tensor(ac[:, 1:T], bk[:, 0:T - 1], scal("ffn_cw", tile + 2 * FT), ac[:, 1:T],
                                                ALU.mult, ALU.add).then_inc(S["up_seq"], 1)
                        ve.wait_ge(S["up_seq"], n * 4 + (c + 1))
                        ve.scalar_tensor_tensor(ac[:, 2:T], bk[:, 0:T - 2], scal("ffn_cw", tile), ac[:, 2:T],
                                                ALU.mult, ALU.add).then_inc(S["up_free"], 1)
                        if c % 2:
                            ve.wait_ge(S["up_free"], n * 4 + (c + 1))
                            ve.wait_ge(S["up_silu"], n * 2 + (c // 2 + 1))
                            at = n * (2 * T) + (c // 2) * T
                            dst = actT[:, n * 2 + c // 2, :] if isinstance(n, int) else \
                                actT.rearrange("p f t -> p (f t)")[:, ds(at, T)]
                            ve.tensor_tensor(dst, acc[:, j, c - 1, :], ac, ALU.mult).then_inc(S["up_g"], 1)

                slab(0, 0)
                slab(1, 1)
                with ve.Fori(1, 5) as i:
                    slab(i * 2, 0)
                    slab(i * 2 + 1, 1)
                slab(10, 0)
                for n in range(KD):
                    ve.wait_ge(S["dn_full"], n + 1)
                    tell(ve.scalar_tensor_tensor(xT[:, n, :], bank[n % 2][:, :], mod[:, 40 + n:41 + n], xT[:, n, :],
                                                 ALU.mult, ALU.add), "dn_free")
                own("dn_free")
            if on("norm2"):
                norm(2, col("final_norm", 0, 8), None, xT)
                norm(3, col("norm1", 0, 8), None, hT)
            if on("proj2"):
                empties(G_QA, G_OM - G_QA)
                ve.wait_ge(S["gt_full"], 1)
                tell(ve.tensor_tensor(gt, bank[5][:, 0:64].rearrange("p (t e) -> p t e", e=16), bmid(row("gate_b"), NT), ALU.add),
                     "gt_rdy")
                seq(ve.tensor_scalar(gk[:, 0:1], col("q_gain"), HD ** -0.5, None, ALU.mult))
                seq(ve.tensor_copy(gk[:, 1:2], col("k_gain")))
            if on("att2"):
                own("dve_free")
                for i in range(5):
                    ve.wait_ge(S["qsum"], i + 1)
                    tell(ve.tensor_scalar(sq2[:, i, :], bank[i][:, :], 1.0 / HD, EPS, ALU.mult, ALU.add), "qvar")
                for i in range(5):
                    ve.wait_ge(S["qroot"], i + 1)
                    seq(ve.reciprocal(sq2[:, i, :], sq2[:, i, :]))
                    tell(ve.scalar_tensor_tensor(qaT[:, i, :], qaT[:, i, :], gk[:, (1 if i == 4 else 0):(2 if i == 4 else 1)],
                                                 sq2[:, i, :], ALU.mult, ALU.mult), "qn_rdy")
                ve.wait_ge(S["pads"], 1)
                ve.wait_ge(*emptied(G_QM + 6))
                ve.wait_ge(*emptied(G_QM + 7))
                for f in range(KD):
                    conv(mraw, mconv, f, 5, "ml_cw", 8)
                own("conv_rdy")
                ve.wait_ge(S["ld_T2"], 16)

                def bias2(h, q, n, sc, p):
                    j0 = P if q == 0 else 0
                    return ve.tensor_tensor(p[:, 0:n * P], sc[:, 0:n * P], T2[:, h, j0:j0 + n * P], ALU.add)

                attention(ATT2, NI, bias2, pr2, lambda j: yaT[:, j, :], True)
            if on("mlstm"):
                flat = lambda v: v.rearrange("p t e -> p (t e)")
                g5 = gt.rearrange("p t (d k h) -> p t d k h", d=2, k=2)
                fx, ix = lp[3][:, 32:64], lp[2][:, 32:64]
                own("gt_rdy")
                for t in range(NT):
                    ve.tensor_copy(fx[:, t * 8:t * 8 + 8].rearrange("p (d h) -> p d h", d=2), g5[:, t, :, 1, :])
                    ins = ve.tensor_copy(ix[:, t * 8:t * 8 + 8].rearrange("p (d h) -> p d h", d=2), g5[:, t, :, 0, :])
                seq(ins)
                l = log1p_exp(fx, 32)
                tell(ve.scalar_tensor_tensor(flat(lf), fx, 0.0, l, ALU.min, ALU.subtract), "dta")
                ve.wait_ge(S["f_full"], 1)
                seq(ve.tensor_copy(flat(Ft), bank[0][:, 0:32]))
                tell(ve.tensor_tensor(flat(vt), ix, flat(Ft), ALU.subtract), "vt_rdy")
                ve.wait_ge(S["vr_full"], 1)
                for d in range(2):
                    seq(ve.tensor_copy(rowv[0:4, d, :], bank[1 + d][0:4, :]))
                    r = rowv[0:4, d, :] if d == 0 else rowv[0:4, d, ::-1]
                    tell(ve.tensor_tensor_scan(r, r, r, 0.0, ALU.max, ALU.max), "scan_rdy")
                ve.wait_ge(S["mk_full"], 1)
                seq(ve.tensor_scalar(flat(nM), bank[3][:, 0:32], -1.0, None, ALU.mult))
                tell(ve.tensor_tensor(flat(em), flat(Ft), flat(nM), ALU.subtract), "m_rdy")
                ve.wait_ge(S["m_exp"], 1)
                for h in range(MH):
                    for d in range(2):
                        x = 2 * h + d
                        ci = 4 * d + h
                        if x >= 1:
                            ve.wait_ge(S["u_full"], x)
                        tell(ve.tensor_tensor(dgm, bmid(ident[:, :], NT),
                                              nM[:, :, ci:ci + 1].to_broadcast([P, NT, P]), ALU.mult), "dgm_rdy")
                        ve.wait_ge(S["u_full"], x + 1)
                        if x >= 1:
                            ve.wait_ge(S["n_full"], x)
                        for j in range(NT):
                            b = slice(j * P, (j + 1) * P)
                            tell(ve.scalar_tensor_tensor(Wm[:, j, b], bank[0][:, b], vt[:, j, ci:ci + 1],
                                                         (mnf if d == 0 else mnb)[:, :], ALU.add, ALU.add), "wd_rdy")
                        for j in range(NT):
                            r = slice(j * P, T) if d == 0 else slice(0, (j + 1) * P)
                            ve.wait_ge(S["w_exp"], 4 * x + j + 1)
                            ve.wait_ge(S["ms_full"], 4 * h + j + 1)
                            tell(ve.scalar_tensor_tensor(Wm[:, j, r], bank[4 + j][:, r], P ** -0.5, Wm[:, j, r],
                                                         ALU.mult, ALU.mult), "w_rdy")
                        ve.wait_ge(S["n_full"], x + 1)
                        if d == 0 and h >= 1:
                            ve.wait_ge(S["hmt_full"], h)
                        for b in range(2):
                            both = bank[2 + b][:, 0:2 * (P + 1)].rearrange("p (t e) -> p t e", e=P + 1)
                            ins = ve.tensor_copy(dn[:, 2 * b:2 * b + 2], both[:, :, P])
                        seq(ins)
                        seq(ve.scalar_tensor_tensor(dn, dn, -1.0, dn, ALU.mult, ALU.max))
                        seq(ve.tensor_tensor(dn, dn, em[:, :, ci], ALU.max))
                        seq(ve.reciprocal(dn, dn))
                        for t in range(NT):
                            num = bank[2 + t // 2][:, (t % 2) * (P + 1):(t % 2) * (P + 1) + P]
                            if d == 0:
                                ins = ve.tensor_scalar(hm[:, t, :], num, dn[:, t:t + 1], None, ALU.mult)
                            else:
                                ins = ve.scalar_tensor_tensor(hm[:, t, :], num, dn[:, t:t + 1], hm[:, t, :], ALU.mult, ALU.add)
                        tell(ins, "hm_rdy")
                        own("hm_rdy")
                    ve.wait_ge(S["hm_sq"], 4 * h + 4)
                    tell(ve.tensor_scalar(rsq, ssq, 1.0 / P, EPS, ALU.mult, ALU.add), "row_var")
                    ve.wait_ge(S["row_root"], NT + h + 1)
                    seq(ve.reciprocal(rsq, rsq))
                    for t in range(NT):
                        ins = ve.scalar_tensor_tensor(hm[:, t, :], hm[:, t, :], rsq[:, t:t + 1], row("out_gain", h * P, P),
                                                      ALU.mult, ALU.mult)
                    seq(ins)
                    tell(ve.tensor_tensor(hm, hm, omtok[:, :, h * P:(h + 1) * P], ALU.mult), "hm_fin")
                    ve.wait_ge(S["hmt_full"], h + 1)
                    tell(ve.tensor_copy(ymT[:, h, :], bank[1][:, :]), "hmt_ev")
            if on("merge"):
                for m in range(KD):
                    ve.wait_ge(S["mg_sig"], 2 * m + 2)
                    b = m % 2
                    ve.wait_ge(S["mg_full"], 4 * m + 4)
                    ve.tensor_tensor(mg_s[:, b, 2, :], mg_s[:, b, 0, :], bank[(4 * m + 2) % 8][:, :], ALU.mult)
                    tell(ve.tensor_tensor(mg_s[:, b, 3, :], mg_s[:, b, 1, :], bank[(4 * m + 3) % 8][:, :], ALU.mult), "mg_free")
                    own("mg_free")
                    tell(ve.tensor_tensor(uT[:, m, :], mg_s[:, b, 2, :], mg_s[:, b, 3, :], ALU.add), "u_rdy")
                for m in range(KD):
                    ve.wait_ge(S["dense_full"], G_WO2 + m + 1)
                    tell(ve.tensor_tensor(xT[:, m, :], bank[(G_WO2 + m) % 4][:, :], xT[:, m, :], ALU.add), "dve_free")
                own("dve_free")
            if on("route"):
                for x in range(2 * NT):
                    ve.wait_ge(S["xk_full"], x + 1)
                    tell(ve.tensor_copy(xtok[:, x // 2, (x % 2) * 512:(x % 2 + 1) * 512], bank[x % 2][:, :]), "xk_ev")
                for k in range(KD):
                    tell(ve.tensor_scalar(hT[:, k, :], xT[:, k, :], col("norm2", k), None, ALU.mult), "xg_rdy")
                ve.wait_ge(S["xk_sq"], NT)
                tell(ve.tensor_scalar(rsq, ssq, 1.0 / D, EPS, ALU.mult, ALU.add), "row_var")
                ve.wait_ge(S["row_root"], NT + MH + 1)
                seq(ve.reciprocal(rsq, rsq))
                for t in range(NT):
                    tell(ve.tensor_scalar(htok[:, t, :], xtok[:, t, :], rsq[:, t:t + 1], None, ALU.mult), "htok_rdy")
                ve.wait_ge(S["lg_full"], 1)
                for t in range(NT):
                    ins = ve.scalar_tensor_tensor(R["lg"][:, t, :], bank[4][:, t * 36:(t + 1) * 36], rsq[:, t:t + 1],
                                                  row("b_router"), ALU.mult, ALU.add)
                seq(ins)
                seq(ve.tensor_copy(R["io"], io_i))
                seq(ve.tensor_scalar(R["r4"], R["io"][:, 0:4], -1.0, 4.0, ALU.mult, ALU.add))
                seq(ve.tensor_reduce(R["gm"], R["lg"][:, :, 0:4], AX, ALU.max))
                tell(ve.tensor_tensor(R["gs"], R["lg"][:, :, 0:4], blast(R["gm"], 4), ALU.subtract), "lg_rdy")
                own("lg_rdy")
                seq(ve.tensor_scalar(R["g1"], R["gs"], 0.0, None, ALU.is_equal))
                seq(ve.tensor_tensor(R["g1"], R["g1"], bmid(R["r4"], NT), ALU.mult))
                seq(ve.tensor_reduce(R["gx"], R["g1"], AX, ALU.max))
                seq(ve.tensor_tensor(R["g1"], R["g1"], blast(R["gx"], 4), ALU.is_equal))
                seq(ve.tensor_scalar(R["g1"], R["g1"], -NEG, NEG, ALU.mult, ALU.add))
                for t in range(NT):
                    ins = ve.tensor_tensor(R["em"][:, t, :].rearrange("p (g e) -> p g e", e=8),
                                           R["lg"][:, t, 4:36].rearrange("p (g e) -> p g e", e=8),
                                           blast(R["g1"][:, t, :], 8), ALU.add)
                seq(ins)
                for t in range(NT):
                    seq(ve.max(R["top"][:, t, :], R["em"][:, t, :]))
                    seq(ve.max_index(R["ix"][:, t, :].bitcast(U32), R["top"][:, t, :], R["em"][:, t, :]))
                seq(ve.tensor_copy(R["ix"].rearrange("p t e -> p (t e)"), R["ix"].rearrange("p t e -> p (t e)").bitcast(U32)))
                tell(ve.tensor_tensor(R["d"], R["top"][:, :, 1], R["top"][:, :, 0], ALU.subtract), "top_rdy")
                io4 = bmid(R["io"], NT)
                seq(ve.tensor_tensor(R["oh1"], io4, R["ix"][:, :, 0:1].to_broadcast([P, NT, E]), ALU.is_equal))
                seq(ve.tensor_tensor(R["oh2"], io4, R["ix"][:, :, 1:2].to_broadcast([P, NT, E]), ALU.is_equal))
                tell(ve.tensor_tensor(R["ohs"], R["oh1"], R["oh2"], ALU.add), "oh_rdy")
                ve.wait_ge(S["lg_exp"], 2)
                seq(ve.tensor_reduce(R["pg"], R["ge"], AX, ALU.add))
                seq(ve.tensor_scalar(R["w1"], R["ed"], 1.0, None, ALU.add))
                seq(ve.tensor_tensor(R["w1"], R["w1"], R["pg"], ALU.mult))
                seq(ve.reciprocal(wt[:, 0, :], R["w1"]))
                seq(ve.tensor_tensor(wt[:, 1, :], wt[:, 0, :], R["ed"], ALU.mult))
                ve.wait_ge(S["rank_full"], 1)
                seq(ve.tensor_copy(R["rk"].rearrange("p t e -> p (t e)"), bank[5][:, 0:NT * E]))
                seq(ve.tensor_copy(R["ct"], bank[5][:, NT * E:(NT + 1) * E]))
                seq(ve.tensor_scalar(R["nb"], R["ct"], float(CAP), None, ALU.is_gt))
                for b in range(2, T // CAP):
                    seq(ve.tensor_scalar(R["t1"], R["ct"], float(CAP * b), None, ALU.is_gt))
                    seq(ve.tensor_tensor(R["nb"], R["nb"], R["t1"], ALU.add))
                seq(ve.memset(R["t1"], 0.0))
                seq(ve.tensor_tensor_scan(R["cin"], R["nb"], R["t1"], 0.0, ALU.add, ALU.add))
                seq(ve.tensor_tensor(R["adj"], R["cin"], R["nb"], ALU.subtract))
                seq(ve.tensor_tensor(R["adj"], R["adj"], R["io"], ALU.subtract))
                seq(ve.tensor_scalar(R["adj"], R["adj"], float(CAP), float(CAP * (E - 1)), ALU.mult, ALU.add))
                seq(ve.tensor_scalar(R["t2"], R["rk"], float(CAP), None, ALU.is_ge))
                seq(ve.tensor_tensor(R["t2"], R["t2"], bmid(R["adj"], NT), ALU.mult))
                seq(ve.tensor_tensor(R["fs"], R["rk"], R["t2"], ALU.add))
                seq(ve.tensor_scalar(R["t1"], R["io"], float(CAP), None, ALU.mult))
                seq(ve.tensor_tensor(R["fs"], R["fs"], bmid(R["t1"], NT), ALU.add))
                for b, oh in enumerate(("oh1", "oh2")):
                    seq(ve.tensor_tensor(R["t2"], R[oh], R["fs"], ALU.mult))
                    seq(ve.tensor_reduce(R["sl"][:, b, :], R["t2"], AX, ALU.add))
                tell(ve.tensor_copy(slot_i, R["sl"].rearrange("p b t -> p (b t)")), "slots_rdy")
                for i in range(OVB):
                    ins = ve.tensor_scalar(R["be"][0:1, i, :], R["cin"][0:1, :], float(i), None, ALU.is_le)
                seq(ins)
                seq(ve.tensor_reduce(R["bx"][0:1, 0:OVB], R["be"][0:1, 0:OVB, :], AX, ALU.add))
                seq(ve.tensor_scalar(R["bx"][0:1, 0:OVB], R["bx"][0:1, 0:OVB], float(E - 1), None, ALU.min))
                seq(ve.tensor_copy(smi[0:1, 41:41 + OVB], R["bx"][0:1, 0:OVB]))
                tell(ve.tensor_copy(smi[0:1, 40:41], R["cin"][0:1, E - 1:E]), "tab_rdy")
                own("tab_rdy")
            if on("end"):
                n2 = col("norm2", 0, 8)

                def pair(p, first):
                    for x in range(2):
                        ve.wait_ge(S["xt_full"], p * 2 + (x + 1))
                        if not first and x == 0:
                            ve.wait_ge(S["uu_full"], p * 2)
                        ve.tensor_tensor(xsT[:, 4 * x:4 * x + 4, :], bank[x][:, :].rearrange("p (f t) -> p f t", t=P),
                                         blast(n2[:, 4 * x:4 * x + 4], P), ALU.mult).then_inc(S["xt_ev"], 1)
                    for b in range(2):
                        ve.wait_ge(S["sil_rdy"], p * 2 + (b + 1))
                        ve.wait_ge(S["uu_full"], p * 2 + (b + 1))
                        if not first:
                            ve.wait_ge(S["yy_full"], p * 2 + (b - 1))
                        ve.tensor_tensor(hE[:, b, :], sg[:, b, :], bank[4 + b][:, 0:256], ALU.mult).then_inc(S["he_rdy"], 1)

                pair(0, True)
                with ve.Fori(1, E // 2) as p:
                    pair(p, False)
                n_more = ve.value_load(smi[0:1, 40:41], min_val=0, max_val=OVB)
                with ve.Fori(0, OVB) as i:
                    with ve.If(n_more > i):
                        ve.wait_ge(S["ov_xt"], i + 1)
                        for x in range(2):
                            ins = ve.tensor_tensor(xsT[:, 4 * x:4 * x + 4, 0:CAP],
                                                   bank[x][:, :].rearrange("p (f t) -> p f t", t=P)[:, :, 0:CAP],
                                                   blast(n2[:, 4 * x:4 * x + 4], CAP), ALU.mult)
                        ins.then_inc(S["ov_xte"], 1)
                        ve.wait_ge(S["ov_sil"], i + 1)
                        ve.tensor_tensor(hE[:, 0, :], sg[:, 0, :], bank[3][:, 0:256], ALU.mult).then_inc(S["ov_he"], 1)
                for t in range(NT):
                    ve.wait_ge(gath[t], 32)
                    for b in range(2):
                        ins = ve.scalar_tensor_tensor(xtok[:, t, :], ws[b][:, t * D:(t + 1) * D], wt[:, b, t:t + 1],
                                                      xtok[:, t, :], ALU.mult, ALU.add)
                        if b == 0:
                            seq(ins)
                    tell(ins, "comb")

        @block.scalar
        def _(ac):
            done = {n: 0 for n in S}

            def act(dst, src, f, name=None, **kw):
                ins = nc.scalar.activation(dst, src, f, **kw)
                if name:
                    ins.then_inc(S[name], 1)
                    done[name] += 1

            def own(name):
                ac.wait_ge(S[name], done[name])

            def empty(g, f=ACT.Copy):
                dst, fac = dest[g]
                ac.wait_ge(S["dense_full"], g + 1)
                act(dst, src_of(g), f, "act_free", scale=fac)

            def empties(g0, n):
                for g in range(g0, g0 + n):
                    if owners[g] == "A":
                        empty(g)

            def norm(n):
                act(hT[:, :, :], xT[:, :, :], ACT.Square, "nsq")
                ac.wait_ge(S["nvar"], n + 1)
                act(rs, rs, ACT.Sqrt, "nroot")

            def attention(items, first, P_, PT_, sink):
                def exps(i):
                    h, q, k0, n = items[i]
                    x = first + i
                    b = slice(x % 2, x % 2 + 1)
                    ac.wait_ge(S["p_max"], x + 1)
                    if sink:
                        act(esk[:, b], row("sink", h, 1), ACT.Exp, bias=nmax[:, b])
                    act(P_[:, x % 2, 0:n * P], P_[:, x % 2, 0:n * P], ACT.Exp, "p_exp", bias=nmax[:, b], accum_out=asum[:, b])

                def turned(i):
                    h, q, k0, n = items[i]
                    x = first + i
                    ac.wait_ge(S["pt_full"], x + 1)
                    if x >= 2:
                        ac.wait_ge(S["o_full"], x - 1)
                    act(PT_[:, x % 2, 0:n * P], bank[6 + x % 2][:, 0:n * P], ACT.Copy, "pt_ev")

                exps(0)
                for i in range(NI):
                    if i + 1 < NI:
                        exps(i + 1)
                    turned(i)

            ac.dma_start(rows[:, :], a["rows"].partition_broadcast(P)).then_inc(S["ld_rows"], 16)
            ac.dma_start(tabT[:, :], a["table_t"]).then_inc(S["ld_tab"], 16)
            rr = a["rel_rev"]
            ac.dma_start(e1[:, 127:383], rr[:, 0:256]).then_inc(S["ld_rel"], 16)
            for dst, name, c0, n in ((w_dt, "w_in", DT0, 8), (w_gm, "w_in_2", GM0, 16), (w_rt, "w_router", 0, 36)):
                ac.dma_start(dst[:, :, :], kp(a[name], c0, n)).then_inc(S["ld_small"], 16)
            ac.wait_ge(S["ld_cols"], 16)
            act(cact[:, :], col("c", 0, 8), ACT.Silu, "cact_rdy")
            ac.wait_ge(S["ld_rel"], 16)
            act(e1[:, 0:127], e1[:, 127:128].to_broadcast([HEADS, 127]), ACT.Copy, "e1_rdy")
            own("e1_rdy")
            ac.dma_start(ext1, e1).then_inc(S["ext1_w"], 16)
            ac.wait_ge(S["ext1_w"], 16)
            ac.dma_start(skew1, ext1.unsqueeze(0).to_broadcast([P, HEADS, 383])).then_inc(S["ext1_w"], 16)
            ac.wait_ge(S["ext1_w"], 32)
            ac.dma_start(T1, bass.AP(tensor=skew1.tensor, offset=127, ap=[[HEADS * 383 - 1, P], [383, HEADS], [1, 256]]))\
              .then_inc(S["ld_T1"], 16)
            ac.wait_ge(S["ld_rows"], 16)
            act(expa, row("a_log"), ACT.Exp, "alog_exp")
            ac.wait_ge(S["e2_rdy"], 1)
            ac.dma_start(ext2[:, :], e2[0:8, :]).then_inc(S["ext2_w"], 16)
            if on("norm"):
                ac.wait_ge(S["ld_x"], 16)
                norm(0)
            if on("proj"):
                empties(G_Q, 24)
                ac.wait_ge(*emptied(G_Z + 3))
                own("act_free")
                act(ztok, ztok, ACT.Silu, "z_rdy")
                for f in range(KD):
                    ac.wait_ge(S["conv_rdy"], f + 1)
                    act(xbcT[:, f, :], xbcT[:, f, :], ACT.Silu, "conv_silu", bias=col("ssd_cb", f))
            if on("att"):
                ac.wait_ge(S["ext2_w"], 16)
                ac.dma_start(skew2, ext2.unsqueeze(0).to_broadcast([P, HEADS, 512])).then_inc(S["ext2_w"], 16)
                attention(ATT1, 0, pr, prT, False)
            if on("ssd"):
                ac.wait_ge(S["lx_rdy"], 1)
                act(lp[0][:, 0:32], lp[0][:, 0:32], ACT.Exp, "lx_exp", scale=-1.0)
                ac.wait_ge(S["a_rdy"], 1)
                act(ea, acs, ACT.Exp)
                act(cd, tot, ACT.Exp)
                act(dte, dte, ACT.Exp, "a_exp")
                for c in range(NT):
                    ac.wait_ge(S["seg_rdy"], c + 1)
                    act(Mt, Mt, ACT.Exp, "seg_exp")
                    ac.wait_ge(S["y_rdy"], c + 1)
                    act(y2, y, ACT.Square, "y_sq", accum_out=ssq[:, 0:1])
                    ac.wait_ge(S["row_var"], c + 1)
                    act(rsq[:, 0:1], rsq[:, 0:1], ACT.Sqrt, "row_root")
            if on("ffn"):
                ac.wait_ge(*emptied(G_WO + 7))
                norm(1)

                def slab(n, j):
                    for c in range(4):
                        tile = n * 2 + (c // 2 + (FT if c % 2 else 0))
                        w2 = col("ffn_cw", tile + 2 * (2 * FT)) if isinstance(n, int) else \
                            cols[:, ds(tile + (4 * FT + COLS["ffn_cw"][0]), 1)]
                        ac.wait_ge(S["up_full"], n * 4 + (c + 1))
                        if not isinstance(n, int) or n >= 2:
                            ac.wait_ge(S["up_g"], n * 2 + (c // 2 - 3))
                        nc.scalar.activation(acc[:, j, c, :], bank[4 * j + c][:, :], ACT.Copy, scale=w2).then_inc(S["up_first"], 1)
                        if c % 2:
                            ac.wait_ge(S["up_free"], n * 4 + c)
                            nc.scalar.activation(acc[:, j, c - 1, :], acc[:, j, c - 1, :], ACT.Silu).then_inc(S["up_silu"], 1)

                slab(0, 0)
                slab(1, 1)
                with ac.Fori(1, 5) as i:
                    slab(i * 2, 0)
                    slab(i * 2 + 1, 1)
                slab(10, 0)
            if on("norm2"):
                ac.wait_ge(S["dn_free"], 8)
                norm(2)
                ac.wait_ge(S["h_rdy"], 3)
                norm(3)
            if on("proj2"):
                ac.wait_ge(S["ext2_w"], 32)
                ac.wait_ge(S["dn_full"], 8)
                ac.dma_start(T2, bass.AP(tensor=skew2.tensor, offset=127, ap=[[HEADS * 512 - 1, P], [512, HEADS], [1, 384]])).then_inc(S["ld_T2"], 16)
                empties(G_QA, G_OM - G_QA)
                for t in range(NT):
                    ac.wait_ge(S["dense_full"], G_OM + t + 1)
                    act(omtok[:, t, :], bank[(G_OM + t) % 4][:, :], ACT.Sigmoid, "act_free")
            if on("att2"):
                act(sq2, qaT, ACT.Square, "qsq")
                for i in range(5):
                    ac.wait_ge(S["qvar"], i + 1)
                    act(sq2[:, i, :], sq2[:, i, :], ACT.Sqrt, "qroot")
                for f in range(KD):
                    ac.wait_ge(S["conv_rdy"], KD + f + 1)
                    act(mconv[:, f, :], mconv[:, f, :], ACT.Silu, "conv_silu", bias=col("ml_cb", f))
                attention(ATT2, NI, pr2, pr2T, True)
            if on("mlstm"):
                ac.wait_ge(S["lx_rdy"], 2)
                act(lp[0][:, 0:32], lp[0][:, 0:32], ACT.Exp, "lx_exp", scale=-1.0)
                ac.wait_ge(S["m_rdy"], 1)
                act(em, em, ACT.Exp, "m_exp", scale=-1.0)
                for h in range(MH):
                    for d in range(2):
                        x = 2 * h + d
                        ac.wait_ge(S["wd_rdy"], 4 * x + 4)
                        for j in range(NT):
                            b = slice(j * P, (j + 1) * P)
                            r = slice((j + 1) * P, T) if d == 0 else slice(0, j * P)
                            if r.start < r.stop:
                                act(Wm[:, j, r], bank[0][:, r], ACT.Exp, bias=vt[:, j, 4 * d + h:4 * d + h + 1])
                            act(Wm[:, j, b], Wm[:, j, b], ACT.Exp, "w_exp")
                    ac.wait_ge(S["hm_rdy"], 2 * h + 2)
                    for t in range(NT):
                        act(junk[:, t, :], hm[:, t, :], ACT.Square, "hm_sq", accum_out=ssq[:, t:t + 1])
                    ac.wait_ge(S["row_var"], NT + h + 1)
                    act(rsq, rsq, ACT.Sqrt, "row_root")
            if on("merge"):
                for m in range(KD):
                    for c in range(2):
                        ac.wait_ge(S["mg_full"], 4 * m + c + 1)
                        if m >= 2:
                            ac.wait_ge(S["mg_free"], m - 1)
                        act(mg_s[:, m % 2, c, :], bank[(4 * m + c) % 8][:, :], ACT.Sigmoid, "mg_sig",
                            bias=col("merge_b", 8 * c + m))
            if on("route"):
                for t in range(NT):
                    ac.wait_ge(S["xk_ev"], 2 * t + 2)
                    act(htok[:, t, :], xtok[:, t, :], ACT.Square, "xk_sq", accum_out=ssq[:, t:t + 1])
                ac.wait_ge(S["row_var"], NT + MH + 1)
                act(rsq, rsq, ACT.Sqrt, "row_root")
                ac.wait_ge(S["lg_rdy"], 1)
                act(R["ge"], R["gs"], ACT.Exp, "lg_exp")
                ac.wait_ge(S["top_rdy"], 1)
                act(R["ed"], R["d"], ACT.Exp, "lg_exp")
            if on("end"):
                ac.wait_ge(S["scattered"], 16 * 2 * NT)
                ac.dma_start(xsr[:, 0, :], xs_d[0:P, :]).then_inc(S["ld_xs"], 16)

                def pair(p, first, last):
                    for b in range(2):
                        ac.wait_ge(S["g_full"], p * 2 + (b + 1))
                        if not first:
                            ac.wait_ge(S["he_rdy"], p * 2 + (b - 1))
                        nc.scalar.activation(sg[:, b, :], bank[2 + b][:, 0:256], ACT.Silu).then_inc(S["sil_rdy"], 1)
                    if not last:
                        ac.wait_ge(S["xt_full"], p * 2 + 2)
                        ac.dma_start(xsr[:, 0, :], xs_d[ds(p * P + P, P), :]).then_inc(S["ld_xs"], 16)
                    ac.wait_ge(S["yy_full"], p * 2 + 2)
                    if not first:
                        ac.wait_ge(S["y_st"], p * 16)
                    nc.scalar.activation(ysb[:, 0:512], bank[6][:, :], ACT.Copy)
                    nc.scalar.activation(ysb[:, 512:D], bank[7][:, :], ACT.Copy).then_inc(S["yy_ev"], 1)
                    ac.wait_ge(S["yy_ev"], p + 1)
                    ac.dma_start(ys_d[ds(p * P, P), :], ysb[:, :]).then_inc(S["y_st"], 16)

                pair(0, True, False)
                with ac.Fori(1, E // 2 - 1) as p:
                    pair(p, False, False)
                pair(E // 2 - 1, False, True)
                ac.wait_ge(S["y_st"], 16 * (E // 2))
                ac.wait_ge(S["tab_rdy"], 1)
                n_more = ac.value_load(smi[0:1, 40:41], min_val=0, max_val=OVB)
                with ac.Fori(0, OVB) as i:
                    with ac.If(n_more > i):
                        ac.dma_start(xsr[0:CAP, 0, :], xs_d[ds(i * CAP + E * CAP, CAP), :]).then_inc(S["ov_xs"], 16)
                        ac.wait_ge(S["ov_g"], i + 1)
                        nc.scalar.activation(sg[:, 0, :], bank[2][:, 0:256], ACT.Silu).then_inc(S["ov_sil"], 1)
                        ac.wait_ge(S["ov_y"], i + 2)
                        nc.scalar.activation(ysb[0:CAP, 0:512], bank[6][0:CAP, :], ACT.Copy)
                        nc.scalar.activation(ysb[0:CAP, 512:D], bank[7][0:CAP, :], ACT.Copy).then_inc(S["ov_ye"], 1)
                        ac.wait_ge(S["ov_ye"], i + 1)
                        ac.dma_start(ys_d[ds(i * CAP + E * CAP, CAP), :], ysb[0:CAP, :]).then_inc(S["ov_st"], 16)
                        ac.wait_ge(S["ov_st"], i * 16 + 16)
                        nc.scalar.activation(esk[:, 0:1], esk[:, 0:1], ACT.Copy)
                ac.sem_inc(S["stored"], 1)

        @block.gpsimd
        def _(po):
            def then(ins):
                ins.then_inc(S["pseq"], 1)
                steps[0] += 1
                po.wait_ge(S["pseq"], steps[0])

            steps = [0]
            po.memset(ident[:, :], 0.0)
            po.memset(ones[:, :], 1.0)
            po.memset(zero, 0.0)
            then(po.memset(block1[:, :], 0.0))
            then(po.memset(block1[0:HD, 0:HD], 1.0))
            then(po.memset(block1[HD:P, HD:P], 1.0))
            po.affine_select(out=ident[:, :], in_=ident[:, :], compare_op=ALU.not_equal, fill=1.0, base=0,
                             pattern=[[-1, P]], channel_multiplier=1)
            po.memset(xraw[:, :, 0:3], 0.0)
            po.iota(io_i, [[1, E]], base=0, channel_multiplier=0)
            for m, step, mul, op in ((tri, 1, -1, ALU.is_ge), (trib, -1, 1, ALU.is_ge), (tris, 1, -1, ALU.is_gt)):
                ins = po.affine_select(out=m[:, :], in_=ones[:, :], compare_op=op, fill=0.0, base=0, pattern=[[step, P]],
                                       channel_multiplier=mul)
            ins.then_inc(S["consts"], 1)
            po.wait_ge(S["consts"], 1)
            for i in range(4):
                n = ROWS // P // 4
                for j in range(n):
                    r0 = (i * n + j) * P
                    po.dma_start(xs_d[r0:r0 + P, :].rearrange("p (b d) -> p b d", d=256), bmid(zero, 4))\
                      .then_inc(S["zeroed"], 16)
            for r0 in range(E * CAP, ROWS, P):
                po.dma_start(ys_d[r0:r0 + P, :].rearrange("p (b d) -> p b d", d=256), bmid(zero, 4)).then_inc(S["zeroed"], 16)
            po.wait_ge(S["ld_T1"], 16)
            po.memset(T1[0:HD, :, 3 * HD:4 * HD], NEG).then_inc(S["t1_masked"], 1)
            if on("proj2"):
                po.wait_ge(S["dn_full"], 8)
                po.memset(mraw[:, :, 0:2], 0.0)
                po.memset(vaug.rearrange("p t (h d) -> p (t h) d", d=P + 1)[:, :, P:P + 1], 1.0)
                po.memset(mraw[:, :, T + 2:T + 4], 0.0).then_inc(S["pads"], 1)
            if on("att2"):
                po.wait_ge(S["qn_rdy"], 5)
                po.dma_start(kaS[0:HD, :], qaT[HD:P, 4, :]).then_inc(S["swapped"], 16)
                po.dma_start(kaS[HD:P, :], qaT[0:HD, 4, :]).then_inc(S["swapped"], 16)
            if on("end"):
                po.wait_ge(S["slots_rdy"], 1)
                po.wait_ge(S["zeroed"], 16 * (2 * ROWS // P - E * CAP // P))
                for t in range(NT):
                    po.wait_ge(S["htok_rdy"], t + 1)
                    for b in range(2):
                        po.indirect_dma_start(xs_d, bass.IndirectOffsetOnAxis(ap=slot_i[:, b * NT + t:b * NT + t + 1], axis=0),
                                              htok[:, t, :], None).then_inc(S["scattered"], 16)
                po.wait_ge(S["stored"], 1)
                for t in range(NT):
                    for b in range(2):
                        po.indirect_dma_start(ws[b][:, t * D:(t + 1) * D], None, ys_d,
                                              bass.IndirectOffsetOnAxis(ap=slot_i[:, b * NT + t:b * NT + t + 1], axis=0))\
                          .then_inc(gath[t], 16)
                for t in range(NT):
                    po.wait_ge(gath[t], 32)

    return nc


def columns(v, tiles):
    return np.asarray(v).reshape(-1, P).T


def kernel(**inp):
    import concourse.bacc as bacc
    from concourse.bass_utils import run_bass_kernel_spmd as run

    x = {k: np.asarray(v) for k, v in inp.items()}
    one = {k: (v[0] if k not in ("x", "c", "final_norm_w", "rel_bias_table_2") else v) for k, v in x.items()}
    cvals = {
        "c": one["c"], "norm_mix": one["norm_mix_w"], "b_ada": one["b_ada"], "ssd_cw": one["ssd_conv_w"],
        "ssd_cb": one["ssd_conv_b"], "norm_ffn": one["norm_ffn_w"], "ffn_cw": one["ffn_conv_w"],
        "final_norm": one["final_norm_w"], "norm1": one["norm1_g_2"], "ssd_norm": one["ssd_norm_w"],
        "ml_cw": one["mlstm_conv_w_2"], "ml_cb": one["mlstm_conv_b_2"], "merge_b": one["merge_b_2"],
        "norm2": one["norm2_g_2"], "q_gain": np.tile(one["attn_q_gain_2"], 2), "k_gain": np.tile(one["attn_k_gain_2"], 2),
    }
    rvals = {
        "dt_bias": one["dt_bias"], "a_log": one["a_log"], "d_skip": one["d_skip"], "rel_far": one["rel_bias"][:, 2 * MAX_REL],
        "sink": one["attn_sink_2"], "b_router": np.concatenate([one["b_router_group_2"], one["b_router_expert_2"]]),
        "gate_b": one["mlstm_gate_b_2"].reshape(-1), "out_gain": one["mlstm_out_gain_2"].reshape(-1),
    }
    arrays = {
        "x_t": x["x"][0].T,
        "cols": np.concatenate([columns(cvals[n], w) for n, (_, w) in COLS.items()], axis=1),
        "rows": np.concatenate([rvals[n].reshape(-1) for n in ROWP]),
        "table_t": one["rel_bias_table_2"].T,
        "rel_rev": one["rel_bias"][:, ::-1],
        "w_router": np.concatenate([one["w_router_group_2"], one["w_router_expert_2"]], axis=1),
        "w_expert_gate_2": one["w_expert_gate_2"].reshape(E * D, EF),
        "w_expert_up_2": one["w_expert_up_2"].reshape(E * D, EF),
        "w_expert_down_2": one["w_expert_down_2"].reshape(E * EF, D),
    }
    for n in ("w_ada", "w_in", "w_out", "w_up", "w_down", "w_in_2", "w_branch_attn_2", "w_branch_mlstm_2", "w_out_2"):
        arrays[n] = one[n]
    arrays = {k: np.ascontiguousarray(v) for k, v in arrays.items()}
    nc = bacc.Bacc("TRN2", target_bir_lowering=False, num_devices=1)
    aps = {k: nc.dram_tensor(f"in_{k}", v.shape, F32, kind="ExternalInput").ap() for k, v in arrays.items()}
    out = nc.dram_tensor("out", (T, D), F32, kind="ExternalOutput").ap()
    two_blocks(nc, aps, out)
    r = run(nc, [{f"in_{k}": v for k, v in arrays.items()}], core_ids=[0])
    return r.results[0]["out"].reshape(1, T, D)
```

```python
import math
from contextlib import ExitStack

import numpy as np

import concourse.bass as bass
from concourse import mybir

F32 = mybir.dt.float32
I32 = mybir.dt.int32
U32 = mybir.dt.uint32
ALU = mybir.AluOpType
ACT = mybir.ActivationFunctionType
AX = mybir.AxisListType.X
ds = bass.ds

P = 128
T = 512
NT = T // P
D = 1024
KD = D // P
EPS = 1e-6
NEG = -1e30

HEADS = 8
HD = 64
FFN = 2816
FT = FFN // P
MAX_REL = 128
Z0, XBC0, DT0, Q0, K0, V0 = 0, 512, 1536, 1544, 2056, 2568
QA0, KA0, QM0, KM0, VM0, OM0, GM0, MG0 = 0, 512, 768, 1280, 1792, 2304, 2816, 2832
WIN = 128
BUCKETS = 32
MH = 4
E = 32
EF = 512
CAP = 64
OVB = (2 * T) // CAP - 1
ROWS = 3072
assert ROWS >= (E + OVB) * CAP

COLS = {}
_at = 0
for _n, _w in (("c", 8), ("norm_mix", 8), ("b_ada", 48), ("ssd_cw", 32), ("ssd_cb", 8), ("norm_ffn", 8),
               ("ffn_cw", 3 * 2 * FT), ("final_norm", 8), ("norm1", 8), ("ssd_norm", 4), ("ml_cw", 40),
               ("ml_cb", 8), ("merge_b", 16), ("norm2", 8), ("q_gain", 1), ("k_gain", 1)):
    COLS[_n] = (_at, _w)
    _at += _w
NCOL = _at
ROWP = {}
_at = 0
for _n, _w in (("dt_bias", 8), ("a_log", 8), ("d_skip", 8), ("rel_far", 8), ("sink", 8), ("b_router", 36),
               ("gate_b", 16), ("out_gain", 512)):
    ROWP[_n] = (_at, _w)
    _at += _w
NROW = _at


def bucket_runs():
    half, exact = BUCKETS // 2, BUCKETS // 4
    rel = np.arange(-WIN, WIN + 1)
    n = np.abs(rel)
    nf = np.maximum(n, 1).astype(np.float32)
    large = exact + (np.log(nf / exact) / math.log(128 / exact) * (half - exact)).astype(np.int32)
    b = np.where(rel > 0, half, 0) + np.where(n < exact, n, np.minimum(large, half - 1))
    runs, s = [], 0
    for i in range(1, len(b) + 1):
        if i == len(b) or b[i] != b[s]:
            runs.append((s - WIN + 255, i - WIN + 255, int(b[s])))
            s = i
    return runs


def two_blocks(nc, a, out):
    ctx = ExitStack()
    with ctx:
        def sb(name, shape, dt=F32):
            return ctx.enter_context(nc.sbuf_tensor(name, shape, dt))

        def sem(name):
            return ctx.enter_context(nc.semaphore(name))

        bank = [ctx.enter_context(nc.psum_tensor(f"bank{i}", [P, 512], F32)) for i in range(8)]

        SLOT = 4096
        ring = [sb(f"slot{i}", [P, SLOT]) for i in range(4)]
        upper = sb("upper", [P, 2 * SLOT])
        xT = sb("xT", [P, KD, T])
        hT = sb("hT", [P, KD, T])
        W = 16896
        arena = sb("arena", [P, W])
        cols = sb("cols", [P, NCOL])
        rows = sb("rows", [P, NROW])
        ident = sb("ident", [P, P])
        ones = sb("ones", [P, P])
        tri = sb("tri", [P, P])
        trib = sb("trib", [P, P])
        tris = sb("tris", [P, P])
        block1 = sb("block1", [P, P])
        w_dt = sb("w_dt", [P, KD, 8])
        w_gm = sb("w_gm", [P, KD, 16])
        w_rt = sb("w_rt", [P, KD, 36])
        mod = sb("mod", [P, 48])
        cact = sb("cact", [P, 8])
        aff = sb("aff", [P, 8])
        small = sb("small", [P, 960])
        smi = sb("smi", [P, 64], I32)
        tabT = arena[0:8, 13336:13336 + BUCKETS]
        e1 = arena[0:8, 13400:13400 + 383]
        zero = arena[:, 16128:16128 + 256]

        def view(base, at, *shape):
            n = int(np.prod(shape))
            v = base[:, at:at + n]
            if len(shape) == 1:
                return v
            if len(shape) == 2:
                return v.rearrange("p (a b) -> p a b", b=shape[1])
            return v.rearrange("p (a b c) -> p a b c", b=shape[1], c=shape[2])

        sm_at = [0]

        def sm(*shape):
            at = sm_at[0]
            sm_at[0] += int(np.prod(shape))
            assert sm_at[0] <= 960
            return view(small, at, *shape)

        def col(name, i=0, n=1):
            at, w = COLS[name]
            return cols[:, at + i:at + i + n]

        def row(name, i=0, n=None):
            at, w = ROWP[name]
            return rows[:, at + i:at + i + (w if n is None else n)]

        qT = view(upper, 0, 4, T)
        kT = view(upper, 2048, 4, T)
        vtok = view(upper, 4096, NT, 512)
        ztok = view(upper, 6144, NT, 512)
        xraw = view(arena, 0, KD, T + 3)
        yT = view(arena, 0, KD, T)
        xbcT = view(arena, 4120, KD, T)
        T1 = view(arena, 8216, HEADS, 256)
        Btok = view(arena, 10264, NT, 256)
        xstok = view(arena, 11288, NT, 512)
        pr = view(arena, 13336, 3, 512)
        prT = view(arena, 14872, 2, 512)
        ada1 = view(arena, 4120, 4, 512)
        ada2 = view(arena, 10264, 6, 512)
        diag = view(arena, 8216, 8, P)
        Mt2 = (view(arena, 9240, 8, P), view(upper, 512, 8, P))
        xdt2 = (view(arena, 13336, 512), view(upper, 1536, 512))
        xde2 = (view(arena, 13848, 512), view(upper, 2048, 512))
        H = view(arena, 14360, 512)
        y = view(arena, 14872, 512)
        y2 = view(upper, 0, 512)
        CBm = view(arena, 15872, 2, P)
        actT = view(arena, 0, FT, T)
        acc = view(arena, FT * T, 2, 4, T)
        mraw = view(arena, 0, KD, T + 4)
        yaT = view(arena, 0, 4, T)
        ymT = view(arena, 2048, 4, T)
        vaug = view(arena, 4128, NT, MH * (P + 1))
        omtok = view(arena, 6192, NT, 512)
        qaT = view(arena, 8240, 5, T)
        kaS = view(arena, 10800, T)
        vatok = view(arena, 11312, NT, P)
        T2 = view(arena, 11824, HEADS, 384)
        pr2 = view(arena, 14896, 3, 384)
        pr2T = view(arena, 16048, 2, 384)
        mconv = view(upper, 0, KD, T)
        sq2 = view(upper, 4096, 5, T)
        Wm2 = (view(upper, 4096, NT, T), view(arena, 8240, NT, T))
        dgm = view(upper, 6144, NT, P)
        hm = view(upper, 6656, NT, P)
        rowv = view(upper, 7168, 2, T)
        uT = view(upper, 0, KD, T)
        mg_s = view(arena, 8240, 2, 4, T)
        xtok = view(arena, 0, NT, D)
        htok = view(arena, 4096, NT, D)
        xsr = view(arena, 8192, D)
        hET = view(arena, 9216, 4, P)
        xsT = view(arena, 10240, KD, P)
        sg = view(arena, 11264, EF)
        hE = view(arena, 11776, EF)
        ysb = view(arena, 12288, D)
        ws = [ring[0], ring[1], ring[2], ring[3], upper[:, 0:SLOT], upper[:, SLOT:2 * SLOT]]

        def slot(i, k, n):
            return ws[i][:, 0:k * n].rearrange("p (k n) -> p k n", n=n)

        dtr = sm(NT, 8)
        dtv = sm(NT, 8)
        adt = sm(NT, 8)
        acs = sm(NT, 8)
        nacs = sm(NT, 8)
        tot = sm(NT, 8)
        ea = sm(NT, 8)
        dte = sm(NT, 8)
        cd = sm(NT, 8)
        expa = sm(8)
        lp = [sm(64) for _ in range(4)]
        nmax = sm(3)
        asum = sm(3)
        arec = sm(3)
        esk = sm(3)
        ssq = sm(4)
        rsq = sm(4)
        gt = sm(NT, 16)
        lf = sm(NT, 8)
        Ft = sm(NT, 8)
        vt = sm(NT, 8)
        nM = sm(NT, 8)
        em = sm(NT, 8)
        dn = sm(4)
        gk = sm(2)
        eps = sm(1)
        one = sm(1)

        def scratch(name, shape):
            return nc.dram_tensor(name, shape, F32, kind="Internal").ap()

        ext1 = scratch("ext1", (8, 383))
        ext2 = scratch("ext2", (8, 512))
        skew1 = scratch("skew1", (P, HEADS, 383))
        skew2 = scratch("skew2", (P, HEADS, 512))
        xs_d = scratch("xs_d", (ROWS, D))
        ys_d = scratch("ys_d", (ROWS, D))

        names = """ld_cols ld_x ld_rows ld_small ld_tab ld_rel e1_rdy ext1_w ld_T1 ext2_w ld_T2
        consts zeroed t1_masked cact_rdy ada_used1 ada_used2 ada_full mod_rdy
        nsq nsum nvar nroot h_rdy
        dense_full act_free dve_free pads dt_full dt_raw
        s_full s_bias p_max p_exp p_norm pt_full pt_ev o_full o_ev
        conv_rdy conv_silu lx_rdy lx_exp alog_exp dta a_full a_rdy a_exp e2_rdy row_var row_root negs tk_full tk_ev z_rdy
        cb_full dg_rdy r_full seg_rdy seg_exp mt_rdy xd_rdy y_full st_full y_rdy y_sq y_nrm yt_full yt_ev h_upd
        up_full up_first up_g up_silu up_free up_seq dn_full dn_free
        gt_full gt_rdy f_full vt_rdy vr_full scan_rdy mk_full m_rdy m_exp
        qsq qsum qvar qroot qn_rdy swapped ms_full dgm_rdy u_full wd_rdy w_exp w_rdy n_full hm_rdy hm_sq hm_fin hmt_full hmt_ev
        mg_full mg_sig mg_free u_rdy
        xk_full xk_ev xk_sq htok_rdy xg_rdy lg_full lg_rdy lg_exp top_rdy oh_rdy rank_full slots_rdy tab_rdy scattered
        ld_xs xt_full xt_ev g_full uu_full sil_rdy he_rdy yy_full yy_ev y_st
        ht_full ht_ev ov_w ov_xs ov_st stored comb out_st
        vseq pseq """.split()
        S = {n: sem(n) for n in names}
        landed = [sem(f"landed{i}") for i in range(6)]
        gath = [sem(f"gathered{t}") for t in range(NT)]


        owners = []

        def groups(n, who):
            first = len(owners)
            owners.extend(who[i % len(who)] for i in range(n))
            return first

        G_Q = groups(4, "AV")
        G_K = groups(4, "AV")
        G_V = groups(4, "AV")
        G_XBC = groups(8, "AV")
        G_Z = groups(4, "AV")
        G_WO = groups(8, "V")
        G_QA = groups(4, "AV")
        G_KA = groups(1, "A")
        G_VA = groups(1, "V")
        G_QM = groups(8, "AV")
        G_VM = groups(4, "AV")
        G_OM = groups(4, "A")
        G_WO2 = groups(8, "V")

        def emptied(g):
            who = owners[g]
            return (S["act_free"] if who == "A" else S["dve_free"]), owners[:g + 1].count(who)

        loads = [0] * 6

        ATT1 = [(h, q, 0, q + 1) for h in range(HEADS) for q in range(NT)]
        ATT2 = [(h, q, max(q - 1, 0), min(q + 1, NT - 1) - max(q - 1, 0) + 1) for h in range(HEADS) for q in range(NT)]
        NI = len(ATT1)

        R = {}
        r_at = 13312
        for name, shape in (("lg", (NT, 36)), ("gs", (NT, 4)), ("ge", (NT, 4)), ("g1", (NT, 4)), ("r4", (4,)), ("io", (E,)),
                            ("gm", (NT,)), ("gx", (NT,)), ("pg", (NT,)), ("em", (NT, E)), ("top", (NT, 8)), ("ix", (NT, 8)),
                            ("d", (NT,)), ("w1", (NT,)), ("ed", (NT,)), ("oh1", (NT, E)), ("oh2", (NT, E)), ("ohs", (NT, E)),
                            ("rk", (NT, E)), ("ct", (E,)), ("nb", (E,)), ("t1", (E,)), ("cin", (E,)), ("adj", (E,)),
                            ("fs", (NT, E)), ("t2", (NT, E)), ("sl", (2, NT)), ("be", (OVB + 1, E)), ("bx", (OVB + 1,)),
                            ("i15", (OVB + 1,))):
            R[name] = view(arena, r_at, *shape)
            r_at += int(np.prod(shape))
        assert r_at <= W, r_at
        wt = sm(2, NT)
        io_i = smi[:, 0:32]
        slot_i = smi[:, 32:40]
        e2 = view(arena, 15360, 512)
        rs = view(arena, W - 512, 512)
        mnf = sb("mnf", [P, P])
        mnb = sb("mnb", [P, P])
        junk = view(arena, 14896, NT, P)

        ADA_SLOT = (2, 2, 2, 3, 2, 0, 3, 2)
        QBANK = (4, 6, 7, 4, 6)

        dest = {}
        for c in range(4):
            dest[G_Q + c] = (qT[:, c, :], HD ** -0.5)
            dest[G_K + c] = (kT[:, c, :], 1.0)
            dest[G_V + c] = (vtok[:, c, :], 1.0)
            dest[G_Z + c] = (ztok[:, c, :], 1.0)
            dest[G_QA + c] = (qaT[:, c, :], 1.0)
            dest[G_VM + c] = (vaug[:, c, :].rearrange("p (h d) -> p h d", d=P + 1)[:, :, 0:P], 1.0)
        dest[G_KA] = (qaT[:, 4, :], 1.0)
        dest[G_VA] = (vatok.rearrange("p t d -> p (t d)"), 1.0)
        for c in range(8):
            dest[G_XBC + c] = (xraw[:, c, 3:3 + T], 1.0)
            dest[G_QM + c] = (mraw[:, c, 2:2 + T], 1.0)

        def src_of(g):
            b = bank[g % 4][:, :]
            return b.rearrange("p (h d) -> p h d", d=P) if G_VM <= g < G_VM + 4 else b

        block = ctx.enter_context(nc.Block())

        def kp(w, c0, n):
            return w[:, c0:c0 + n].rearrange("(k p) n -> p k n", p=P)

        arrived = {}

        @block.sync
        def _(sp):
            def load(tag, i, src, after=None, part=None):
                if after is not None:
                    sp.wait_ge(*after)
                k, n = src.shape[1], src.shape[2]
                dst = slot(i, k, n) if part is None else slot(i, k, 512)[:, :, part:part + n]
                sp.dma_start(dst, src).then_inc(landed[i], 16)
                loads[i] += 1
                arrived[tag] = (landed[i], 16 * loads[i])

            def dense(g):
                return (S["dense_full"], g)

            sp.dma_start(cols[:, :], a["cols"]).then_inc(S["ld_cols"], 16)
            sp.dma_start(xT[:, :, :], a["x_t"].rearrange("(k p) t -> p k t", p=P)).then_inc(S["ld_x"], 16)
            for j in range(4):
                load(("ada", j), j, kp(a["w_ada"], j * 512, 512))
            w = a["w_in"]
            load("q", 0, kp(w, Q0, 512), (S["ada_used1"], 1))
            load("k", 1, kp(w, K0, 512), (S["ada_used1"], 2))
            load("v", 2, kp(w, V0, 512), (S["ada_used1"], 3))
            load("xbc0", 3, kp(w, XBC0, 512), (S["ada_used1"], 4))
            load("xbc1", 0, kp(w, XBC0 + 512, 512), dense(G_K))
            load("z", 1, kp(w, Z0, 512), dense(G_V))
            used = S["ada_used2"]
            for j, after in enumerate((dense(G_XBC), (used, 1), (used, 2), dense(G_XBC + 4), (used, 3), dense(G_Z),
                                       (used, 4), (used, 5))):
                load(("ada", 4 + j), ADA_SLOT[j], kp(a["w_ada"], (4 + j) * 512, 512), after)
            load("wo0", 2, kp(a["w_out"], 0, 512), (S["ada_used2"], 8))
            load("wo1", 3, kp(a["w_out"], 512, 512), (S["ada_used2"], 7))
            wu, wd = a["w_up"], a["w_down"]

            def up(n, i, after):
                load(("up", i), i, kp(wu, n * 256, 256), after, part=0)
                load(("up", i), i, kp(wu, FFN + n * 256, 256), None, part=256)

            up(0, 0, (S["ada_used2"], 6))
            arrived["up0"] = arrived[("up", 0)]
            up(1, 1, dense(G_WO))
            arrived["up1"] = arrived[("up", 1)]
            load("dn0", 2, kp(wd, 0, P), dense(G_WO + 4))
            load("dn1", 3, kp(wd, P, P), dense(G_WO + 8))
            with sp.Fori(1, 5) as i:
                for j in range(2):
                    sp.wait_ge(S["up_full"], i * 8 + (4 * j - 4))
                    for half in range(2):
                        src = wu[:, ds(i * 512 + (j * 256 + half * FFN), 256)].rearrange("(k p) n -> p k n", p=P)
                        sp.dma_start(slot(j, KD, 512)[:, :, half * 256:half * 256 + 256], src).then_inc(landed[j], 16)
            for j in range(2):
                loads[j] += 8
            up(10, 0, (S["up_full"], 36))
            arrived["up10"] = arrived[("up", 0)]
            w = a["w_in_2"]
            load("kv", 1, kp(w, KA0, 256), (S["up_full"], 40))
            load("qa", 0, kp(w, QA0, 512), (S["up_full"], 44))
            with sp.Fori(1, 4) as i:
                for j in range(2):
                    sp.wait_ge(S["dn_full"], i * 2 + (j - 1))
                    sp.dma_start(slot(2 + j, FT, P), wd[:, ds(i * 256 + j * P, P)].rearrange("(k p) n -> p k n", p=P))\
                      .then_inc(landed[2 + j], 16)
            loads[2] += 3
            loads[3] += 3
            load("qm", 2, kp(w, QM0, 512), (S["dn_full"], 7))
            load("km", 3, kp(w, KM0, 512), (S["dn_full"], 8))
            load("vm", 0, kp(w, VM0, 512), dense(G_KA))
            load("om", 1, kp(w, OM0, 512), dense(G_QM))
            load("wa", 2, a["w_branch_attn_2"].rearrange("(k p) n -> p k n", p=P), dense(G_QM + 4))
            load("wm", 3, a["w_branch_mlstm_2"].rearrange("(k p) n -> p k n", p=P), dense(G_VM))
            for j in range(4):
                after = (dense(G_OM), dense(G_WO2), (S["mg_full"], 8), (S["mg_full"], 16))[j]
                load(("mg", j), j % 2, kp(w, MG0 + j * 256, 256), after, part=0)
                load(("mg", j), j % 2, kp(w, MG0 + D + j * 256, 256), None, part=256)
            load("wo2_0", 2, kp(a["w_out_2"], 0, 512), (S["mg_full"], 32))
            load("wo2_1", 3, kp(a["w_out_2"], 512, 512), (S["mg_full"], 32))
            wg, wu, wd = a["w_expert_gate_2"], a["w_expert_up_2"], a["w_expert_down_2"]

            def gate_of(e):
                return wg[ds(e * D, D), :].rearrange("(k p) f -> p k f", p=P)

            def up_of(e):
                return wu[ds(e * D, D), :].rearrange("(k p) f -> p k f", p=P)

            def down_of(e):
                return wd[ds(e * EF, EF), :].rearrange("(k p) d -> p k d", p=P)

            load(("eg", 0), 0, gate_of(0), (S["mg_full"], 24))
            load(("eu", 0), 1, up_of(0), (S["mg_full"], 32))
            load(("ed", 0), 2, down_of(0), dense(G_WO2 + 4))
            load(("eg", 1), 3, gate_of(1), dense(G_WO2 + 8))
            load(("eu", 1), 4, up_of(1))
            load(("ed", 1), 5, down_of(1))
            with sp.Fori(1, E // 2) as p:
                for b in range(2):
                    sp.wait_ge(S["g_full"], p * 2 + (b - 1))
                    sp.dma_start(slot(3 * b, KD, EF), gate_of(p * 2 + b)).then_inc(landed[3 * b], 16)
                    sp.wait_ge(S["uu_full"], p * 2 + (b - 1))
                    sp.dma_start(slot(3 * b + 1, KD, EF), up_of(p * 2 + b)).then_inc(landed[3 * b + 1], 16)
                for b in range(2):
                    sp.wait_ge(S["yy_full"], p * 2 + (b - 1))
                    sp.dma_start(slot(3 * b + 2, 4, D), down_of(p * 2 + b)).then_inc(landed[3 * b + 2], 16)
            sp.wait_ge(S["yy_full"], E)
            sp.wait_ge(S["tab_rdy"], 1)
            n_more = sp.value_load(smi[0:1, 40:41], min_val=0, max_val=OVB)
            with sp.Fori(0, OVB) as i:
                with sp.If(n_more > i):
                    e = sp.value_load(smi[0:1, ds(i + 41, 1)], min_val=0, max_val=E - 1)
                    sp.wait_ge(S["yy_full"], i + E)
                    sp.dma_start(slot(0, KD, EF), gate_of(e)).then_inc(S["ov_w"], 16)
                    sp.dma_start(slot(1, KD, EF), up_of(e)).then_inc(S["ov_w"], 16)
                    sp.dma_start(slot(2, 4, D), down_of(e)).then_inc(S["ov_w"], 16)
            for t in range(NT):
                sp.wait_ge(S["comb"], t + 1)
                sp.dma_start(out[t * P:(t + 1) * P, :], xtok[:, t, :]).then_inc(S["out_st"], 16)
            sp.wait_ge(S["out_st"], 16 * NT)

        @block.tensor
        def _(pe):
            def full_k(bk, lhs, rhs, n_k=KD, sl=None):
                dst = bank[bk][:, :] if sl is None else sl
                for k in range(n_k):
                    ins = pe.matmul(dst, lhs(k), rhs(k), start=(k == 0), stop=(k == n_k - 1))
                return ins

            def come(tag):
                pe.wait_ge(*arrived[tag])

            def free(g):
                if g >= 4:
                    pe.wait_ge(*emptied(g - 4))

            def feature(g, w, c0, src=None):
                src = hT if src is None else src
                free(g)
                full_k(g % 4, lambda k: w[:, k, c0:c0 + P], lambda k: src[:, k, :]).then_inc(S["dense_full"], 1)

            def token(g, w, t):
                free(g)
                full_k(g % 4, lambda k: hT[:, k, t * P:(t + 1) * P], lambda k: w[:, k, :]).then_inc(S["dense_full"], 1)

            def ada(j):
                pe.wait_ge(S["ada_used1"], j + 1) if j < 4 else pe.wait_ge(S["ada_used2"], j - 3)
                acc_, bk = (ada1[:, j, :], 7) if j < 4 else (ada2[:, (j - 4) % 6, :], 1)
                for c in range(4):
                    m = 4 * j + c
                    ins = pe.matmul(bank[bk][:, m:m + 1], acc_[:, c * P:(c + 1) * P], ones[:, 0:1], start=True, stop=True)
                ins.then_inc(S["ada_full"], 1)

            def norm_sums(n):
                pe.wait_ge(S["nsq"], n + 1)
                full_k(0, lambda k: ones[:, :], lambda k: hT[:, k, :], sl=bank[6][:, :]).then_inc(S["nsum"], 1)

            def attention(items, first, q_of, k_of, v_of, nblk, pT, between=None):
                def scores(i):
                    h, q, k0, n = items[i]
                    x = first + i
                    if x >= 2:
                        pe.wait_ge(S["s_bias"], x - 1)
                    pe.matmul(bank[4 + x % 2][:, 0:n * P], q_of(h, q), k_of(h, k0, n), start=True, stop=True)\
                      .then_inc(S["s_full"], 1)

                def turn(i):
                    h, q, k0, n = items[i]
                    x = first + i
                    pe.wait_ge(S["p_norm"], x + 1)
                    if x >= 2:
                        pe.wait_ge(S["pt_ev"], x - 1)
                    for b in range(n):
                        ins = pe.transpose(bank[6 + x % 2][:, b * P:(b + 1) * P], nblk[:, x % 3, b * P:(b + 1) * P],
                                           ident[:, :])
                    ins.then_inc(S["pt_full"], 1)

                def values(i):
                    h, q, k0, n = items[i]
                    x = first + i
                    pe.wait_ge(S["pt_ev"], x + 1)
                    if i % 8 == 0 and x >= 16:
                        pe.wait_ge(S["o_ev"], x // 8 - 1)
                    po = HD * (h % 2)
                    dst = bank[2 + (x // 8) % 2][po:po + HD, q * P:(q + 1) * P]
                    for b in range(n):
                        ins = pe.matmul(dst, v_of(h, k0 + b), pT[:, x % 2, b * P:(b + 1) * P], start=(b == 0), stop=(b == n - 1))
                    ins.then_inc(S["o_full"], 1)

                scores(0)
                scores(1)
                for i in range(NI):
                    if i + 2 < NI:
                        scores(i + 2)
                    turn(i)
                    if i >= 1:
                        values(i - 1)
                    if between:
                        between(i)
                values(NI - 1)

            pe.wait_ge(S["consts"], 1)
            norm_sums(0)
            for j in range(4):
                ada(j)
            pe.wait_ge(S["h_rdy"], 1)
            come("q")
            for c in range(4):
                feature(G_Q + c, slot(0, KD, 512), c * P)
            come("k")
            for c in range(4):
                feature(G_K + c, slot(1, KD, 512), c * P)
            come("v")
            for t in range(NT):
                token(G_V + t, slot(2, KD, 512), t)
            come("xbc0")
            for c in range(4):
                feature(G_XBC + c, slot(3, KD, 512), c * P)
            come("xbc1")
            for c in range(4):
                feature(G_XBC + 4 + c, slot(0, KD, 512), c * P)
            come("z")
            for t in range(NT):
                token(G_Z + t, slot(1, KD, 512), t)
            pe.wait_ge(S["ld_small"], 48)
            for t in range(NT):
                ins = full_k(0, lambda k: hT[:, k, t * P:(t + 1) * P], lambda k: w_dt[:, k, :],
                             sl=bank[5][:, t * 8:t * 8 + 8])
            ins.then_inc(S["dt_full"], 1)
            pe.wait_ge(S["dt_raw"], 1)
            pe.wait_ge(*emptied(G_Z + 3))
            pe.wait_ge(*emptied(G_Z + 2))
            attention(ATT1, 0,
                      lambda h, q: qT[HD * (h % 2):HD * (h % 2) + HD, h // 2, q * P:(q + 1) * P],
                      lambda h, k0, n: kT[HD * (h % 2):HD * (h % 2) + HD, h // 2, 0:n * P],
                      lambda h, kt: vtok[:, kt, h * HD:(h + 1) * HD], pr, prT,
                      between=lambda i: ada(4 + i // 4) if i % 4 == 3 else None)
            pe.wait_ge(S["dta"], 1)
            pe.wait_ge(S["o_ev"], 4)
            pe.wait_ge(S["mod_rdy"], 2)
            pe.matmul(bank[0][:, 0:32], tri[:, :], adt.rearrange("p t e -> p (t e)"), start=True, stop=True)
            pe.matmul(bank[0][:, 32:64], ones[:, :], adt.rearrange("p t e -> p (t e)"), start=True, stop=True)\
              .then_inc(S["a_full"], 1)
            pe.wait_ge(S["conv_silu"], 8)
            for t in range(NT):
                if t >= 1:
                    pe.wait_ge(S["tk_ev"], 2 * t)
                for f in range(4):
                    ins = pe.transpose(bank[1][:, f * P:(f + 1) * P], xbcT[:, f, t * P:(t + 1) * P], ident[:, :])
                ins.then_inc(S["tk_full"], 1)
                for g in range(2):
                    ins = pe.transpose(bank[2][:, g * P:(g + 1) * P], xbcT[:, 4 + g, t * P:(t + 1) * P], ident[:, :])
                ins.then_inc(S["tk_full"], 1)
            pe.wait_ge(S["tk_ev"], 8)

            def cb(c):
                ch = slice(c * P, (c + 1) * P)
                if c >= 1:
                    pe.wait_ge(S["xd_rdy"], c)
                for g in range(2):
                    ins = pe.matmul(bank[3][:, g * P:(g + 1) * P], xbcT[:, 4 + g, ch], xbcT[:, 6 + g, ch],
                                    start=True, stop=True)
                ins.then_inc(S["cb_full"], 1)

            def decays(c):
                pe.wait_ge(S["dg_rdy"], c + 1)
                if c >= 1:
                    pe.wait_ge(S["seg_rdy"], c)
                for g in range(2):
                    ins = pe.matmul(bank[4 + g][:, :], ones[:, :], diag[:, 4 * g:4 * g + 4, :],
                                    start=True, stop=True)
                ins.then_inc(S["r_full"], 1)

            def turn_y(c):
                pe.wait_ge(S["y_nrm"], c + 1)
                if c >= 1:
                    pe.wait_ge(S["yt_ev"], c)
                for f in range(4):
                    ins = pe.transpose(bank[1][:, f * P:(f + 1) * P], y[:, f * P:(f + 1) * P], ident[:, :])
                ins.then_inc(S["yt_full"], 1)

            cb(0)
            decays(0)
            for c in range(NT):
                ch = slice(c * P, (c + 1) * P)
                if c >= 1:
                    turn_y(c - 1)
                if c + 1 < NT:
                    cb(c + 1)
                pe.wait_ge(S["xd_rdy"], c + 1)
                if c >= 1:
                    pe.wait_ge(S["h_upd"], c)
                for g in range(2):
                    gs = slice(g * 256, (g + 1) * 256)
                    ins = pe.matmul(bank[7][:, gs], Btok[:, c, g * P:(g + 1) * P], xde2[c % 2][:, gs], start=True, stop=True)
                ins.then_inc(S["st_full"], 1)
                if c >= 1:
                    for g in range(2):
                        gs = slice(g * 256, (g + 1) * 256)
                        pe.matmul(bank[6][:, gs], xbcT[:, 6 + g, ch], H[:, gs], start=True, stop=True)
                pe.wait_ge(S["mt_rdy"], c + 1)
                for e in range(HEADS):
                    ins = pe.matmul(bank[0][:, e * HD:(e + 1) * HD], Mt2[c % 2][:, e, :],
                                    xdt2[c % 2][:, e * HD:(e + 1) * HD], start=True, stop=True)
                ins.then_inc(S["y_full"], 1)
                if c + 1 < NT:
                    decays(c + 1)
            turn_y(NT - 1)
            pe.wait_ge(S["yt_ev"], NT)
            for i in range(2):
                come(f"wo{i}")
                for c in range(4):
                    feature(G_WO + 4 * i + c, slot(2 + i, KD, 512), c * P, yT)
            norm_sums(1)
            pe.wait_ge(S["h_rdy"], 2)

            def up_slab(j, landed_at, reuse):
                pe.wait_ge(landed[j], landed_at)
                w = slot(j, KD, 512)
                for c in range(4):
                    if reuse is not None:
                        pe.wait_ge(S["up_free"], reuse + (c + 1))
                    half = (c % 2) * 256 + (c // 2) * P
                    full_k(4 * j + c, lambda k: w[:, k, half:half + P], lambda k: hT[:, k, :]).then_inc(S["up_full"], 1)

            base = [arrived["up0"][1], arrived["up1"][1]]
            up_slab(0, base[0], None)
            up_slab(1, base[1], None)
            with pe.Fori(1, 5) as i:
                for j in range(2):
                    up_slab(j, i * 32 + base[j], i * 8 + (4 * j - 8))
            up_slab(0, arrived["up10"][1], 32)
            pe.wait_ge(S["up_free"], 44)
            pe.wait_ge(S["up_silu"], 22)
            pe.wait_ge(S["up_g"], 22)
            base = [arrived["dn0"][1], arrived["dn1"][1]]

            def down_tile(j, landed_at, reuse):
                pe.wait_ge(landed[2 + j], landed_at)
                if reuse is not None:
                    pe.wait_ge(S["dn_free"], reuse)
                w = slot(2 + j, FT, P)
                full_k(j, lambda k: w[:, k, :], lambda k: actT[:, k, :], n_k=FT).then_inc(S["dn_full"], 1)

            down_tile(0, base[0], None)
            down_tile(1, base[1], None)
            with pe.Fori(1, 4) as i:
                for j in range(2):
                    down_tile(j, i * 16 + base[j], i * 2 + (j - 1))
            pe.wait_ge(S["dn_free"], 8)
            norm_sums(2)
            norm_sums(3)
            pe.wait_ge(S["h_rdy"], 4)
            come("qa")
            for c in range(4):
                feature(G_QA + c, slot(0, KD, 512), c * P)
            come("kv")
            feature(G_KA, slot(1, KD, 256), 0)
            free(G_VA)
            wkv = slot(1, KD, 256)
            for t in range(NT):
                ins = full_k(0, lambda k: hT[:, k, t * P:(t + 1) * P], lambda k: wkv[:, k, P:2 * P],
                             sl=bank[G_VA % 4][:, t * P:(t + 1) * P])
            ins.then_inc(S["dense_full"], 1)
            for i, tag in enumerate(("qm", "km")):
                come(tag)
                for c in range(4):
                    feature(G_QM + 4 * i + c, slot(2 + i, KD, 512), c * P)
                if i == 0:
                    pe.wait_ge(S["qsq"], 1)
                for n in ((0, 1, 2), (3, 4))[i]:
                    if n >= 3:
                        pe.wait_ge(S["qvar"], n - 2)
                    pe.matmul(bank[QBANK[n]][:, :], block1[:, :], sq2[:, n, :], start=True, stop=True).then_inc(S["qsum"], 1)
            for i, (tag, g0) in enumerate((("vm", G_VM), ("om", G_OM))):
                come(tag)
                for t in range(NT):
                    token(g0 + t, slot(i, KD, 512), t)
            for t in range(NT):
                ins = full_k(0, lambda k: hT[:, k, t * P:(t + 1) * P], lambda k: w_gm[:, k, :],
                             sl=bank[5][:, t * 16:t * 16 + 16])
            ins.then_inc(S["gt_full"], 1)
            pe.wait_ge(*emptied(G_OM + 3))
            pe.wait_ge(*emptied(G_VM + 3))
            pe.wait_ge(S["qn_rdy"], 5)
            pe.wait_ge(S["swapped"], 32)
            pe.wait_ge(S["gt_rdy"], 1)

            def k2(h, k0, n):
                po, kv = HD * (h % 2), h // 4
                src = qaT[:, 4, :] if kv == h % 2 else kaS
                return src[po:po + HD, k0 * P:(k0 + n) * P]

            attention(ATT2, NI,
                      lambda h, q: qaT[HD * (h % 2):HD * (h % 2) + HD, h // 2, q * P:(q + 1) * P], k2,
                      lambda h, kt: vatok[:, kt, (h // 4) * HD:(h // 4 + 1) * HD], pr2, pr2T)
            pe.wait_ge(S["dta"], 2)
            pe.wait_ge(S["o_ev"], 8)
            for t in range(NT):
                for d in range(2):
                    others = range(t) if d == 0 else range(t + 1, NT)
                    dst = bank[0][:, t * 8 + 4 * d:t * 8 + 4 * d + 4]
                    for n, i in enumerate(others):
                        pe.matmul(dst, ones[:, :], lf[:, i, 4 * d:4 * d + 4], start=(n == 0), stop=False)
                    ins = pe.matmul(dst, (tri if d == 0 else trib)[:, :], lf[:, t, 4 * d:4 * d + 4],
                                    start=(len(others) == 0), stop=True)
            ins.then_inc(S["f_full"], 1)
            pe.wait_ge(S["vt_rdy"], 1)
            for d in range(2):
                for t in range(NT):
                    ins = pe.transpose(bank[1 + d][0:4, t * P:(t + 1) * P], vt[:, t, 4 * d:4 * d + 4], ident[:, :])
            ins.then_inc(S["vr_full"], 1)
            pe.wait_ge(S["scan_rdy"], 2)
            for d in range(2):
                for t in range(NT):
                    ins = pe.transpose(bank[3][:, t * 8 + 4 * d:t * 8 + 4 * d + 4],
                                       rowv[0:4, d, t * P:(t + 1) * P], ident[0:4, 0:4])
            ins.then_inc(S["mk_full"], 1)
            pe.wait_ge(S["m_rdy"], 1)
            pe.wait_ge(S["conv_silu"], 16)

            def spread(x):
                pe.wait_ge(S["dgm_rdy"], x + 1)
                if x >= 2:
                    pe.wait_ge(S["w_exp"], 4 * (x - 1))
                pe.matmul(bank[x % 2][:, :], ones[:, :], dgm[:, :, :], start=True, stop=True).then_inc(S["u_full"], 1)

            def turn_head(h):
                pe.wait_ge(S["hm_fin"], h + 1)
                for half in range(2):
                    if h or half:
                        pe.wait_ge(S["hmt_ev"], 2 * h + half)
                    for i in range(2):
                        ins = pe.transpose(bank[2 + i][:, 258:258 + P], hm[:, 2 * half + i, :], ident[:, :])
                    ins.then_inc(S["hmt_full"], 1)

            spread(0)
            for x in range(2 * MH):
                h, d = x // 2, x % 2
                if d == 0:
                    if h >= 1:
                        pe.wait_ge(S["w_rdy"], 8 * h)
                    for j in range(NT):
                        pe.matmul(bank[4 + j][:, :], mconv[:, 4 + h, j * P:(j + 1) * P], mconv[:, h, :],
                                  start=True, stop=True).then_inc(S["ms_full"], 1)
                if x + 1 < 2 * MH:
                    spread(x + 1)
                if d == 0 and h >= 1:
                    turn_head(h - 1)
                    pe.wait_ge(S["hmt_ev"], 2 * h)
                pe.wait_ge(S["w_rdy"], 4 * x + 4)
                if x >= 1:
                    pe.wait_ge(S["hm_rdy"], x)
                for t in range(NT):
                    js = list(range(t + 1)) if d == 0 else list(range(t, NT))
                    dst = bank[2 + t // 2][:, (t % 2) * (P + 1):(t % 2 + 1) * (P + 1)]
                    for n, j in enumerate(js):
                        ins = pe.matmul(dst, Wm2[d][:, j, t * P:(t + 1) * P], vaug[:, j, h * (P + 1):(h + 1) * (P + 1)],
                                        start=(n == 0), stop=(n == len(js) - 1))
                ins.then_inc(S["n_full"], 1)
            turn_head(MH - 1)
            pe.wait_ge(S["hmt_ev"], 2 * MH)
            pe.wait_ge(S["w_rdy"], 32)
            come("wa")
            come("wm")
            for m in range(KD):
                if m % 2 == 0:
                    come(("mg", m // 2))
                wgm = slot((m // 2) % 2, KD, 512)
                for c in range(4):
                    g = 4 * m + c
                    if g >= 8:
                        pe.wait_ge(S["mg_free"], m - 1)
                    bk = g % 8
                    if c < 2:
                        o = 256 * c + (m % 2) * P
                        ins = full_k(bk, lambda k: wgm[:, k, o:o + P], lambda k: hT[:, k, :])
                    else:
                        w, src = (slot(2, 4, D), yaT) if c == 2 else (slot(3, 4, D), ymT)
                        ins = full_k(bk, lambda k: w[:, k, m * P:(m + 1) * P], lambda k: src[:, k, :], n_k=4)
                    ins.then_inc(S["mg_full"], 1)
            pe.wait_ge(S["u_rdy"], KD)
            for i in range(2):
                come(f"wo2_{i}")
                for c in range(4):
                    feature(G_WO2 + 4 * i + c, slot(2 + i, KD, 512), c * P, uT)
            pe.wait_ge(*emptied(G_WO2 + 7))
            for x in range(2 * NT):
                if x >= 2:
                    pe.wait_ge(S["xk_ev"], x - 1)
                for f in range(4):
                    k = 4 * (x % 2) + f
                    ins = pe.transpose(bank[x % 2][:, f * P:(f + 1) * P], xT[:, k, (x // 2) * P:(x // 2 + 1) * P],
                                       ident[:, :])
                ins.then_inc(S["xk_full"], 1)
            pe.wait_ge(S["xg_rdy"], KD)
            for t in range(NT):
                ins = full_k(0, lambda k: hT[:, k, t * P:(t + 1) * P], lambda k: w_rt[:, k, :],
                             sl=bank[4][:, t * 36:t * 36 + 36])
            ins.then_inc(S["lg_full"], 1)
            pe.wait_ge(S["oh_rdy"], 1)
            for t in range(NT):
                dst = bank[5][:, t * E:(t + 1) * E]
                for i in range(t):
                    pe.matmul(dst, ones[:, :], R["ohs"][:, i, :], start=(i == 0), stop=False)
                pe.matmul(dst, tris[:, :], R["ohs"][:, t, :], start=(t == 0), stop=True)
            full_k(0, lambda k: ones[:, :], lambda k: R["ohs"][:, k, :], n_k=NT, sl=bank[5][:, NT * E:(NT + 1) * E])\
                .then_inc(S["rank_full"], 1)
            base = [arrived[(n, b)][1] for b in range(2) for n in ("eg", "eu", "ed")]

            def turn_rows():
                for x in range(2):
                    for f in range(4):
                        ins = pe.transpose(bank[x][:, f * P:(f + 1) * P], xsr[:, (4 * x + f) * P:(4 * x + f + 1) * P],
                                           ident[:, :])
                    ins.then_inc(S["xt_full"], 1)

            def turn_inner():
                for f in range(4):
                    ins = pe.transpose(bank[4][:, f * P:(f + 1) * P], hE[:, f * P:(f + 1) * P], ident[:, :])
                ins.then_inc(S["ht_full"], 1)

            def pair(p, first, last):
                pe.wait_ge(S["xt_ev"], p * 2 + 2)
                for b in range(2):
                    ro = slice(b * CAP, (b + 1) * CAP)
                    for half, full in enumerate(("g_full", "uu_full")):
                        pe.wait_ge(landed[3 * b + half], p * 16 + base[3 * b + half])
                        w = slot(3 * b + half, KD, EF)
                        full_k(0, lambda k: xsT[:, k, ro], lambda k: w[:, k, :], sl=bank[2 + half][ro, :])\
                            .then_inc(S[full], 1)
                if not last:
                    pe.wait_ge(S["ld_xs"], p * 16 + 32)
                    turn_rows()
                pe.wait_ge(S["he_rdy"], p * 2 + 2)
                turn_inner()
                for b in range(2):
                    pe.wait_ge(landed[3 * b + 2], p * 16 + base[3 * b + 2])
                    if b == 0:
                        pe.wait_ge(S["ht_ev"], p + 1)
                        if not first:
                            pe.wait_ge(S["yy_ev"], p)
                    w = slot(3 * b + 2, 4, D)
                    ro = slice(b * CAP, (b + 1) * CAP)
                    for half in range(2):
                        ins = full_k(0, lambda k: hET[:, k, ro], lambda k: w[:, k, half * 512:(half + 1) * 512], n_k=4,
                                     sl=bank[6 + half][ro, :])
                    ins.then_inc(S["yy_full"], 1)

            pe.wait_ge(S["ld_xs"], 16)
            turn_rows()
            pair(0, True, False)
            with pe.Fori(1, E // 2 - 1) as p:
                pair(p, False, False)
            pair(E // 2 - 1, False, True)
            pe.wait_ge(S["tab_rdy"], 1)
            n_more = pe.value_load(smi[0:1, 40:41], min_val=0, max_val=OVB)
            with pe.Fori(0, OVB) as i:
                with pe.If(n_more > i):
                    pe.wait_ge(S["ov_xs"], i * 16 + 16)
                    turn_rows()
                    pe.wait_ge(S["xt_ev"], i + (E + 1))
                    pe.wait_ge(S["ov_w"], i * 48 + 48)
                    for half in range(2):
                        w = slot(half, KD, EF)
                        ins = full_k(0, lambda k: xsT[:, k, 0:CAP], lambda k: w[:, k, :], sl=bank[2 + half][0:CAP, :])
                    ins.then_inc(S["g_full"], 1)
                    pe.wait_ge(S["he_rdy"], i + (E + 1))
                    turn_inner()
                    pe.wait_ge(S["ht_ev"], i + (E // 2 + 1))
                    pe.wait_ge(S["yy_ev"], i + E // 2)
                    w = slot(2, 4, D)
                    for half in range(2):
                        ins = full_k(0, lambda k: hET[:, k, 0:CAP], lambda k: w[:, k, half * 512:(half + 1) * 512], n_k=4,
                                     sl=bank[6 + half][0:CAP, :])
                    ins.then_inc(S["yy_full"], 1)

        def bmid(v, n):
            return v.unsqueeze(1).to_broadcast([v.shape[0], n, v.shape[1]])

        def blast(v, n):
            return v.unsqueeze(len(v.shape)).to_broadcast(list(v.shape) + [n])

        @block.vector
        def _(ve):
            done = {n: 0 for n in S}

            def tell(ins, name):
                ins.then_inc(S[name], 1)
                done[name] += 1
                return done[name]

            def own(name):
                ve.wait_ge(S[name], done[name])

            def seq(ins):
                tell(ins, "vseq")
                own("vseq")

            def empty(g):
                dst, f = dest[g]
                ve.wait_ge(S["dense_full"], g + 1)
                if f == 1.0:
                    ins = ve.tensor_copy(dst, src_of(g))
                else:
                    ins = ve.tensor_scalar(dst, src_of(g), f, None, ALU.mult)
                tell(ins, "dve_free")

            def empties(g0, n):
                for g in range(g0, g0 + n):
                    if owners[g] == "V":
                        empty(g)

            def norm_var(n):
                ve.wait_ge(S["nsum"], n + 1)
                tell(ve.tensor_scalar(rs, bank[6][:, :], 1.0 / D, EPS, ALU.mult, ALU.add), "nvar")

            def norm(n, weight, shift, dst):
                norm_var(n)
                ve.wait_ge(S["nroot"], n + 1)
                seq(ve.reciprocal(rs, rs))
                for k in range(KD):
                    if shift is None:
                        ins = ve.scalar_tensor_tensor(dst[:, k, :], xT[:, k, :], weight[:, k:k + 1], rs, ALU.mult, ALU.mult)
                    else:
                        seq(ve.tensor_tensor(dst[:, k, :], xT[:, k, :], rs, ALU.mult))
                        ins = ve.tensor_scalar(dst[:, k, :], dst[:, k, :], weight[:, k:k + 1], shift[:, k:k + 1],
                                               ALU.mult, ALU.add)
                tell(ins, "h_rdy")
                own("h_rdy")

            def log1p_exp(x, n):
                e, z, z2, p = (v[:, 0:n] for v in lp)
                tell(ve.scalar_tensor_tensor(e, x, -1.0, x, ALU.mult, ALU.max), "lx_rdy")
                ve.wait_ge(S["lx_exp"], done["lx_rdy"])
                seq(ve.tensor_scalar(z2, e, 2.0, None, ALU.add))
                seq(ve.reciprocal(z2, z2))
                seq(ve.tensor_tensor(z, e, z2, ALU.mult))
                seq(ve.tensor_tensor(z2, z, z, ALU.mult))
                seq(ve.tensor_scalar(p, z2, 1.0 / 17, None, ALU.mult))
                for m in (15, 13, 11, 9, 7, 5, 3):
                    seq(ve.scalar_tensor_tensor(p, p, 1.0 / m, z2, ALU.add, ALU.mult))
                seq(ve.scalar_tensor_tensor(p, p, 1.0, z, ALU.add, ALU.mult))
                seq(ve.tensor_scalar(p, p, 2.0, None, ALU.mult))
                return p

            def conv(src, dst, f, taps, name, n_f):
                seq(ve.tensor_scalar(dst[:, f, :], src[:, f, 0:T], col(name, f), None, ALU.mult))
                for j in range(1, taps):
                    ins = ve.scalar_tensor_tensor(dst[:, f, :], src[:, f, j:j + T], col(name, j * n_f + f), dst[:, f, :],
                                                  ALU.mult, ALU.add)
                    if j < taps - 1:
                        seq(ins)
                tell(ins, "conv_rdy")

            def empties_conv(g0, *args, after={}):
                for f in range(KD):
                    if owners[g0 + f] == "V":
                        empty(g0 + f)
                        own("dve_free")
                    else:
                        ve.wait_ge(*emptied(g0 + f))
                    conv(args[0], args[1], f, *args[2:])
                    if f in after:
                        after[f]()

            def attention(items, first, bias, P_, out_of, sink):
                def masked_max(i):
                    h, q, k0, n = items[i]
                    x = first + i
                    ve.wait_ge(S["s_full"], x + 1)
                    if x >= 3:
                        ve.wait_ge(S["pt_full"], x - 2)
                    sc, p = bank[4 + x % 2], P_[:, x % 3, :]
                    tell(bias(h, q, n, sc, p), "s_bias")
                    own("s_bias")
                    m = nmax[:, x % 3:x % 3 + 1]
                    if sink:
                        seq(ve.tensor_reduce(m, p[:, 0:n * P], AX, ALU.max))
                        tell(ve.tensor_scalar(m, m, row("sink", h, 1), -1.0, ALU.max, ALU.mult), "p_max")
                    else:
                        tell(ve.tensor_reduce(m, p[:, 0:n * P], AX, ALU.max, negate=True), "p_max")

                def normalize(i):
                    h, q, k0, n = items[i]
                    x = first + i
                    b = slice(x % 3, x % 3 + 1)
                    ve.wait_ge(S["p_exp"], x + 1)
                    if sink:
                        seq(ve.tensor_tensor(asum[:, b], asum[:, b], esk[:, b], ALU.add))
                    seq(ve.reciprocal(arec[:, b], asum[:, b]))
                    tell(ve.tensor_scalar(P_[:, x % 3, 0:n * P], P_[:, x % 3, 0:n * P], arec[:, b], None, ALU.mult), "p_norm")

                def take(j):
                    ve.wait_ge(S["o_full"], first + 8 * j + 8)
                    tell(ve.tensor_copy(out_of(j), bank[2 + (first // 8 + j) % 2][:, :]), "o_ev")

                masked_max(0)
                for i in range(NI):
                    if i + 1 < NI:
                        masked_max(i + 1)
                    normalize(i)
                    if i % 8 == 3 and i > 8:
                        take(i // 8 - 1)
                take(NI // 8 - 1)

            ve.wait_ge(S["consts"], 1)
            tell(ve.tensor_scalar(mnf[:, :], tri[:, :], -NEG, NEG, ALU.mult, ALU.add), "negs")
            tell(ve.tensor_scalar(mnb[:, :], trib[:, :], -NEG, NEG, ALU.mult, ALU.add), "negs")
            seq(ve.memset(e2[0:8, :], NEG))
            ve.wait_ge(S["ld_tab"], 16)
            for m0, m1, b in bucket_runs():
                ins = ve.tensor_copy(e2[0:8, m0:m1], tabT[:, b:b + 1].to_broadcast([8, m1 - m0]))
            tell(ins, "e2_rdy")

            ve.wait_ge(S["ld_cols"], 16)
            ve.wait_ge(S["cact_rdy"], 1)
            for j in range(4):
                ve.wait_ge(*arrived[("ada", j)])
                w = slot(j, KD, 512)
                seq(ve.tensor_scalar(ada1[:, j, :], w[:, 0, :], cact[:, 0:1], None, ALU.mult))
                for k in range(1, KD):
                    ins = ve.scalar_tensor_tensor(ada1[:, j, :], w[:, k, :], cact[:, k:k + 1], ada1[:, j, :],
                                                  ALU.mult, ALU.add)
                    if k < KD - 1:
                        seq(ins)
                tell(ins, "ada_used1")
                if j == 1:
                    ve.wait_ge(S["ld_x"], 16)
                    norm_var(0)
                if j == 2:
                    ve.wait_ge(S["nroot"], 1)
                    seq(ve.reciprocal(rs, rs))
                    for k in range(KD):
                        ins = ve.tensor_tensor(hT[:, k, :], xT[:, k, :], rs, ALU.mult)
                    seq(ins)
            ve.wait_ge(S["ada_full"], 4)
            tell(ve.tensor_tensor(mod[:, 0:16], bank[7][:, 0:16], col("b_ada", 0, 16), ALU.add), "mod_rdy")
            own("mod_rdy")
            seq(ve.scalar_tensor_tensor(aff[:, :], mod[:, 8:16], 1.0, col("norm_mix", 0, 8), ALU.add, ALU.mult))
            for k in range(KD):
                ins = ve.tensor_scalar(hT[:, k, :], hT[:, k, :], aff[:, k:k + 1], mod[:, k:k + 1], ALU.mult, ALU.add)
            tell(ins, "h_rdy")
            own("h_rdy")
            empties(G_Q, 12)
            empties_conv(G_XBC, xraw, xbcT, 4, "ssd_cw", 8)
            empties(G_Z, 4)
            ve.wait_ge(S["dt_full"], 1)
            ve.wait_ge(S["ld_rows"], 16)
            tell(ve.tensor_tensor(dtr, bank[5][:, 0:32].rearrange("p (t e) -> p t e", e=8), bmid(row("dt_bias"), NT), ALU.add),
                 "dt_raw")
            ve.wait_ge(S["t1_masked"], 1)
            own("conv_rdy")

            def bias1(h, q, n, sc, p):
                if q == 0:
                    return ve.tensor_tensor(p[:, 0:P], sc[:, 0:P], T1[:, h, P:2 * P], ALU.add)
                far = (q - 1) * P
                if far:
                    ve.tensor_scalar(p[:, 0:far], sc[:, 0:far], row("rel_far", h, 1), None, ALU.add)
                return ve.tensor_tensor(p[:, far:far + 2 * P], sc[:, far:far + 2 * P], T1[:, h, :], ALU.add)

            attention(ATT1, 0, bias1, pr, lambda j: yT[:, 4 + j, :], False)
            ve.wait_ge(S["ada_full"], 12)
            tell(ve.tensor_tensor(mod[:, 16:48], bank[1][:, 16:48], col("b_ada", 16, 32), ALU.add), "mod_rdy")
            x = dtr.rearrange("p t e -> p (t e)")
            own("dt_raw")
            l = log1p_exp(x, 32)
            seq(ve.scalar_tensor_tensor(dtv.rearrange("p t e -> p (t e)"), x, 0.0, l, ALU.max, ALU.add))
            ve.wait_ge(S["alog_exp"], 1)
            tell(ve.scalar_tensor_tensor(adt, dtv, -1.0, bmid(expa, NT), ALU.mult, ALU.mult), "dta")
            ve.wait_ge(S["a_full"], 1)
            flat = lambda v: v.rearrange("p t e -> p (t e)")
            seq(ve.tensor_copy(flat(acs), bank[0][:, 0:32]))
            seq(ve.tensor_copy(flat(tot), bank[0][:, 32:64]))
            seq(ve.tensor_scalar(flat(nacs), flat(acs), -1.0, None, ALU.mult))
            tell(ve.tensor_tensor(flat(dte), flat(tot), flat(acs), ALU.subtract), "a_rdy")
            for t in range(NT):
                ve.wait_ge(S["tk_full"], 2 * t + 1)
                tell(ve.tensor_copy(xstok[:, t, :], bank[1][:, :]), "tk_ev")
                ve.wait_ge(S["tk_full"], 2 * t + 2)
                tell(ve.tensor_copy(Btok[:, t, :], bank[2][:, 0:256]), "tk_ev")
            ve.wait_ge(S["a_exp"], 1)
            ve.wait_ge(S["z_rdy"], 1)
            own("tk_ev")

            def heads(v):
                return v.rearrange("p (e d) -> p e d", d=HD)

            def inputs(c):
                if c >= 1:
                    ve.wait_ge(S["r_full"], c)
                tell(ve.tensor_tensor(diag, bmid(ident[:, :], 8), blast(acs[:, c, :], P), ALU.mult), "dg_rdy")
                ve.wait_ge(S["cb_full"], c + 1)
                seq(ve.tensor_tensor(CBm, bank[3][:, 0:256].rearrange("p (g l) -> p g l", l=P), bmid(tri[:, :], 2), ALU.mult))
                seq(ve.tensor_tensor(heads(xdt2[c % 2]), heads(xstok[:, c, :]), blast(dtv[:, c, :], HD), ALU.mult))
                tell(ve.tensor_tensor(heads(xde2[c % 2]), heads(xdt2[c % 2]), blast(dte[:, c, :], HD), ALU.mult), "xd_rdy")

            def exponents(c):
                ve.wait_ge(S["r_full"], c + 1)
                for e in range(HEADS):
                    ins = ve.tensor_scalar(Mt2[c % 2][:, e, :], bank[4 + e // 4][:, (e % 4) * P:(e % 4 + 1) * P],
                                           nacs[:, c, e:e + 1], 0.0, ALU.add, ALU.min)
                tell(ins, "seg_rdy")

            def y_turned(c):
                ve.wait_ge(S["yt_full"], c + 1)
                tell(ve.tensor_tensor(yT[:, 0:4, c * P:(c + 1) * P], bank[1][:, :].rearrange("p (f t) -> p f t", t=P),
                                      blast(col("ssd_norm", 0, 4), P), ALU.mult), "yt_ev")

            inputs(0)
            exponents(0)
            for c in range(NT):
                Mt = Mt2[c % 2]
                ve.wait_ge(S["seg_exp"], c + 1)
                ve.tensor_tensor(Mt[:, 0:4, :], Mt[:, 0:4, :], bmid(CBm[:, 0, :], 4), ALU.mult)
                tell(ve.tensor_tensor(Mt[:, 4:8, :], Mt[:, 4:8, :], bmid(CBm[:, 1, :], 4), ALU.mult), "mt_rdy")
                own("mt_rdy")
                if c + 1 < NT:
                    inputs(c + 1)
                if c >= 1:
                    y_turned(c - 1)
                if c + 1 < NT:
                    exponents(c + 1)
                seq(ve.tensor_tensor(heads(y2), heads(xstok[:, c, :]), blast(row("d_skip"), HD), ALU.mult))
                ve.wait_ge(S["y_full"], c + 1)
                if c == 0:
                    tell(ve.tensor_copy(H, bank[7][:, :]), "h_upd")
                else:
                    seq(ve.tensor_tensor(heads(H), heads(H), blast(cd[:, c, :], HD), ALU.mult))
                    tell(ve.tensor_tensor(H, H, bank[7][:, :], ALU.add), "h_upd")
                    own("h_upd")
                seq(ve.tensor_tensor(y2, y2, bank[0][:, :], ALU.add))
                if c >= 1:
                    seq(ve.tensor_tensor(heads(y), heads(bank[6][:, :]), blast(ea[:, c, :], HD), ALU.mult))
                    seq(ve.tensor_tensor(y2, y, y2, ALU.add))
                own("h_upd")
                tell(ve.tensor_tensor(y, y2, ztok[:, c, :], ALU.mult), "y_rdy")
                ve.wait_ge(S["y_sq"], c + 1)
                tell(ve.tensor_scalar(rsq[:, 0:1], ssq[:, 0:1], 1.0 / 512, EPS, ALU.mult, ALU.add), "row_var")
                ve.wait_ge(S["row_root"], c + 1)
                seq(ve.reciprocal(rsq[:, 0:1], rsq[:, 0:1]))
                tell(ve.tensor_scalar(y, y, rsq[:, 0:1], None, ALU.mult), "y_nrm")
            y_turned(NT - 1)
            own("mod_rdy")
            for m in range(KD):
                ve.wait_ge(S["dense_full"], G_WO + m + 1)
                tell(ve.scalar_tensor_tensor(xT[:, m, :], bank[(G_WO + m) % 4][:, :], mod[:, 16 + m:17 + m],
                                             xT[:, m, :], ALU.mult, ALU.add), "dve_free")
            own("dve_free")
            seq(ve.scalar_tensor_tensor(aff[:, :], mod[:, 32:40], 1.0, col("norm_ffn", 0, 8), ALU.add, ALU.mult))
            norm(1, aff, mod[:, 24:32], hT)

            def scal(name, i):
                return cols[:, ds(i + COLS[name][0], 1)] if not isinstance(i, int) else col(name, i)

            def slab(n, j):
                for c in range(4):
                    bk, ac = bank[4 * j + c], acc[:, j, c, :]
                    tile = n * 2 + (c // 2 + (FT if c % 2 else 0))
                    ve.wait_ge(S["up_first"], n * 4 + (c + 1))
                    ve.scalar_tensor_tensor(ac[:, 1:T], bk[:, 0:T - 1], scal("ffn_cw", tile + 2 * FT), ac[:, 1:T],
                                            ALU.mult, ALU.add).then_inc(S["up_seq"], 1)
                    ve.wait_ge(S["up_seq"], n * 4 + (c + 1))
                    ve.scalar_tensor_tensor(ac[:, 2:T], bk[:, 0:T - 2], scal("ffn_cw", tile), ac[:, 2:T],
                                            ALU.mult, ALU.add).then_inc(S["up_free"], 1)
                    if c % 2:
                        ve.wait_ge(S["up_free"], n * 4 + (c + 1))
                        ve.wait_ge(S["up_silu"], n * 2 + (c // 2 + 1))
                        at = n * (2 * T) + (c // 2) * T
                        dst = actT[:, n * 2 + c // 2, :] if isinstance(n, int) else \
                            actT.rearrange("p f t -> p (f t)")[:, ds(at, T)]
                        ve.tensor_tensor(dst, acc[:, j, c - 1, :], ac, ALU.mult).then_inc(S["up_g"], 1)

            slab(0, 0)
            slab(1, 1)
            with ve.Fori(1, 5) as i:
                slab(i * 2, 0)
                slab(i * 2 + 1, 1)
            slab(10, 0)
            for n in range(KD):
                ve.wait_ge(S["dn_full"], n + 1)
                tell(ve.scalar_tensor_tensor(xT[:, n, :], bank[n % 2][:, :], mod[:, 40 + n:41 + n], xT[:, n, :],
                                             ALU.mult, ALU.add), "dn_free")
            own("dn_free")
            norm(2, col("final_norm", 0, 8), None, xT)
            norm(3, col("norm1", 0, 8), None, hT)
            empties(G_QA, G_QM - G_QA)
            ve.wait_ge(S["pads"], 1)
            seq(ve.tensor_scalar(gk[:, 0:1], col("q_gain"), HD ** -0.5, None, ALU.mult))
            seq(ve.tensor_copy(gk[:, 1:2], col("k_gain")))

            def q_variances(lo, hi):
                for i in range(lo, hi):
                    ve.wait_ge(S["qsum"], i + 1)
                    tell(ve.tensor_scalar(sq2[:, i, :], bank[QBANK[i]][:, :], 1.0 / HD, EPS, ALU.mult, ALU.add), "qvar")

            def q_normed(i):
                ve.wait_ge(S["qroot"], i + 1)
                seq(ve.reciprocal(sq2[:, i, :], sq2[:, i, :]))
                gain = gk[:, 1:2] if i == 4 else gk[:, 0:1]
                tell(ve.scalar_tensor_tensor(qaT[:, i, :], qaT[:, i, :], gain, sq2[:, i, :], ALU.mult, ALU.mult), "qn_rdy")

            empties_conv(G_QM, mraw, mconv, 5, "ml_cw", 8, after={4: lambda: q_variances(0, 3)})
            q_variances(3, 5)
            own("dve_free")
            q_normed(0)
            q_normed(1)
            for t in range(NT):
                if owners[G_VM + t] == "V":
                    empty(G_VM + t)
                    if t < NT - 1:
                        q_normed(2)
                        q_normed(3)
            q_normed(4)
            ve.wait_ge(S["gt_full"], 1)
            tell(ve.tensor_tensor(gt, bank[5][:, 0:64].rearrange("p (t e) -> p t e", e=16), bmid(row("gate_b"), NT), ALU.add),
                 "gt_rdy")
            own("dve_free")
            own("conv_rdy")
            ve.wait_ge(S["ld_T2"], 16)

            def bias2(h, q, n, sc, p):
                j0 = P if q == 0 else 0
                return ve.tensor_tensor(p[:, 0:n * P], sc[:, 0:n * P], T2[:, h, j0:j0 + n * P], ALU.add)

            attention(ATT2, NI, bias2, pr2, lambda j: yaT[:, j, :], True)
            flat = lambda v: v.rearrange("p t e -> p (t e)")
            g5 = gt.rearrange("p t (d k h) -> p t d k h", d=2, k=2)
            fx, ix = lp[3][:, 32:64], lp[2][:, 32:64]
            own("gt_rdy")
            for t in range(NT):
                ve.tensor_copy(fx[:, t * 8:t * 8 + 8].rearrange("p (d h) -> p d h", d=2), g5[:, t, :, 1, :])
                ins = ve.tensor_copy(ix[:, t * 8:t * 8 + 8].rearrange("p (d h) -> p d h", d=2), g5[:, t, :, 0, :])
            seq(ins)
            l = log1p_exp(fx, 32)
            tell(ve.scalar_tensor_tensor(flat(lf), fx, 0.0, l, ALU.min, ALU.subtract), "dta")
            ve.wait_ge(S["f_full"], 1)
            seq(ve.tensor_copy(flat(Ft), bank[0][:, 0:32]))
            tell(ve.tensor_tensor(flat(vt), ix, flat(Ft), ALU.subtract), "vt_rdy")
            ve.wait_ge(S["vr_full"], 1)
            for d in range(2):
                seq(ve.tensor_copy(rowv[0:4, d, :], bank[1 + d][0:4, :]))
                r = rowv[0:4, d, :] if d == 0 else rowv[0:4, d, ::-1]
                tell(ve.tensor_tensor_scan(r, r, r, 0.0, ALU.max, ALU.max), "scan_rdy")
            ve.wait_ge(S["mk_full"], 1)
            seq(ve.tensor_scalar(flat(nM), bank[3][:, 0:32], -1.0, None, ALU.mult))
            tell(ve.tensor_tensor(flat(em), flat(Ft), flat(nM), ALU.subtract), "m_rdy")
            ve.wait_ge(S["m_exp"], 1)

            def diagonals(x):
                ci = 4 * (x % 2) + x // 2
                if x >= 1:
                    ve.wait_ge(S["u_full"], x)
                tell(ve.tensor_tensor(dgm, bmid(ident[:, :], NT),
                                      nM[:, :, ci:ci + 1].to_broadcast([P, NT, P]), ALU.mult), "dgm_rdy")

            def masked(x):
                d, ci = x % 2, 4 * (x % 2) + x // 2
                ve.wait_ge(S["u_full"], x + 1)
                if x >= 2:
                    ve.wait_ge(S["n_full"], x - 1)
                for j in range(NT):
                    b = slice(j * P, (j + 1) * P)
                    tell(ve.scalar_tensor_tensor(Wm2[d][:, j, b], bank[d][:, b], vt[:, j, ci:ci + 1],
                                                 (mnf if d == 0 else mnb)[:, :], ALU.add, ALU.add), "wd_rdy")

            diagonals(0)
            masked(0)
            for x in range(2 * MH):
                h, d = x // 2, x % 2
                ci = 4 * d + h
                if x + 1 < 2 * MH:
                    diagonals(x + 1)
                for j in range(NT):
                    r = slice(j * P, T) if d == 0 else slice(0, (j + 1) * P)
                    ve.wait_ge(S["w_exp"], 4 * x + j + 1)
                    ve.wait_ge(S["ms_full"], 4 * h + j + 1)
                    tell(ve.scalar_tensor_tensor(Wm2[d][:, j, r], bank[4 + j][:, r], P ** -0.5, Wm2[d][:, j, r],
                                                 ALU.mult, ALU.mult), "w_rdy")
                if x + 1 < 2 * MH:
                    masked(x + 1)
                ve.wait_ge(S["n_full"], x + 1)
                if d == 0 and h >= 1:
                    ve.wait_ge(S["hmt_full"], 2 * h)
                for b in range(2):
                    both = bank[2 + b][:, 0:2 * (P + 1)].rearrange("p (t e) -> p t e", e=P + 1)
                    ins = ve.tensor_copy(dn[:, 2 * b:2 * b + 2], both[:, :, P])
                seq(ins)
                seq(ve.scalar_tensor_tensor(dn, dn, -1.0, dn, ALU.mult, ALU.max))
                seq(ve.tensor_tensor(dn, dn, em[:, :, ci], ALU.max))
                seq(ve.reciprocal(dn, dn))
                for t in range(NT):
                    num = bank[2 + t // 2][:, (t % 2) * (P + 1):(t % 2) * (P + 1) + P]
                    if d == 0:
                        ins = ve.tensor_scalar(hm[:, t, :], num, dn[:, t:t + 1], None, ALU.mult)
                    else:
                        ins = ve.scalar_tensor_tensor(hm[:, t, :], num, dn[:, t:t + 1], hm[:, t, :], ALU.mult, ALU.add)
                tell(ins, "hm_rdy")
                own("hm_rdy")
                if d == 1:
                    ve.wait_ge(S["hm_sq"], 4 * h + 4)
                    tell(ve.tensor_scalar(rsq, ssq, 1.0 / P, EPS, ALU.mult, ALU.add), "row_var")
                    ve.wait_ge(S["row_root"], NT + h + 1)
                    seq(ve.reciprocal(rsq, rsq))
                    for t in range(NT):
                        ins = ve.scalar_tensor_tensor(hm[:, t, :], hm[:, t, :], rsq[:, t:t + 1],
                                                      row("out_gain", h * P, P), ALU.mult, ALU.mult)
                    seq(ins)
                    tell(ve.tensor_tensor(hm, hm, omtok[:, :, h * P:(h + 1) * P], ALU.mult), "hm_fin")
            for m in range(KD):
                ve.wait_ge(S["mg_sig"], 2 * m + 2)
                b = m % 2
                ve.wait_ge(S["mg_full"], 4 * m + 4)
                ve.tensor_tensor(mg_s[:, b, 2, :], mg_s[:, b, 0, :], bank[(4 * m + 2) % 8][:, :], ALU.mult)
                tell(ve.tensor_tensor(mg_s[:, b, 3, :], mg_s[:, b, 1, :], bank[(4 * m + 3) % 8][:, :], ALU.mult), "mg_free")
                own("mg_free")
                tell(ve.tensor_tensor(uT[:, m, :], mg_s[:, b, 2, :], mg_s[:, b, 3, :], ALU.add), "u_rdy")
            for m in range(KD):
                ve.wait_ge(S["dense_full"], G_WO2 + m + 1)
                tell(ve.tensor_tensor(xT[:, m, :], bank[(G_WO2 + m) % 4][:, :], xT[:, m, :], ALU.add), "dve_free")
            own("dve_free")
            for x in range(2 * NT):
                ve.wait_ge(S["xk_full"], x + 1)
                tell(ve.tensor_copy(xtok[:, x // 2, (x % 2) * 512:(x % 2 + 1) * 512], bank[x % 2][:, :]), "xk_ev")
            for k in range(KD):
                tell(ve.tensor_scalar(hT[:, k, :], xT[:, k, :], col("norm2", k), None, ALU.mult), "xg_rdy")
            ve.wait_ge(S["xk_sq"], NT)
            tell(ve.tensor_scalar(rsq, ssq, 1.0 / D, EPS, ALU.mult, ALU.add), "row_var")
            ve.wait_ge(S["row_root"], NT + MH + 1)
            seq(ve.reciprocal(rsq, rsq))
            for t in range(NT):
                tell(ve.tensor_scalar(htok[:, t, :], xtok[:, t, :], rsq[:, t:t + 1], None, ALU.mult), "htok_rdy")
            ve.wait_ge(S["lg_full"], 1)
            for t in range(NT):
                ins = ve.scalar_tensor_tensor(R["lg"][:, t, :], bank[4][:, t * 36:(t + 1) * 36], rsq[:, t:t + 1],
                                              row("b_router"), ALU.mult, ALU.add)
            seq(ins)
            seq(ve.tensor_copy(R["io"], io_i))
            seq(ve.tensor_scalar(R["r4"], R["io"][:, 0:4], -1.0, 4.0, ALU.mult, ALU.add))
            seq(ve.tensor_reduce(R["gm"], R["lg"][:, :, 0:4], AX, ALU.max))
            tell(ve.tensor_tensor(R["gs"], R["lg"][:, :, 0:4], blast(R["gm"], 4), ALU.subtract), "lg_rdy")
            own("lg_rdy")
            seq(ve.tensor_scalar(R["g1"], R["gs"], 0.0, None, ALU.is_equal))
            seq(ve.tensor_tensor(R["g1"], R["g1"], bmid(R["r4"], NT), ALU.mult))
            seq(ve.tensor_reduce(R["gx"], R["g1"], AX, ALU.max))
            seq(ve.tensor_tensor(R["g1"], R["g1"], blast(R["gx"], 4), ALU.is_equal))
            seq(ve.tensor_scalar(R["g1"], R["g1"], -NEG, NEG, ALU.mult, ALU.add))
            for t in range(NT):
                ins = ve.tensor_tensor(R["em"][:, t, :].rearrange("p (g e) -> p g e", e=8),
                                       R["lg"][:, t, 4:36].rearrange("p (g e) -> p g e", e=8),
                                       blast(R["g1"][:, t, :], 8), ALU.add)
            seq(ins)
            for t in range(NT):
                seq(ve.max(R["top"][:, t, :], R["em"][:, t, :]))
                seq(ve.max_index(R["ix"][:, t, :].bitcast(U32), R["top"][:, t, :], R["em"][:, t, :]))
            seq(ve.tensor_copy(R["ix"].rearrange("p t e -> p (t e)"), R["ix"].rearrange("p t e -> p (t e)").bitcast(U32)))
            tell(ve.tensor_tensor(R["d"], R["top"][:, :, 1], R["top"][:, :, 0], ALU.subtract), "top_rdy")
            io4 = bmid(R["io"], NT)
            seq(ve.tensor_tensor(R["oh1"], io4, R["ix"][:, :, 0:1].to_broadcast([P, NT, E]), ALU.is_equal))
            seq(ve.tensor_tensor(R["oh2"], io4, R["ix"][:, :, 1:2].to_broadcast([P, NT, E]), ALU.is_equal))
            tell(ve.tensor_tensor(R["ohs"], R["oh1"], R["oh2"], ALU.add), "oh_rdy")
            ve.wait_ge(S["lg_exp"], 2)
            seq(ve.tensor_reduce(R["pg"], R["ge"], AX, ALU.add))
            seq(ve.tensor_scalar(R["w1"], R["ed"], 1.0, None, ALU.add))
            seq(ve.tensor_tensor(R["w1"], R["w1"], R["pg"], ALU.mult))
            seq(ve.reciprocal(wt[:, 0, :], R["w1"]))
            seq(ve.tensor_tensor(wt[:, 1, :], wt[:, 0, :], R["ed"], ALU.mult))
            ve.wait_ge(S["rank_full"], 1)
            seq(ve.tensor_copy(R["rk"].rearrange("p t e -> p (t e)"), bank[5][:, 0:NT * E]))
            seq(ve.tensor_copy(R["ct"], bank[5][:, NT * E:(NT + 1) * E]))
            seq(ve.tensor_scalar(R["nb"], R["ct"], float(CAP), None, ALU.is_gt))
            for b in range(2, T // CAP):
                seq(ve.tensor_scalar(R["t1"], R["ct"], float(CAP * b), None, ALU.is_gt))
                seq(ve.tensor_tensor(R["nb"], R["nb"], R["t1"], ALU.add))
            seq(ve.memset(R["t1"], 0.0))
            seq(ve.tensor_tensor_scan(R["cin"], R["nb"], R["t1"], 0.0, ALU.add, ALU.add))
            seq(ve.tensor_tensor(R["adj"], R["cin"], R["nb"], ALU.subtract))
            seq(ve.tensor_tensor(R["adj"], R["adj"], R["io"], ALU.subtract))
            seq(ve.tensor_scalar(R["adj"], R["adj"], float(CAP), float(CAP * (E - 1)), ALU.mult, ALU.add))
            seq(ve.tensor_scalar(R["t2"], R["rk"], float(CAP), None, ALU.is_ge))
            seq(ve.tensor_tensor(R["t2"], R["t2"], bmid(R["adj"], NT), ALU.mult))
            seq(ve.tensor_tensor(R["fs"], R["rk"], R["t2"], ALU.add))
            seq(ve.tensor_scalar(R["t1"], R["io"], float(CAP), None, ALU.mult))
            seq(ve.tensor_tensor(R["fs"], R["fs"], bmid(R["t1"], NT), ALU.add))
            for b, oh in enumerate(("oh1", "oh2")):
                seq(ve.tensor_tensor(R["t2"], R[oh], R["fs"], ALU.mult))
                seq(ve.tensor_reduce(R["sl"][:, b, :], R["t2"], AX, ALU.add))
            tell(ve.tensor_copy(slot_i, R["sl"].rearrange("p b t -> p (b t)")), "slots_rdy")
            for i in range(OVB):
                ins = ve.tensor_scalar(R["be"][0:1, i, :], R["cin"][0:1, :], float(i), None, ALU.is_le)
            seq(ins)
            seq(ve.tensor_reduce(R["bx"][0:1, 0:OVB], R["be"][0:1, 0:OVB, :], AX, ALU.add))
            seq(ve.tensor_scalar(R["bx"][0:1, 0:OVB], R["bx"][0:1, 0:OVB], float(E - 1), None, ALU.min))
            seq(ve.tensor_copy(smi[0:1, 41:41 + OVB], R["bx"][0:1, 0:OVB]))
            tell(ve.tensor_copy(smi[0:1, 40:41], R["cin"][0:1, E - 1:E]), "tab_rdy")
            own("tab_rdy")
            n2 = col("norm2", 0, 8)

            def rows_turned(p):
                for x in range(2):
                    ve.wait_ge(S["xt_full"], p * 2 + (x + 1))
                    ve.tensor_tensor(xsT[:, 4 * x:4 * x + 4, :], bank[x][:, :].rearrange("p (f t) -> p f t", t=P),
                                     blast(n2[:, 4 * x:4 * x + 4], P), ALU.mult).then_inc(S["xt_ev"], 1)

            def pair(p, first, last):
                for b in range(2):
                    ro = slice(b * CAP, (b + 1) * CAP)
                    ve.wait_ge(S["sil_rdy"], p * 2 + (b + 1))
                    ve.wait_ge(S["uu_full"], p * 2 + (b + 1))
                    if not first and b == 0:
                        ve.wait_ge(S["ht_full"], p)
                    ve.tensor_tensor(hE[ro, :], sg[ro, :], bank[3][ro, :], ALU.mult).then_inc(S["he_rdy"], 1)
                if not last:
                    rows_turned(p + 1)

            rows_turned(0)
            pair(0, True, False)
            with ve.Fori(1, E // 2 - 1) as p:
                pair(p, False, False)
            pair(E // 2 - 1, False, True)
            n_more = ve.value_load(smi[0:1, 40:41], min_val=0, max_val=OVB)
            with ve.Fori(0, OVB) as i:
                with ve.If(n_more > i):
                    ve.wait_ge(S["xt_full"], i * 2 + (E + 2))
                    for x in range(2):
                        ins = ve.tensor_tensor(xsT[:, 4 * x:4 * x + 4, 0:CAP],
                                               bank[x][:, :].rearrange("p (f t) -> p f t", t=P)[:, :, 0:CAP],
                                               blast(n2[:, 4 * x:4 * x + 4], CAP), ALU.mult)
                    ins.then_inc(S["xt_ev"], 1)
                    ve.wait_ge(S["sil_rdy"], i + (E + 1))
                    ve.tensor_tensor(hE[0:CAP, :], sg[0:CAP, :], bank[3][0:CAP, :], ALU.mult).then_inc(S["he_rdy"], 1)
            for t in range(NT):
                ve.wait_ge(gath[t], 32)
                for b in range(2):
                    ins = ve.scalar_tensor_tensor(xtok[:, t, :], ws[b][:, t * D:(t + 1) * D], wt[:, b, t:t + 1],
                                                  xtok[:, t, :], ALU.mult, ALU.add)
                    if b == 0:
                        seq(ins)
                tell(ins, "comb")

        @block.scalar
        def _(ac):
            done = {n: 0 for n in S}

            def act(dst, src, f, name=None, **kw):
                ins = nc.scalar.activation(dst, src, f, **kw)
                if name:
                    ins.then_inc(S[name], 1)
                    done[name] += 1

            def own(name):
                ac.wait_ge(S[name], done[name])

            def empty(g, f=ACT.Copy):
                dst, fac = dest[g]
                ac.wait_ge(S["dense_full"], g + 1)
                act(dst, src_of(g), f, "act_free", scale=fac)

            def empties(g0, n):
                for g in range(g0, g0 + n):
                    if owners[g] == "A":
                        empty(g)

            def norm(n):
                act(hT[:, :, :], xT[:, :, :], ACT.Square, "nsq")
                ac.wait_ge(S["nvar"], n + 1)
                act(rs, rs, ACT.Sqrt, "nroot")

            def attention(items, first, P_, PT_, sink):
                def exps(i):
                    h, q, k0, n = items[i]
                    x = first + i
                    b = slice(x % 3, x % 3 + 1)
                    ac.wait_ge(S["p_max"], x + 1)
                    if sink:
                        act(esk[:, b], row("sink", h, 1), ACT.Exp, bias=nmax[:, b])
                    act(P_[:, x % 3, 0:n * P], P_[:, x % 3, 0:n * P], ACT.Exp, "p_exp", bias=nmax[:, b], accum_out=asum[:, b])

                def turned(i):
                    h, q, k0, n = items[i]
                    x = first + i
                    ac.wait_ge(S["pt_full"], x + 1)
                    if x >= 2:
                        ac.wait_ge(S["o_full"], x - 1)
                    act(PT_[:, x % 2, 0:n * P], bank[6 + x % 2][:, 0:n * P], ACT.Copy, "pt_ev")

                exps(0)
                for i in range(NI):
                    if i + 1 < NI:
                        exps(i + 1)
                    turned(i)

            ac.dma_start(rows[:, :], a["rows"].partition_broadcast(P)).then_inc(S["ld_rows"], 16)
            ac.dma_start(tabT[:, :], a["table_t"]).then_inc(S["ld_tab"], 16)
            rr = a["rel_rev"]
            ac.dma_start(e1[:, 127:383], rr[:, 0:256]).then_inc(S["ld_rel"], 16)
            ac.wait_ge(S["ld_cols"], 16)
            act(cact[:, :], col("c", 0, 8), ACT.Silu, "cact_rdy")
            ac.wait_ge(S["ld_x"], 16)
            norm(0)
            for dst, name, c0, n in ((w_dt, "w_in", DT0, 8), (w_gm, "w_in_2", GM0, 16), (w_rt, "w_router", 0, 36)):
                ac.dma_start(dst[:, :, :], kp(a[name], c0, n)).then_inc(S["ld_small"], 16)
            ac.wait_ge(S["ld_rel"], 16)
            act(e1[:, 0:127], e1[:, 127:128].to_broadcast([HEADS, 127]), ACT.Copy, "e1_rdy")
            own("e1_rdy")
            ac.dma_start(ext1, e1).then_inc(S["ext1_w"], 16)
            ac.wait_ge(S["ext1_w"], 16)
            ac.dma_start(skew1, ext1.unsqueeze(0).to_broadcast([P, HEADS, 383])).then_inc(S["ext1_w"], 16)
            ac.wait_ge(S["ld_rows"], 16)
            act(expa, row("a_log"), ACT.Exp, "alog_exp")
            ac.wait_ge(S["e2_rdy"], 1)
            ac.dma_start(ext2[:, :], e2[0:8, :]).then_inc(S["ext2_w"], 16)
            empties(G_Q, 4)
            ac.wait_ge(S["ext1_w"], 32)
            ac.dma_start(T1, bass.AP(tensor=skew1.tensor, offset=127, ap=[[HEADS * 383 - 1, P], [383, HEADS], [1, 256]]))\
              .then_inc(S["ld_T1"], 16)
            empties(G_Q + 4, 20)
            ac.wait_ge(*emptied(G_Z + 3))
            own("act_free")
            act(ztok, ztok, ACT.Silu, "z_rdy")
            for f in range(KD):
                ac.wait_ge(S["conv_rdy"], f + 1)
                act(xbcT[:, f, :], xbcT[:, f, :], ACT.Silu, "conv_silu", bias=col("ssd_cb", f))
            ac.wait_ge(S["ext2_w"], 16)
            ac.dma_start(skew2, ext2.unsqueeze(0).to_broadcast([P, HEADS, 512])).then_inc(S["ext2_w"], 16)
            attention(ATT1, 0, pr, prT, False)
            ac.wait_ge(S["lx_rdy"], 1)
            act(lp[0][:, 0:32], lp[0][:, 0:32], ACT.Exp, "lx_exp", scale=-1.0)
            ac.wait_ge(S["a_rdy"], 1)
            act(ea, acs, ACT.Exp)
            act(cd, tot, ACT.Exp)
            act(dte, dte, ACT.Exp, "a_exp")

            def decay(c):
                ac.wait_ge(S["seg_rdy"], c + 1)
                act(Mt2[c % 2], Mt2[c % 2], ACT.Exp, "seg_exp")

            decay(0)
            for c in range(NT):
                if c + 1 < NT:
                    decay(c + 1)
                ac.wait_ge(S["y_rdy"], c + 1)
                act(y2, y, ACT.Square, "y_sq", accum_out=ssq[:, 0:1])
                ac.wait_ge(S["row_var"], c + 1)
                act(rsq[:, 0:1], rsq[:, 0:1], ACT.Sqrt, "row_root")
            ac.wait_ge(*emptied(G_WO + 7))
            norm(1)

            def slab(n, j):
                for c in range(4):
                    tile = n * 2 + (c // 2 + (FT if c % 2 else 0))
                    w2 = col("ffn_cw", tile + 2 * (2 * FT)) if isinstance(n, int) else \
                        cols[:, ds(tile + (4 * FT + COLS["ffn_cw"][0]), 1)]
                    ac.wait_ge(S["up_full"], n * 4 + (c + 1))
                    if not isinstance(n, int) or n >= 2:
                        ac.wait_ge(S["up_g"], n * 2 + (c // 2 - 3))
                    nc.scalar.activation(acc[:, j, c, :], bank[4 * j + c][:, :], ACT.Copy, scale=w2).then_inc(S["up_first"], 1)
                    if c % 2:
                        ac.wait_ge(S["up_free"], n * 4 + c)
                        nc.scalar.activation(acc[:, j, c - 1, :], acc[:, j, c - 1, :], ACT.Silu).then_inc(S["up_silu"], 1)

            slab(0, 0)
            slab(1, 1)
            with ac.Fori(1, 5) as i:
                slab(i * 2, 0)
                slab(i * 2 + 1, 1)
            slab(10, 0)
            ac.wait_ge(S["dn_free"], 8)
            norm(2)
            ac.wait_ge(S["h_rdy"], 3)
            norm(3)
            ac.wait_ge(S["ext2_w"], 32)
            ac.wait_ge(S["dn_full"], 8)
            ac.dma_start(T2, bass.AP(tensor=skew2.tensor, offset=127, ap=[[HEADS * 512 - 1, P], [512, HEADS], [1, 384]]))\
              .then_inc(S["ld_T2"], 16)
            empties(G_QA, G_QM - G_QA)
            own("act_free")
            ac.wait_ge(*emptied(G_QA + 3))
            act(sq2, qaT, ACT.Square, "qsq")
            empties(G_QM, G_VM - G_QM)
            for i in range(5):
                ac.wait_ge(S["qvar"], i + 1)
                act(sq2[:, i, :], sq2[:, i, :], ACT.Sqrt, "qroot")
            empties(G_VM, G_OM - G_VM)
            for t in range(NT):
                ac.wait_ge(S["dense_full"], G_OM + t + 1)
                act(omtok[:, t, :], bank[(G_OM + t) % 4][:, :], ACT.Sigmoid, "act_free")
            for f in range(KD):
                ac.wait_ge(S["conv_rdy"], KD + f + 1)
                act(mconv[:, f, :], mconv[:, f, :], ACT.Silu, "conv_silu", bias=col("ml_cb", f))
            attention(ATT2, NI, pr2, pr2T, True)
            ac.wait_ge(S["lx_rdy"], 2)
            act(lp[0][:, 0:32], lp[0][:, 0:32], ACT.Exp, "lx_exp", scale=-1.0)
            ac.wait_ge(S["m_rdy"], 1)
            act(em, em, ACT.Exp, "m_exp", scale=-1.0)

            def exps(x):
                h, d = x // 2, x % 2
                ac.wait_ge(S["wd_rdy"], 4 * x + 4)
                for j in range(NT):
                    b = slice(j * P, (j + 1) * P)
                    r = slice((j + 1) * P, T) if d == 0 else slice(0, j * P)
                    if r.start < r.stop:
                        act(Wm2[d][:, j, r], bank[d][:, r], ACT.Exp, bias=vt[:, j, 4 * d + h:4 * d + h + 1])
                    act(Wm2[d][:, j, b], Wm2[d][:, j, b], ACT.Exp, "w_exp")

            def turned(h):
                for half in range(2):
                    ac.wait_ge(S["hmt_full"], 2 * h + half + 1)
                    for i in range(2):
                        t0 = (2 * half + i) * P
                        act(ymT[:, h, t0:t0 + P], bank[2 + i][:, 258:258 + P], ACT.Copy, "hmt_ev" if i else None)

            exps(0)
            for x in range(2 * MH):
                h, d = x // 2, x % 2
                if d == 0 and h >= 1:
                    turned(h - 1)
                if x + 1 < 2 * MH:
                    exps(x + 1)
                if d == 1:
                    ac.wait_ge(S["hm_rdy"], 2 * h + 2)
                    for t in range(NT):
                        act(junk[:, t, :], hm[:, t, :], ACT.Square, "hm_sq", accum_out=ssq[:, t:t + 1])
                    ac.wait_ge(S["row_var"], NT + h + 1)
                    act(rsq, rsq, ACT.Sqrt, "row_root")
            turned(MH - 1)
            for m in range(KD):
                for c in range(2):
                    ac.wait_ge(S["mg_full"], 4 * m + c + 1)
                    if m >= 2:
                        ac.wait_ge(S["mg_free"], m - 1)
                    act(mg_s[:, m % 2, c, :], bank[(4 * m + c) % 8][:, :], ACT.Sigmoid, "mg_sig",
                        bias=col("merge_b", 8 * c + m))
            for t in range(NT):
                ac.wait_ge(S["xk_ev"], 2 * t + 2)
                act(htok[:, t, :], xtok[:, t, :], ACT.Square, "xk_sq", accum_out=ssq[:, t:t + 1])
            ac.wait_ge(S["row_var"], NT + MH + 1)
            act(rsq, rsq, ACT.Sqrt, "row_root")
            ac.wait_ge(S["lg_rdy"], 1)
            act(R["ge"], R["gs"], ACT.Exp, "lg_exp")
            ac.wait_ge(S["top_rdy"], 1)
            act(R["ed"], R["d"], ACT.Exp, "lg_exp")
            ac.wait_ge(S["scattered"], 16 * 2 * NT)
            ac.dma_start(xsr, xs_d[0:P, :]).then_inc(S["ld_xs"], 16)
            ac.wait_ge(S["xt_full"], 2)
            ac.dma_start(xsr, xs_d[P:2 * P, :]).then_inc(S["ld_xs"], 16)

            def pair(p, first, more):
                for b in range(2):
                    ro = slice(b * CAP, (b + 1) * CAP)
                    ac.wait_ge(S["g_full"], p * 2 + (b + 1))
                    if not first:
                        ac.wait_ge(S["he_rdy"], p * 2 + (b - 1))
                    nc.scalar.activation(sg[ro, :], bank[2][ro, :], ACT.Silu).then_inc(S["sil_rdy"], 1)
                ac.wait_ge(S["ht_full"], p + 1)
                nc.scalar.activation(hET.rearrange("p k r -> p (k r)"), bank[4][:, :], ACT.Copy).then_inc(S["ht_ev"], 1)
                if more:
                    ac.wait_ge(S["xt_full"], p * 2 + 4)
                    ac.dma_start(xsr, xs_d[ds(p * P + 2 * P, P), :]).then_inc(S["ld_xs"], 16)
                ac.wait_ge(S["yy_full"], p * 2 + 2)
                if not first:
                    ac.wait_ge(S["y_st"], p * 16)
                nc.scalar.activation(ysb[:, 0:512], bank[6][:, :], ACT.Copy)
                nc.scalar.activation(ysb[:, 512:D], bank[7][:, :], ACT.Copy).then_inc(S["yy_ev"], 1)
                ac.wait_ge(S["yy_ev"], p + 1)
                ac.dma_start(ys_d[ds(p * P, P), :], ysb[:, :]).then_inc(S["y_st"], 16)

            pair(0, True, True)
            with ac.Fori(1, E // 2 - 2) as p:
                pair(p, False, True)
            pair(E // 2 - 2, False, False)
            pair(E // 2 - 1, False, False)
            ac.wait_ge(S["y_st"], 16 * (E // 2))
            ac.wait_ge(S["tab_rdy"], 1)
            n_more = ac.value_load(smi[0:1, 40:41], min_val=0, max_val=OVB)
            with ac.Fori(0, OVB) as i:
                with ac.If(n_more > i):
                    ac.dma_start(xsr[0:CAP, :], xs_d[ds(i * CAP + E * CAP, CAP), :]).then_inc(S["ov_xs"], 16)
                    ac.wait_ge(S["g_full"], i + (E + 1))
                    nc.scalar.activation(sg[0:CAP, :], bank[2][0:CAP, :], ACT.Silu).then_inc(S["sil_rdy"], 1)
                    ac.wait_ge(S["ht_full"], i + (E // 2 + 1))
                    nc.scalar.activation(hET.rearrange("p k r -> p (k r)"), bank[4][:, :], ACT.Copy)\
                        .then_inc(S["ht_ev"], 1)
                    ac.wait_ge(S["yy_full"], i + (E + 1))
                    nc.scalar.activation(ysb[0:CAP, 0:512], bank[6][0:CAP, :], ACT.Copy)
                    nc.scalar.activation(ysb[0:CAP, 512:D], bank[7][0:CAP, :], ACT.Copy).then_inc(S["yy_ev"], 1)
                    ac.wait_ge(S["yy_ev"], i + (E // 2 + 1))
                    ac.dma_start(ys_d[ds(i * CAP + E * CAP, CAP), :], ysb[0:CAP, :]).then_inc(S["ov_st"], 16)
                    ac.wait_ge(S["ov_st"], i * 16 + 16)
                    nc.scalar.activation(esk[:, 0:1], esk[:, 0:1], ACT.Copy)
            ac.sem_inc(S["stored"], 1)

        @block.gpsimd
        def _(po):
            def then(ins):
                ins.then_inc(S["pseq"], 1)
                steps[0] += 1
                po.wait_ge(S["pseq"], steps[0])

            steps = [0]
            po.memset(ident[:, :], 0.0)
            po.memset(ones[:, :], 1.0)
            po.memset(zero, 0.0)
            then(po.memset(block1[:, :], 0.0))
            then(po.memset(block1[0:HD, 0:HD], 1.0))
            then(po.memset(block1[HD:P, HD:P], 1.0))
            po.affine_select(out=ident[:, :], in_=ident[:, :], compare_op=ALU.not_equal, fill=1.0, base=0,
                             pattern=[[-1, P]], channel_multiplier=1)
            po.memset(xraw[:, :, 0:3], 0.0)
            po.iota(io_i, [[1, E]], base=0, channel_multiplier=0)
            for m, step, mul, op in ((tri, 1, -1, ALU.is_ge), (trib, -1, 1, ALU.is_ge), (tris, 1, -1, ALU.is_gt)):
                ins = po.affine_select(out=m[:, :], in_=ones[:, :], compare_op=op, fill=0.0, base=0, pattern=[[step, P]],
                                       channel_multiplier=mul)
            ins.then_inc(S["consts"], 1)
            po.wait_ge(S["ld_T1"], 16)
            po.memset(T1[0:HD, :, 3 * HD:4 * HD], NEG).then_inc(S["t1_masked"], 1)
            for j in range(4, 12):
                po.wait_ge(*arrived[("ada", j)])
                if j >= 10:
                    po.wait_ge(S["ada_full"], j - 5)
                w = slot(ADA_SLOT[j - 4], KD, 512)
                then(po.tensor_tensor(w, w, blast(cact[:, :], 512), ALU.mult))
                then(po.tensor_tensor(w[:, 0:4, :], w[:, 0:4, :], w[:, 4:8, :], ALU.add))
                then(po.tensor_tensor(w[:, 0:2, :], w[:, 0:2, :], w[:, 2:4, :], ALU.add))
                po.tensor_tensor(ada2[:, (j - 4) % 6, :], w[:, 0, :], w[:, 1, :], ALU.add).then_inc(S["ada_used2"], 1)
            po.wait_ge(S["consts"], 1)
            for i in range(4):
                n = ROWS // P // 4
                for j in range(n):
                    r0 = (i * n + j) * P
                    po.dma_start(xs_d[r0:r0 + P, :].rearrange("p (b d) -> p b d", d=256), bmid(zero, 4))\
                      .then_inc(S["zeroed"], 16)
            for r0 in range(E * CAP, ROWS, P):
                po.dma_start(ys_d[r0:r0 + P, :].rearrange("p (b d) -> p b d", d=256), bmid(zero, 4)).then_inc(S["zeroed"], 16)
            po.wait_ge(S["dn_full"], 8)
            po.memset(mraw[:, :, 0:2], 0.0)
            po.memset(vaug.rearrange("p t (h d) -> p (t h) d", d=P + 1)[:, :, P:P + 1], 1.0)
            po.memset(mraw[:, :, T + 2:T + 4], 0.0).then_inc(S["pads"], 1)
            po.wait_ge(S["qn_rdy"], 5)
            po.dma_start(kaS[0:HD, :], qaT[HD:P, 4, :]).then_inc(S["swapped"], 16)
            po.dma_start(kaS[HD:P, :], qaT[0:HD, 4, :]).then_inc(S["swapped"], 16)
            po.wait_ge(S["slots_rdy"], 1)
            po.wait_ge(S["zeroed"], 16 * (2 * ROWS // P - E * CAP // P))
            for t in range(NT):
                po.wait_ge(S["htok_rdy"], t + 1)
                for b in range(2):
                    po.indirect_dma_start(xs_d, bass.IndirectOffsetOnAxis(ap=slot_i[:, b * NT + t:b * NT + t + 1], axis=0),
                                          htok[:, t, :], None).then_inc(S["scattered"], 16)
            po.wait_ge(S["stored"], 1)
            for t in range(NT):
                for b in range(2):
                    po.indirect_dma_start(ws[b][:, t * D:(t + 1) * D], None, ys_d,
                                          bass.IndirectOffsetOnAxis(ap=slot_i[:, b * NT + t:b * NT + t + 1], axis=0))\
                      .then_inc(gath[t], 16)
            for t in range(NT):
                po.wait_ge(gath[t], 32)

    return nc


def columns(v, tiles):
    return np.asarray(v).reshape(-1, P).T


def kernel(**inp):
    import concourse.bacc as bacc
    from concourse.bass_utils import run_bass_kernel_spmd as run

    x = {k: np.asarray(v) for k, v in inp.items()}
    one = {k: (v[0] if k not in ("x", "c", "final_norm_w", "rel_bias_table_2") else v) for k, v in x.items()}
    cvals = {
        "c": one["c"], "norm_mix": one["norm_mix_w"], "b_ada": one["b_ada"], "ssd_cw": one["ssd_conv_w"],
        "ssd_cb": one["ssd_conv_b"], "norm_ffn": one["norm_ffn_w"], "ffn_cw": one["ffn_conv_w"],
        "final_norm": one["final_norm_w"], "norm1": one["norm1_g_2"], "ssd_norm": one["ssd_norm_w"],
        "ml_cw": one["mlstm_conv_w_2"], "ml_cb": one["mlstm_conv_b_2"], "merge_b": one["merge_b_2"],
        "norm2": one["norm2_g_2"], "q_gain": np.tile(one["attn_q_gain_2"], 2), "k_gain": np.tile(one["attn_k_gain_2"], 2),
    }
    rvals = {
        "dt_bias": one["dt_bias"], "a_log": one["a_log"], "d_skip": one["d_skip"], "rel_far": one["rel_bias"][:, 2 * MAX_REL],
        "sink": one["attn_sink_2"], "b_router": np.concatenate([one["b_router_group_2"], one["b_router_expert_2"]]),
        "gate_b": one["mlstm_gate_b_2"].reshape(-1), "out_gain": one["mlstm_out_gain_2"].reshape(-1),
    }
    arrays = {
        "x_t": x["x"][0].T,
        "cols": np.concatenate([columns(cvals[n], w) for n, (_, w) in COLS.items()], axis=1),
        "rows": np.concatenate([rvals[n].reshape(-1) for n in ROWP]),
        "table_t": one["rel_bias_table_2"].T,
        "rel_rev": one["rel_bias"][:, ::-1],
        "w_router": np.concatenate([one["w_router_group_2"], one["w_router_expert_2"]], axis=1),
        "w_expert_gate_2": one["w_expert_gate_2"].reshape(E * D, EF),
        "w_expert_up_2": one["w_expert_up_2"].reshape(E * D, EF),
        "w_expert_down_2": one["w_expert_down_2"].reshape(E * EF, D),
    }
    for n in ("w_ada", "w_in", "w_out", "w_up", "w_down", "w_in_2", "w_branch_attn_2", "w_branch_mlstm_2", "w_out_2"):
        arrays[n] = one[n]
    arrays = {k: np.ascontiguousarray(v) for k, v in arrays.items()}
    nc = bacc.Bacc("TRN2", target_bir_lowering=False, num_devices=1)
    aps = {k: nc.dram_tensor(f"in_{k}", v.shape, F32, kind="ExternalInput").ap() for k, v in arrays.items()}
    out = nc.dram_tensor("out", (T, D), F32, kind="ExternalOutput").ap()
    two_blocks(nc, aps, out)
    r = run(nc, [{f"in_{k}": v for k, v in arrays.items()}], core_ids=[0])
    return r.results[0]["out"].reshape(1, T, D)
```
